# Optimizing a Trainium2 kernel written in Bass

```python
import jax, jax.numpy as jnp
from jax import lax
import numpy as np
import math
import jax
import jax.numpy as jnp

D_MODEL = 1024
BATCH = 1
SEQ = 256
DEPTH = 1

D_MIX = 512
N_BRANCH = 3
GLA_HEADS = 4
GLA_DK = 64
GLA_DV = 128
GLA_RANK = 16
GLA_TAU = 16.0
GLA_CHUNK = 64
POOL_WINDOWS = (2, 4, 8, 16)
POOL_GROUPS = 4
POOL_GC = D_MIX // POOL_GROUPS
MOBA_HEADS = 8
MOBA_DH = D_MIX // MOBA_HEADS
MOBA_BLOCK = 256
MOBA_TOPK = 3
MOBA_QBLOCK = 128
D_FF = -(-8 * D_MODEL // (3 * 256)) * 256
EPS = 1e-6
NEG = -1e30

IN_SIZES = (GLA_HEADS * GLA_DK, GLA_HEADS * GLA_DK, GLA_HEADS * GLA_DV, GLA_RANK,
            GLA_HEADS * GLA_DV, D_MIX, D_MIX, D_MIX, D_MIX, N_BRANCH * D_MODEL)
D_IN = sum(IN_SIZES)


def rmsnorm(x, w):
    xf = x.astype(jnp.float32)
    y = xf * lax.rsqrt(jnp.mean(xf * xf, axis=-1, keepdims=True) + EPS)
    return (y * w.astype(jnp.float32)).astype(x.dtype)

def gla_mixer(q, k, v, g1, r, w_g2, b_g, norm_w):
    B, T, _ = q.shape
    H, DK, DV, C = GLA_HEADS, GLA_DK, GLA_DV, GLA_CHUNK
    NC = T // C
    f32 = jnp.float32
    qf = q.astype(f32).reshape(B, T, H, DK) * (DK ** -0.5)
    kf = k.astype(f32).reshape(B, T, H, DK)
    vf = v.astype(f32).reshape(B, T, H, DV)
    logit = (g1 @ w_g2 + b_g).astype(f32)
    log_a = (jax.nn.log_sigmoid(logit) / GLA_TAU).reshape(B, T, H, DK)

    def to_chunks(a):
        return a.reshape(B, NC, C, H, a.shape[-1]).transpose(1, 0, 3, 2, 4)

    causal = jnp.tril(jnp.ones((C, C), dtype=bool))

    def step(S, inp):
        qc, kc, vc, gc = inp
        bc = jnp.cumsum(gc, axis=2)
        diff = bc[:, :, :, None, :] - bc[:, :, None, :, :]
        decay = jnp.exp(jnp.where(causal[None, None, :, :, None], diff, NEG))
        attn = jnp.einsum('bhtd,bhsd,bhtsd->bhts', qc, kc, decay)
        o = (jnp.einsum('bhts,bhsv->bhtv', attn, vc)
             + jnp.einsum('bhtd,bhdv->bhtv', qc * jnp.exp(bc), S))
        b_last = bc[:, :, -1:, :]
        S = (jnp.exp(b_last[:, :, 0, :])[..., None] * S
             + jnp.einsum('bhsd,bhsv->bhdv', kc * jnp.exp(b_last - bc), vc))
        return S, o

    S0 = jnp.zeros((B, H, DK, DV), f32)
    _, o = lax.scan(step, S0, (to_chunks(qf), to_chunks(kf), to_chunks(vf), to_chunks(log_a)))
    o = o.transpose(1, 0, 3, 2, 4).reshape(B, T, H, DV)
    o = o * lax.rsqrt(jnp.mean(o * o, axis=-1, keepdims=True) + EPS) * norm_w.astype(f32)
    o = o.reshape(B, T, H * DV) * jax.nn.silu(r.astype(f32))
    return o.astype(q.dtype)

def pool_mixer(u, w_pool, scale):
    B, T, _ = u.shape
    f32 = jnp.float32
    uf = u.astype(f32).reshape(B, T, POOL_GROUPS, POOL_GC)
    cs = jnp.cumsum(uf, axis=1)
    t = jnp.arange(T)
    outs = []
    for gi, w in enumerate(POOL_WINDOWS):
        c = cs[:, :, gi]
        lag = jnp.pad(c, ((0, 0), (w, 0), (0, 0)))[:, :T]
        cnt = jnp.minimum(t + 1, w).astype(f32)[None, :, None]
        outs.append((c - lag) / cnt - uf[:, :, gi])
    p = jnp.stack(outs, axis=2)
    y = jnp.einsum('btgc,gcd->btgd', p, w_pool.astype(f32)).reshape(B, T, D_MIX)
    return (y * scale.astype(f32)).astype(u.dtype)

def moba_mixer(q, k, v):
    B, T, _ = q.shape
    H, DH, BLK, QB = MOBA_HEADS, MOBA_DH, MOBA_BLOCK, MOBA_QBLOCK
    NB = -(-T // BLK)
    NQ = T // QB
    KSEL = min(MOBA_TOPK, NB)
    f32 = jnp.float32
    qh = q.reshape(B, T, H, DH).transpose(0, 2, 1, 3)
    kh = k.reshape(B, T, H, DH).transpose(0, 2, 1, 3)
    vh = v.reshape(B, T, H, DH).transpose(0, 2, 1, 3)
    pad = NB * BLK - T
    kp = jnp.pad(kh, ((0, 0), (0, 0), (0, pad), (0, 0)))
    vp = jnp.pad(vh, ((0, 0), (0, 0), (0, pad), (0, 0)))
    kblk = kp.reshape(B, H, NB, BLK, DH)
    vblk = vp.reshape(B, H, NB, BLK, DH)
    kmean = jnp.mean(kblk.astype(f32), axis=3)
    gate = jnp.einsum('bhtd,bhnd->bhtn', qh.astype(f32), kmean)
    tblk = jnp.arange(T) // BLK
    past = jnp.arange(NB)[None, :] < tblk[:, None]
    gate = jnp.where(past[None, None], gate, NEG)
    _, idx = lax.top_k(gate, KSEL)
    valid = jnp.arange(KSEL)[None, :] < tblk[:, None]
    slopes = (2.0 ** (-8.0 * (jnp.arange(H) + 1) / H)).astype(f32)
    scale = DH ** -0.5
    hi = jnp.arange(H)[:, None, None]

    def one_block(i):
        b = i // NQ
        t0 = (i % NQ) * QB
        qb = lax.dynamic_slice(qh, (b, 0, t0, 0), (1, H, QB, DH))[0]
        ib = lax.dynamic_slice(idx, (b, 0, t0, 0), (1, H, QB, KSEL))[0]
        vm = lax.dynamic_slice(valid, (t0, 0), (QB, KSEL))
        kg = kblk[b][hi, ib]
        vg = vblk[b][hi, ib]
        own0 = (t0 // BLK) * BLK
        ko = lax.dynamic_slice(kp, (b, 0, own0, 0), (1, H, BLK, DH))[0]
        vo = lax.dynamic_slice(vp, (b, 0, own0, 0), (1, H, BLK, DH))[0]
        tq = t0 + jnp.arange(QB)
        s_sel = ib[..., None] * BLK + jnp.arange(BLK)
        s_own = own0 + jnp.arange(BLK)
        sc_sel = (jnp.einsum('hqd,hqkjd->hqkj', qb, kg).astype(f32) * scale
                  - slopes[:, None, None, None] * (tq[None, :, None, None] - s_sel).astype(f32))
        sc_sel = jnp.where(vm[None, :, :, None], sc_sel, NEG)
        sc_own = (jnp.einsum('hqd,hjd->hqj', qb, ko).astype(f32) * scale
                  - slopes[:, None, None] * (tq[:, None] - s_own[None, :]).astype(f32)[None])
        sc_own = jnp.where((s_own[None, :] <= tq[:, None])[None], sc_own, NEG)
        sc = jnp.concatenate([sc_sel.reshape(H, QB, KSEL * BLK), sc_own], axis=-1)
        p = jax.nn.softmax(sc, axis=-1).astype(v.dtype)
        p_sel = p[..., :KSEL * BLK].reshape(H, QB, KSEL, BLK)
        p_own = p[..., KSEL * BLK:]
        return (jnp.einsum('hqkj,hqkjd->hqd', p_sel, vg)
                + jnp.einsum('hqj,hjd->hqd', p_own, vo))

    out = lax.map(one_block, jnp.arange(B * NQ))
    return out.reshape(B, NQ, H, QB, DH).transpose(0, 1, 3, 2, 4).reshape(B, T, H * DH)

def first_inputs(seed: int = 0) -> dict:
    key = jax.random.key(seed)
    ks = jax.random.split(key, 20)
    f32 = jnp.float32

    def nrm(k, shape, fan_in):
        return jax.random.normal(k, shape, f32) * (fan_in ** -0.5)

    def gain(k, shape):
        return 1.0 + 0.05 * jax.random.normal(k, shape, f32)

    L = DEPTH
    return {
        "x": jax.random.normal(ks[0], (BATCH, SEQ, D_MODEL), f32),
        "norm_mix_pre": gain(ks[1], (L, D_MODEL)),
        "w_in": nrm(ks[2], (L, D_MODEL, D_IN), D_MODEL),
        "gla_w_g2": nrm(ks[3], (L, GLA_RANK, GLA_HEADS * GLA_DK), GLA_RANK),
        "gla_b_g": 0.1 * jax.random.normal(ks[4], (L, GLA_HEADS * GLA_DK), f32),
        "gla_norm": gain(ks[5], (L, GLA_DV)),
        "pool_w": nrm(ks[6], (L, POOL_GROUPS, POOL_GC, POOL_GC), POOL_GC),
        "pool_scale": gain(ks[7], (L, D_MIX)),
        "w_branch_a": nrm(ks[8], (L, D_MIX, D_MODEL), D_MIX),
        "w_branch_b": nrm(ks[9], (L, D_MIX, D_MODEL), D_MIX),
        "w_branch_c": nrm(ks[10], (L, D_MIX, D_MODEL), D_MIX),
        "w_out": nrm(ks[11], (L, D_MODEL, D_MODEL), D_MODEL),
        "norm_mix_post": gain(ks[12], (L, D_MODEL)),
        "norm_ffn_pre": gain(ks[13], (L, D_MODEL)),
        "ffn_w_gate": nrm(ks[14], (L, D_MODEL, D_FF), D_MODEL),
        "ffn_w_up": nrm(ks[15], (L, D_MODEL, D_FF), D_MODEL),
        "ffn_w_down": nrm(ks[16], (L, D_FF, D_MODEL), D_FF),
        "norm_ffn_post": gain(ks[17], (L, D_MODEL)),
    }

def first_block(x, norm_mix_pre, w_in, gla_w_g2, gla_b_g, gla_norm, pool_w, pool_scale,
              w_branch_a, w_branch_b, w_branch_c, w_out, norm_mix_post, norm_ffn_pre,
              ffn_w_gate, ffn_w_up, ffn_w_down, norm_ffn_post):
    B, T, D = x.shape
    splits = [int(s) for s in np.cumsum(IN_SIZES)[:-1]]
    for l in range(DEPTH):
        h = rmsnorm(x, norm_mix_pre[l])
        proj = h @ w_in[l]
        gq, gk, gv, gg1, gr, pu, mq, mk, mv, gates = jnp.split(proj, splits, axis=-1)
        ya = gla_mixer(gq, gk, gv, gg1, gr, gla_w_g2[l], gla_b_g[l], gla_norm[l]) @ w_branch_a[l]
        yb = pool_mixer(pu, pool_w[l], pool_scale[l]) @ w_branch_b[l]
        yc = moba_mixer(mq, mk, mv) @ w_branch_c[l]
        gs = jax.nn.sigmoid(gates).reshape(B, T, N_BRANCH, D)
        mixed = gs[:, :, 0] * ya + gs[:, :, 1] * yb + gs[:, :, 2] * yc
        x = x + rmsnorm(mixed @ w_out[l], norm_mix_post[l])
        h = rmsnorm(x, norm_ffn_pre[l])
        f = (jax.nn.silu(h @ ffn_w_gate[l]) * (h @ ffn_w_up[l])) @ ffn_w_down[l]
        x = x + rmsnorm(f, norm_ffn_post[l])
    return x


CHUNK = 64
NEG_BIG = -1e30
HG_HEADS = 8
HG_DK = 128
HG_DV = 128
HG_QK = HG_HEADS * HG_DK
HG_W = HG_HEADS * HG_DV
ML_HEADS = 4
ML_DQK = 128
ML_DV = 256
ML_CONV = 4
ML_QK = ML_HEADS * ML_DQK
ML_W = ML_HEADS * ML_DV
MB_HEADS = 16
MB_P = 64
MB_GROUPS = 4
MB_N = 128
MB_CONV = 4
MB_W = MB_HEADS * MB_P
MB_CONV_DIM = MB_W + 2 * MB_GROUPS * MB_N
D_FF_2 = 2816
FFN_CONV = 3
IN_SPLITS = (HG_QK, HG_QK, HG_W, HG_W,
             2 * ML_QK, ML_W, 2 * ML_HEADS, ML_W,
             MB_W, MB_CONV_DIM, MB_HEADS,
             N_BRANCH * D_MODEL)
N_IN = sum(IN_SPLITS)


def rmsnorm_2(x, g):
    xf = x.astype(jnp.float32)
    y = xf * lax.rsqrt(jnp.mean(xf * xf, axis=-1, keepdims=True) + EPS)
    return (y * g.astype(jnp.float32)).astype(x.dtype)

def causal_dwconv(u, w, b):
    K = w.shape[0]
    S = u.shape[1]
    up = jnp.pad(u, ((0, 0), (K - 1, 0), (0, 0)))
    return sum(up[:, k:k + S] * w[k] for k in range(K)) + b

def to_chunks(t):
    B, S = t.shape[:2]
    t = t.astype(jnp.float32).reshape(B, S // CHUNK, CHUNK, *t.shape[2:])
    return jnp.moveaxis(t, 1, 0)

def from_chunks(t):
    t = jnp.moveaxis(t, 0, 1)
    return t.reshape(t.shape[0], -1, *t.shape[3:])

def causal_tri():
    return jnp.tril(jnp.ones((CHUNK, CHUNK), dtype=bool))

def hgrn2_scan(q, log_f, v):
    B, _, H, dk = q.shape
    dv = v.shape[-1]
    k = -jnp.expm1(log_f)
    tri = causal_tri()

    def step(state, inp):
        qc, lfc, kc, vc = inp
        b = jnp.cumsum(lfc, axis=1)
        diff = b[:, :, None] - b[:, None, :]
        decay = jnp.exp(jnp.where(tri[None, :, :, None, None], diff, NEG_BIG))
        attn = jnp.einsum('bthd,btshd->bhts', qc, decay * kc[:, None])
        o_intra = jnp.einsum('bhts,bshv->bthv', attn, vc)
        o_inter = jnp.einsum('bthd,bhdv->bthv', qc * jnp.exp(b), state)
        b_last = b[:, -1]
        k_dec = kc * jnp.exp(b_last[:, None] - b)
        state = jnp.exp(b_last)[..., None] * state + jnp.einsum('bshd,bshv->bhdv', k_dec, vc)
        return state, o_intra + o_inter

    s0 = jnp.zeros((B, H, dk, dv), jnp.float32)
    _, o = lax.scan(step, s0, (to_chunks(q), to_chunks(log_f), to_chunks(k), to_chunks(v)))
    return from_chunks(o)

def mlstm_scan(q, k, v, i_pre, log_f):
    B, _, H, dk = q.shape
    dv = v.shape[-1]
    tri = causal_tri()

    def step(carry, inp):
        C, n, m = carry
        qc, kc, vc, ic, fc = inp
        bh = jnp.moveaxis(jnp.cumsum(fc, axis=1), 1, 2)
        ih = jnp.moveaxis(ic, 1, 2)
        logD = jnp.where(tri, bh[..., :, None] - bh[..., None, :] + ih[..., None, :], NEG_BIG)
        log_inter = bh + m[..., None]
        m_t = jnp.maximum(jnp.max(logD, axis=-1), log_inter)
        s = jnp.einsum('bthd,bshd->bhts', qc, kc) * jnp.exp(logD - m_t[..., None])
        inter_w = jnp.exp(log_inter - m_t)
        inter_wt = jnp.swapaxes(inter_w, 1, 2)[..., None]
        num = jnp.einsum('bhts,bshv->bthv', s, vc) + jnp.einsum('bthd,bhdv->bthv', qc, C) * inter_wt
        den = jnp.sum(s, axis=-1) + jnp.einsum('bthd,bhd->bht', qc, n) * inter_w
        denom = jnp.maximum(jnp.abs(den), jnp.exp(-m_t))
        h = num / jnp.swapaxes(denom, 1, 2)[..., None]
        b_last = bh[..., -1]
        log_w = b_last[..., None] - bh + ih
        m_new = jnp.maximum(b_last + m, jnp.max(log_w, axis=-1))
        w = jnp.swapaxes(jnp.exp(log_w - m_new[..., None]), 1, 2)[..., None]
        dstate = jnp.exp(b_last + m - m_new)
        C = dstate[..., None, None] * C + jnp.einsum('bshd,bshv->bhdv', kc * w, vc)
        n = dstate[..., None] * n + jnp.sum(kc * w, axis=1)
        return (C, n, m_new), h

    c0 = (jnp.zeros((B, H, dk, dv), jnp.float32), jnp.zeros((B, H, dk), jnp.float32),
          jnp.zeros((B, H), jnp.float32))
    _, h = lax.scan(step, c0, (to_chunks(q), to_chunks(k), to_chunks(v), to_chunks(i_pre), to_chunks(log_f)))
    return from_chunks(h)

def ssd_scan(x, dt, A, Bm, Cm):
    B, _, H, P = x.shape
    N = Bm.shape[-1]
    hpg = H // Bm.shape[2]
    tri = causal_tri()
    A = A.astype(jnp.float32)

    def step(state, inp):
        xc, dtc, Bc, Cc = inp
        cum = jnp.moveaxis(jnp.cumsum(dtc * A, axis=1), 1, 2)
        L = jnp.exp(jnp.where(tri, cum[..., :, None] - cum[..., None, :], NEG_BIG))
        CB = jnp.repeat(jnp.einsum('btgn,bsgn->bgts', Cc, Bc), hpg, axis=1)
        xdt = xc * dtc[..., None]
        y_intra = jnp.einsum('bhts,bshp->bthp', CB * L, xdt)
        Ch = jnp.repeat(Cc, hpg, axis=2)
        y_inter = jnp.einsum('bthn,bhpn->bthp', Ch, state) * jnp.swapaxes(jnp.exp(cum), 1, 2)[..., None]
        dec = jnp.swapaxes(jnp.exp(cum[..., -1:] - cum), 1, 2)[..., None]
        Bh = jnp.repeat(Bc, hpg, axis=2)
        state = jnp.exp(cum[..., -1])[..., None, None] * state + jnp.einsum('bshn,bshp->bhpn', Bh * dec, xdt)
        return state, y_intra + y_inter

    s0 = jnp.zeros((B, H, P, N), jnp.float32)
    _, y = lax.scan(step, s0, (to_chunks(x), to_chunks(dt), to_chunks(Bm), to_chunks(Cm)))
    return from_chunks(y)

def second_inputs(seed: int = 0) -> dict:
    key = jax.random.key(seed)
    ks = jax.random.split(key, 32)
    f32 = jnp.float32

    def nrm(k, shape, scale):
        return jax.random.normal(k, shape, f32) * scale

    def gain(k, shape):
        return 1.0 + 0.05 * jax.random.normal(k, shape, f32)

    dt0 = jnp.exp(jax.random.uniform(ks[12], (DEPTH, MB_HEADS), f32, math.log(1e-3), math.log(1e-1)))
    ml_f_bias = jnp.linspace(3.0, 6.0, ML_HEADS, dtype=f32)[None] + nrm(ks[7], (DEPTH, ML_HEADS), 0.1)
    ml_i_bias = nrm(ks[8], (DEPTH, ML_HEADS), 0.1)
    return {
        "x": jax.random.normal(ks[0], (BATCH, SEQ, D_MODEL), f32),
        "norm1_g": gain(ks[1], (DEPTH, D_MODEL)),
        "w_in": nrm(ks[2], (DEPTH, D_MODEL, N_IN), D_MODEL ** -0.5),
        "hg_lb_logits": nrm(ks[3], (DEPTH, HG_QK), 0.1),
        "hg_norm_g": gain(ks[4], (DEPTH, HG_DV)),
        "ml_conv_w": nrm(ks[5], (DEPTH, ML_CONV, 2 * ML_QK), ML_CONV ** -0.5),
        "ml_conv_b": nrm(ks[6], (DEPTH, 2 * ML_QK), 0.02),
        "ml_gate_b": jnp.concatenate([ml_i_bias, ml_f_bias], axis=-1),
        "ml_norm_g": gain(ks[9], (DEPTH, ML_DV)),
        "mb_conv_w": nrm(ks[10], (DEPTH, MB_CONV, MB_CONV_DIM), MB_CONV ** -0.5),
        "mb_conv_b": nrm(ks[11], (DEPTH, MB_CONV_DIM), 0.02),
        "mb_dt_bias": dt0 + jnp.log(-jnp.expm1(-dt0)),
        "mb_a_log": jnp.log(jax.random.uniform(ks[13], (DEPTH, MB_HEADS), f32, 1.0, 16.0)),
        "mb_d": gain(ks[14], (DEPTH, MB_HEADS)),
        "mb_norm_g": gain(ks[15], (DEPTH, MB_W)),
        "w_br_hg": nrm(ks[16], (DEPTH, HG_W, D_MODEL), HG_W ** -0.5),
        "w_br_ml": nrm(ks[17], (DEPTH, ML_W, D_MODEL), ML_W ** -0.5),
        "w_br_mb": nrm(ks[18], (DEPTH, MB_W, D_MODEL), MB_W ** -0.5),
        "w_out": nrm(ks[19], (DEPTH, D_MODEL, D_MODEL), D_MODEL ** -0.5),
        "norm2_g": gain(ks[20], (DEPTH, D_MODEL)),
        "w_up": nrm(ks[21], (DEPTH, D_MODEL, 2 * D_FF_2), D_MODEL ** -0.5),
        "ffn_conv_w": nrm(ks[22], (DEPTH, FFN_CONV, 2 * D_FF_2), FFN_CONV ** -0.5),
        "ffn_conv_b": nrm(ks[23], (DEPTH, 2 * D_FF_2), 0.02),
        "w_down": nrm(ks[24], (DEPTH, D_FF_2, D_MODEL), D_FF_2 ** -0.5),
        "final_g": gain(ks[25], (D_MODEL,)),
    }

def second_block(x, norm1_g, w_in, hg_lb_logits, hg_norm_g, ml_conv_w, ml_conv_b, ml_gate_b, ml_norm_g,
              mb_conv_w, mb_conv_b, mb_dt_bias, mb_a_log, mb_d, mb_norm_g, w_br_hg, w_br_ml, w_br_mb,
              w_out, norm2_g, w_up, ffn_conv_w, ffn_conv_b, w_down, final_g):
    B, S, _ = x.shape
    f32 = jnp.float32
    lb_p = jax.nn.softmax(hg_lb_logits.astype(f32), axis=0)
    lbs = jnp.cumsum(lb_p, axis=0) - lb_p[0]
    split_at = [int(c) for c in np.cumsum(IN_SPLITS)[:-1]]

    for l in range(DEPTH):
        h = rmsnorm_2(x, norm1_g[l])
        (hg_q, hg_f, hg_i, hg_g, ml_qk, ml_v, ml_if, ml_o,
         mb_z, mb_xbc, mb_dt, gate_pre) = jnp.split(h @ w_in[l], split_at, axis=-1)

        lb = lbs[l]
        log_f = jnp.log(lb + (1.0 - lb) * jax.nn.sigmoid(hg_f.astype(f32)))
        o_hg = hgrn2_scan(jax.nn.silu(hg_q).reshape(B, S, HG_HEADS, HG_DK),
                          log_f.reshape(B, S, HG_HEADS, HG_DK),
                          hg_i.reshape(B, S, HG_HEADS, HG_DV))
        y_hg = (rmsnorm_2(o_hg, hg_norm_g[l]).reshape(B, S, HG_W)
                * jax.nn.silu(hg_g.astype(f32))).astype(x.dtype)

        qk = jax.nn.silu(causal_dwconv(ml_qk, ml_conv_w[l], ml_conv_b[l]))
        q_m, k_m = jnp.split(qk, 2, axis=-1)
        gb = ml_gate_b[l]
        i_pre = ml_if[..., :ML_HEADS] + gb[:ML_HEADS]
        log_f_m = jax.nn.log_sigmoid((ml_if[..., ML_HEADS:] + gb[ML_HEADS:]).astype(f32))
        h_ml = mlstm_scan(q_m.reshape(B, S, ML_HEADS, ML_DQK),
                          k_m.reshape(B, S, ML_HEADS, ML_DQK) * (ML_DQK ** -0.5),
                          ml_v.reshape(B, S, ML_HEADS, ML_DV), i_pre, log_f_m)
        y_ml = (rmsnorm_2(h_ml, ml_norm_g[l]).reshape(B, S, ML_W)
                * jax.nn.sigmoid(ml_o.astype(f32))).astype(x.dtype)

        xbc = jax.nn.silu(causal_dwconv(mb_xbc, mb_conv_w[l], mb_conv_b[l]))
        xs, Bm, Cm = jnp.split(xbc, [MB_W, MB_W + MB_GROUPS * MB_N], axis=-1)
        xs = xs.reshape(B, S, MB_HEADS, MB_P)
        dt = jax.nn.softplus((mb_dt + mb_dt_bias[l]).astype(f32))
        A = -jnp.exp(mb_a_log[l].astype(f32))
        y_ssd = ssd_scan(xs, dt, A, Bm.reshape(B, S, MB_GROUPS, MB_N), Cm.reshape(B, S, MB_GROUPS, MB_N))
        y_ssd = y_ssd + mb_d[l].astype(f32)[:, None] * xs
        yz = (y_ssd.reshape(B, S, MB_W) * jax.nn.silu(mb_z.astype(f32))).reshape(B, S, MB_GROUPS, MB_W // MB_GROUPS)
        y_mb = rmsnorm_2(yz, mb_norm_g[l].reshape(MB_GROUPS, MB_W // MB_GROUPS)).reshape(B, S, MB_W).astype(x.dtype)

        gates = jax.nn.sigmoid(gate_pre).reshape(B, S, N_BRANCH, D_MODEL)
        mixed = (gates[:, :, 0] * (y_hg @ w_br_hg[l])
                 + gates[:, :, 1] * (y_ml @ w_br_ml[l])
                 + gates[:, :, 2] * (y_mb @ w_br_mb[l]))
        x = x + mixed @ w_out[l]

        u = causal_dwconv(rmsnorm_2(x, norm2_g[l]) @ w_up[l], ffn_conv_w[l], ffn_conv_b[l])
        u_g, u_v = jnp.split(u, 2, axis=-1)
        x = x + (jax.nn.silu(u_g) * u_v) @ w_down[l]

    return rmsnorm_2(x, final_g)


def setup_inputs(seed=0):
    out = dict(first_inputs(seed))
    for name, value in second_inputs(seed + 1).items():
        if name != "x":
            out[name + "_2"] = value
    return out


def reference(
    x, norm_mix_pre, w_in, gla_w_g2, gla_b_g, gla_norm, pool_w, pool_scale, w_branch_a,
    w_branch_b, w_branch_c, w_out, norm_mix_post, norm_ffn_pre, ffn_w_gate, ffn_w_up,
    ffn_w_down, norm_ffn_post, norm1_g_2, w_in_2, hg_lb_logits_2, hg_norm_g_2, ml_conv_w_2,
    ml_conv_b_2, ml_gate_b_2, ml_norm_g_2, mb_conv_w_2, mb_conv_b_2, mb_dt_bias_2, mb_a_log_2,
    mb_d_2, mb_norm_g_2, w_br_hg_2, w_br_ml_2, w_br_mb_2, w_out_2, norm2_g_2, w_up_2,
    ffn_conv_w_2, ffn_conv_b_2, w_down_2, final_g_2,
):
    x = first_block(
        x, norm_mix_pre, w_in, gla_w_g2, gla_b_g, gla_norm, pool_w, pool_scale, w_branch_a,
        w_branch_b, w_branch_c, w_out, norm_mix_post, norm_ffn_pre, ffn_w_gate, ffn_w_up,
        ffn_w_down, norm_ffn_post,
    )
    return second_block(
        x, norm1_g_2, w_in_2, hg_lb_logits_2, hg_norm_g_2, ml_conv_w_2, ml_conv_b_2,
        ml_gate_b_2, ml_norm_g_2, mb_conv_w_2, mb_conv_b_2, mb_dt_bias_2, mb_a_log_2, mb_d_2,
        mb_norm_g_2, w_br_hg_2, w_br_ml_2, w_br_mb_2, w_out_2, norm2_g_2, w_up_2, ffn_conv_w_2,
        ffn_conv_b_2, w_down_2, final_g_2,
    )


_drawn_inputs = setup_inputs


def setup_inputs(seed=0):
    import zlib

    import numpy as np

    out = dict(_drawn_inputs(seed))
    spreads = {}
    factors = {'hg_norm_g_2': 7.161,
     'ml_conv_b_2': 8.0,
     'ml_norm_g_2': 7.109,
     'mb_conv_b_2': 6.664,
     'mb_d_2': 4.949,
     'mb_norm_g_2': 3.735,
     'ffn_conv_b_2': 6.475,
     'norm2_g_2': 5.228}
    for name, (base, spread) in spreads.items():
        noise = np.random.default_rng([zlib.crc32(name.encode()), seed]).standard_normal(out[name].shape)
        drawn = base * np.exp(spread * noise) if base else spread * noise
        out[name] = jnp.asarray(drawn.astype(out[name].dtype))
    for name, factor in factors.items():
        out[name] = (out[name] * factor).astype(out[name].dtype)
    return out
```

```python
import concourse.bass as bass
from concourse import mybir
from contextlib import ExitStack
import numpy as np

F32 = mybir.dt.float32
F32R = mybir.dt.float32r
I32 = mybir.dt.int32
ACT = mybir.ActivationFunctionType
ALU = mybir.AluOpType
AX = mybir.AxisListType

T = 256
D = 1024
KT = D // 128
FF = 2816
FT = FF // 128
PW = 2048
EPS = 1e-6
NEG = -1e30
RING = 3
LEVELS = [128, 64, 32, 16, 8, 4, 2, 1]

GQ, GK, GR, GV = 0, 2, 4, 8
MQ, MK, MV = 12, 16, 20
PU, GATE1 = 24, 28
HQ, HFG, HI, HG, HK = 0, 8, 16, 24, 48
LQ, LK, LV, LO = 32, 36, 40, 24
XS, XB, XC, XZ = 0, 8, 12, 16
GATE2 = [32, 40, 32]
SQ = 40
RMS_T, RCP_T = 38, 39
OUT = 0
POOL_TILES = 53

PAIRS1 = (
    [("B", "copy", GQ, 0.125)] + [("B", "copy", GK, 1.0)]
    + [("B", "copy", GR + 2 * j, 1.0) for j in range(2)]
    + [("A", "copyA", GV + j, 2) for j in range(2)]
    + [("B", "copy", MQ + 2 * j, 0.125) for j in range(2)]
    + [("B", "copy", MK + 2 * j, 1.0) for j in range(2)]
    + [("A", "copyA", MV + j, 2) for j in range(2)]
    + [("B", "copy", PU + 2 * j, 1.0) for j in range(2)]
    + [("B", "tanh", GATE1 + 2 * j, 0.5) for j in range(12)]
    + [("BR1", "mix1", j, 0) for j in range(6)]
    + [("B", "copy", OUT + 2 * j, 1.0) for j in range(4)]
)
PAIRS2 = (
    [("B", "copy", HQ + 2 * j, 1.0) for j in range(4)]
    + [("B", "copy", HFG + 2 * j, 1.0) for j in range(4)]
    + [("A", "copyA", HI + j, 4) for j in range(4)]
    + [("B", "copy", HG + 2 * j, 1.0) for j in range(4)]
    + [("B", "conv", LQ + 2 * j, 2 * j) for j in range(4)]
    + [("A", "copyA", LV + j, 4) for j in range(4)]
    + [("B", "tanh", LO + 2 * j, 0.5) for j in range(4)]
    + [("B", "conv", XS + 2 * j, 8 + 2 * j) for j in range(8)]
    + [("B", "copy", XZ + 2 * j, 1.0) for j in range(4)]
    + [("B", "tanh", GATE2[0] + 2 * j, 0.5) for j in range(4)]
    + [("Y0", "mix2", j, 0) for j in range(4)]
    + [("B", "tanh", GATE2[1] + 2 * j, 0.5) for j in range(4)]
    + [("Y1", "mix2", j, 1) for j in range(4)]
    + [("B", "tanh", GATE2[2] + 2 * j, 0.5) for j in range(4)]
    + [("Y0", "mix2", j, 2) for j in range(4)]
    + [("B", "resid", 2 * j, 0) for j in range(4)]
)
N1, N2, NF = len(PAIRS1), len(PAIRS2), FT + FT // 2
FFN1 = N1
BLK2 = N1 + NF
FFN2 = BLK2 + N2
NPAIRS = FFN2 + NF
PAIR = dict(enumerate(PAIRS1)) | {BLK2 + n: s for n, s in enumerate(PAIRS2)}


def taken(p):
    who = "act_taken" if PAIR[p][1] in ("copy", "tanh", "copyA") else "dve_taken"
    act = ("copy", "tanh", "copyA")
    return who, sum((PAIR[x][1] in act) == (who == "act_taken") for x in PAIR if x <= p)


COLS = {}
_n = 0
for _name, _k in (("norm_mix_pre", KT), ("norm_mix_post", KT), ("norm_ffn_pre", KT), ("norm_ffn_post", KT),
                  ("gla_b_g", 2), ("gla_norm", 1), ("pool_scale", 4), ("norm1_g", KT), ("hg_norm", 1),
                  ("ml_norm", 2), ("mb_d", KT), ("mb_norm", KT), ("norm2_g", KT), ("final_g", KT),
                  ("conv_b", 24), ("conv_w", 96), ("ffn_conv_b", 44), ("ffn_conv_w", 132)):
    COLS[_name] = _n
    _n += _k
NCOLS = _n

CIDENT, CONES, CMASK, CMASKT, CLEVEL = 0, 128, 384, 512, 640
CALIBI, CALCOL, CHEAD, CINV = 640 + 8 * 128, 640 + 8 * 128 + 256, 640 + 8 * 128 + 272, 640 + 8 * 128 + 303
NCONST = CINV + 64


def constants():
    c = np.zeros((128, NCONST), np.float32)
    s, t = np.arange(128)[:, None], np.arange(128)[None, :]
    c[:, CIDENT:CIDENT + 128] = np.eye(128)
    c[:, CONES:CONES + 256] = 1.0
    c[:, CMASK:CMASK + 128] = np.where(s <= t, 0.0, NEG)
    c[:, CMASKT:CMASKT + 128] = np.where(t <= s, 0.0, NEG)
    for n, half in enumerate(LEVELS[1:]):
        same = (s // (2 * half)) == (t // (2 * half))
        c[:, CLEVEL + n * 128:CLEVEL + (n + 1) * 128] = same & (s % (2 * half) < half) & (t % (2 * half) >= half)
    c[:, CLEVEL + 7 * 128:CLEVEL + 8 * 128] = s == t
    slope = 2.0 ** -(np.arange(8) + 1.0)
    c[:8, CALIBI:CALIBI + 256] = slope[:, None] * np.arange(256)[None, :]
    for v in range(2):
        c[:, CALCOL + v * 8:CALCOL + v * 8 + 8] = slope[None, :] * (np.arange(128)[:, None] + 128 * v)
    c[:, CHEAD + 15] = 1.0
    for g, w in enumerate((2, 4, 8, 16)):
        c[:, CINV + 16 * g:CINV + 16 * g + 16] = 1.0 / np.minimum(np.arange(16) + 1, w)
    return c


def build(nc, stream, xT, cols, consts, g1w, g2w, poolw, ifw, dtw, rows, out):
    ctx = ExitStack()
    with ctx:
        def sb(name, shape, dt=F32):
            return ctx.enter_context(nc.sbuf_tensor(name, shape, dt))

        sems = {}

        def S(name):
            if name not in sems:
                sems[name] = ctx.enter_context(nc.semaphore(name))
            return sems[name]

        raw = sb("raw", [128, RING, PW])
        whi = sb("whi", [128, RING, PW], F32R)
        wlo = sb("wlo", [128, RING, PW], F32R)
        X = sb("X", [128, KT, T])
        HF = sb("HF", [128, KT, T])
        XH = sb("XH", [128, KT, T], F32R)
        XL = sb("XL", [128, KT, T], F32R)
        y_at = nc.sbuf_base
        Y = sb("Y", [128, 32, T], F32R)
        U = nc.alloc_sbuf_tensor_at("U", [128, 16, T], F32, offset=y_at + 16 * T * 4)
        P = sb("P", [128, POOL_TILES, T])
        C = sb("C", [128, NCONST])
        PC = sb("PC", [128, NCOLS])
        G1W = sb("G1W", [128, KT * 16])
        IFW = sb("IFW", [128, KT * 8])
        DTW = sb("DTW", [128, KT * 16])
        RW = sb("RW", [36, 8])
        SC = sb("SC", [128, 128])
        R = sb("R", [36, 7 * T])
        SM = R[0:16, 0:3 * T]
        LR = R[32:36, 0:6 * T].rearrange("p (a t) -> p a t", a=6)
        DR = R[0:16, 3 * T:7 * T].rearrange("p (a t) -> p a t", a=4)
        RMS, RCP = P[:, RMS_T, :], P[:, RCP_T, :]
        G2W, PLW = U[0:16, 4:5, :].rearrange("p a t -> p (a t)"), U[:, 6:8, :].rearrange("p a t -> p (a t)")
        pp = [ctx.enter_context(nc.psum_tensor(f"pp{i}", [128, 512], F32)) for i in range(RING)]
        pm = ctx.enter_context(nc.psum_tensor("pm", [128, 5 * 512], F32))

        arrived = [S(f"weights_arrived{i}") for i in range(RING)]
        hi_ready, lo_ready, pair_done = (S(n) for n in ("hi_ready", "lo_ready", "pair_done"))
        conv_started = S("conv_started")
        ident = C[:, CIDENT:CIDENT + 128]
        ones = C[:, CONES:CONES + 128]

        def col(name, i=0):
            return PC[:, COLS[name] + i:COLS[name] + i + 1]

        block = ctx.enter_context(nc.Block())
        self = dict(locals())

        @block.sync
        def _(sp):
            def load(p, slot):
                src = stream[p] if isinstance(p, int) else stream[bass.ds(p, 1), :, :].rearrange("a p n -> p (a n)")
                sp.dma_start(raw[:, slot, :], src).then_inc(arrived[slot], 16)

            sp.dma_start(X[:, :, :], xT).then_inc(S("x_loaded"), 16)
            sp.dma_start(C[:, :], consts).then_inc(S("consts_loaded"), 16)
            sp.dma_start(PC[:, :], cols).then_inc(S("cols_loaded"), 16)
            for p in range(RING):
                load(p, p)
            for name, dst, src in (("G1W", G1W, g1w), ("G2W", G2W, g2w), ("PLW", PLW, poolw), ("IFW", IFW, ifw),
                                   ("DTW", DTW, dtw), ("RW", RW, rows)):
                sp.dma_start(dst[:, :], src).then_inc(S(f"loaded_{name}"), 16)
            whole = (NPAIRS - RING) // RING
            with sp.Fori(1, 1 + whole) as i:
                for slot in range(RING):
                    sp.wait_ge(lo_ready, i * RING + (slot + 1 - RING))
                    load(i * RING + slot, slot)
            for p in range(RING * (1 + whole), NPAIRS):
                sp.wait_ge(lo_ready, p - RING + 1)
                load(p, p % RING)
            sp.wait_ge(S("result_ready"), 8)
            sp.dma_start(out, P[:, 8:16, :]).then_inc(S("result_stored"), 16)
            sp.wait_ge(S("result_stored"), 16)

        parts = {}
        for engine in ("tensor", "scalar", "vector", "gpsimd"):
            parts[engine] = engine
        program(nc, block, S, self)


def program(nc, block, S, L):
    raw, whi, wlo, X, HF, XH, XL, Y, P, C, PC = (L[k] for k in "raw whi wlo X HF XH XL Y P C PC".split())
    G1W, IFW, DTW, G2W, PLW, RW, RMS, RCP, SM, SC = (L[k] for k in "G1W IFW DTW G2W PLW RW RMS RCP SM SC".split())
    pp, pm, arrived, hi_ready, lo_ready, pair_done, conv_started = (
        L[k] for k in "pp pm arrived hi_ready lo_ready pair_done conv_started".split())
    ident, ones, col = L["ident"], L["ones"], L["col"]

    def bank(n):
        return pm[:, n * 512:(n + 1) * 512]

    def split_hi(act, p, slot, turn):
        act.wait_ge(arrived[slot], turn * 16 + 16)
        if not isinstance(p, int) or p >= RING:
            act.wait_ge(pair_done, p - (RING - 1))
        act.activation(whi[:, slot, :], raw[:, slot, :], ACT.Copy).then_inc(hi_ready, 1)

    def split_lo(dve, p, slot):
        dve.wait_ge(hi_ready, p + 1)
        if not isinstance(p, int) or p >= RING:
            dve.wait_ge(pair_done, p - (RING - 1))
        dve.tensor_tensor(wlo[:, slot, :], raw[:, slot, :], whi[:, slot, :].bitcast(F32), ALU.subtract).then_inc(lo_ready, 1)

    def three_passes(pe, dst, lhs, rhs, first, last, **kw):
        for n, (a, b) in enumerate(((lhs[0], rhs[0]), (lhs[0], rhs[1]), (lhs[1], rhs[0]))):
            done = pe.matmul(dst, a, b, start=first and n == 0, stop=last and n == 2, **kw)
        return done

    def pair_matmuls(pe, p, slot, form):
        pe.wait_ge(lo_ready, p + 1)
        w = [t[:, slot, :] for t in (whi, wlo)]
        if form == "BR1":
            q = p - (FFN1 - 10)
            for g in range(4):
                br = (4 * q + g) % 3
                dst = (pp[slot][:, g * 256:g * 256 + 256] if g < 2
                       else bank(slot)[:, (g - 2) * 256:(g - 2) * 256 + 256])
                for k in range(4):
                    y = [Y[:, 8 * part + br * 4 + k if br < 2 else 16 + 8 * part + k, :] for part in range(2)]
                    at = (g * 4 + k) * 128
                    done = three_passes(pe, dst, [u[:, at:at + 128] for u in w], y, k == 0, k == 3)
            done.then_inc(pair_done, 1)
            return
        x = [XH, XL]
        base = 0
        if form in ("Y0", "Y1"):
            x, base = None, 16 * (form == "Y1")
        for half in range(2):
            for k in range(KT):
                dst = pp[slot][:, half * 256:half * 256 + 256]
                if form == "A":
                    lhs = [u[:, k, half * 128:half * 128 + 128] for u in x]
                    rhs = [u[:, k * 256:k * 256 + 256] for u in w]
                else:
                    at = k * 256 + half * 128
                    lhs = [u[:, at:at + 128] for u in w]
                    rhs = ([u[:, k, :] for u in x] if x else [Y[:, base + 8 * part + k, :] for part in range(2)])
                done = three_passes(pe, dst, lhs, rhs, k == 0, k == KT - 1)
        done.then_inc(pair_done, 1)

    def evac_act(act, p, spec):
        form, kind, at, arg = spec
        ps = pp[p % RING]
        if kind in ("copy", "tanh", "copyA", "conv"):
            act.wait_ge(pair_done, p + 1)
        if kind == "copy":
            act.activation(P[:, at:at + 2, :], ps[:, :].rearrange("p (a t) -> p a t", a=2), ACT.Copy,
                           scale=arg).then_inc(S("act_taken"), 1)
        elif kind == "tanh":
            act.activation(P[:, at:at + 2, :], ps[:, :].rearrange("p (a t) -> p a t", a=2), ACT.Tanh,
                           scale=arg).then_inc(S("act_taken"), 1)
        elif kind == "copyA":
            act.activation(P[:, at:at + arg + 1:arg, :], ps[:, :].rearrange("p (a t) -> p a t", a=2),
                           ACT.Copy).then_inc(S("act_taken"), 1)
        elif kind == "conv":
            for h in range(2):
                act.activation(P[:, at + h, :], ps[:, h * 256:h * 256 + 256], ACT.Identity,
                               bias=col("conv_b", arg + h), scale=col("conv_w", 72 + arg + h)).then_inc(conv_started, 1)

    dve_count = {"conv": 0, "mix": 0}

    def evac_dve(dve, p, spec):
        form, kind, at, arg = spec
        ps = pp[p % RING]
        own = (S("dve_taken"), taken(p)[1])
        if kind == "conv":
            dve_count["conv"] += 2
            dve.wait_ge(conv_started, dve_count["conv"])
            for k in (2, 1, 0):
                lag = 3 - k
                for h in range(2):
                    i = dve.scalar_tensor_tensor(P[:, at + h, lag:], ps[:, h * 256:h * 256 + 256 - lag],
                                                 col("conv_w", 24 * k + arg + h), P[:, at + h, lag:],
                                                 ALU.mult, ALU.add)
                    if (k, h) == (0, 1):
                        i.then_inc(S("dve_taken"), 1)
                    else:
                        link(dve, i)
            dve.wait_ge(*own)
        elif kind == "mix2":
            dve.wait_ge(pair_done, p + 1)
            g = GATE2[arg] + 2 * at
            flat = ps[:, :].rearrange("p (a t) -> p a t", a=2)
            dst = HF[:, 2 * at:2 * at + 2, :] if arg == 0 else P[:, g:g + 2, :]
            dve.scalar_tensor_tensor(dst, P[:, g:g + 2, :], 1.0, flat, ALU.add, ALU.mult).then_inc(S("dve_taken"), 1)
            if arg:
                dve.wait_ge(*own)
                i = dve.tensor_tensor(HF[:, 2 * at:2 * at + 2, :], HF[:, 2 * at:2 * at + 2, :], P[:, g:g + 2, :], ALU.add)
                if arg == 2:
                    i.then_inc(S("mixed_ready2"), 1)
                else:
                    link(dve, i)
        elif kind == "mix1":
            dve.wait_ge(pair_done, p + 1)
            for g in range(4):
                m, br = divmod(4 * at + g, 3)
                src = (ps[:, g * 256:g * 256 + 256] if g < 2
                       else bank(p % RING)[:, (g - 2) * 256:(g - 2) * 256 + 256])
                gt = GATE1 + 8 * br + m
                dst = HF[:, m, :] if br == 0 else P[:, gt, :]
                i = dve.scalar_tensor_tensor(dst, P[:, gt, :], 1.0, src, ALU.add, ALU.mult)
                if g == 3:
                    i.then_inc(S("dve_taken"), 1)
                    dve.wait_ge(*own)
                else:
                    link(dve, i)
                if br:
                    i = dve.tensor_tensor(HF[:, m, :], HF[:, m, :], P[:, gt, :], ALU.add)
                    if br == 2:
                        i.then_inc(S("mixed_ready1"), 1)
                    else:
                        link(dve, i)
        elif kind == "resid":
            dve.wait_ge(pair_done, p + 1)
            dve.tensor_tensor(X[:, at:at + 2, :], X[:, at:at + 2, :],
                              ps[:, :].rearrange("p (a t) -> p a t", a=2), ALU.add).then_inc(S("dve_taken"), 1)

    def wait_evac(eng, p):
        found = {}
        for x in PAIR:
            if x <= p:
                who, n = taken(x)
                found[who] = n
        for who, n in found.items():
            eng.wait_ge(S(who), n)

    chains = {}

    def link(eng, ins):
        name = "chain_" + chains["names"][id(eng)]
        chains[name] = chains.get(name, 0) + 1
        ins.then_inc(S(name), 1)
        eng.wait_ge(S(name), chains[name])

    class Stream:

        def __init__(self, eng, who):
            self.eng, self.who, self.p = eng, who, 0
            chains.setdefault("names", {})[id(eng)] = who

        def start(self):
            for p in range(2):
                if self.who == "act":
                    split_hi(self.eng, p, p, 0)
                elif self.who == "dve":
                    split_lo(self.eng, p, p)

        def ahead(self, p):
            if p + 2 < NPAIRS:
                if self.who == "act":
                    split_hi(self.eng, p + 2, (p + 2) % RING, (p + 2) // RING)
                elif self.who == "dve":
                    split_lo(self.eng, p + 2, (p + 2) % RING)

        def evac(self, p):
            if p in PAIR:
                if self.who == "act":
                    evac_act(self.eng, p, PAIR[p])
                elif self.who == "dve":
                    evac_dve(self.eng, p, PAIR[p])

        def go(self, n=1):
            for _ in range(n):
                p = self.p
                if p >= self.stop:
                    return
                if self.who == "pe":
                    if p - RING in PAIR:
                        who, n = taken(p - RING)
                        self.eng.wait_ge(S(who), n)
                    pair_matmuls(self.eng, p, p % RING, PAIR[p][0])
                else:
                    self.ahead(p)
                    if p > self.first:
                        self.evac(p - 1)
                self.p += 1

        def window(self, first, n):
            assert self.p == first, (self.p, first)
            self.first, self.stop = first, first + n

        def finish(self):
            self.go(self.stop - self.p)
            if self.who != "pe":
                self.evac(self.stop - 1)

    def norm_pe(pe, n):
        for k in range(KT):
            if k % 2 == 0:
                pe.wait_ge(S("norm_squares"), 4 * n + k // 2 + 1)
            i = pe.matmul(bank(0)[:, 0:256], ones, P[:, SQ + k, :], start=k == 0, stop=k == KT - 1)
        i.then_inc(S("norm_sums"), 1)

    def norm_act(act, n, src, split):
        for k in range(0, KT, 2):
            act.activation(P[:, SQ + k:SQ + k + 2, :], src[:, k:k + 2, :], ACT.Square).then_inc(S("norm_squares"), 1)
        act.wait_ge(S("norm_sums"), n + 1)
        act.activation(RMS[:, :], bank(0)[:, 0:256], ACT.Sqrt, bias=SC[:, 127:128], scale=1.0 / D).then_inc(S("norm_rms"), 1)
        if split is not None:
            for k in range(0, KT, 2):
                act.wait_ge(S("norm_tiles"), 8 * split + k + 2)
                act.activation(XH[:, k:k + 2, :], HF[:, k:k + 2, :], ACT.Copy).then_inc(S("x_hi"), 1)

    def norm_dve(dve, n, src, gain, split, dst=None, done=None):
        dve.wait_ge(S("norm_rms"), n + 1)
        link(dve, dve.reciprocal(RCP[:, :], RMS[:, :]))
        for k in range(KT):
            if split is not None:
                dve.scalar_tensor_tensor(HF[:, k, :], src[:, k, :], col(gain, k), RCP[:, :], ALU.mult, ALU.mult)\
                   .then_inc(S("norm_tiles"), 1)
            elif done:
                dve.scalar_tensor_tensor(dst[:, k, :], src[:, k, :], col(gain, k), RCP[:, :], ALU.mult, ALU.mult)\
                   .then_inc(S(done), 1)
            else:
                link(dve, dve.scalar_tensor_tensor(src[:, k, :], src[:, k, :], col(gain, k), RCP[:, :], ALU.mult, ALU.mult))
                dve.tensor_tensor(X[:, k, :], X[:, k, :], src[:, k, :], ALU.add).then_inc(S("x_updated"), 1)
        if split is not None:
            lo_parts(dve, 4 * splits[split])

    splits = {0: 0, 1: 2, 2: 3, 3: 5}
    mixes = {1: 1, 2: 4}

    def lo_parts(dve, base, scale=1.0):
        for k in range(0, KT, 2):
            dve.wait_ge(S("x_hi"), base + k // 2 + 1)
            dve.scalar_tensor_tensor(XL[:, k:k + 2, :], HF[:, k:k + 2, :], scale, XH[:, k:k + 2, :].bitcast(F32),
                                     ALU.mult, ALU.subtract).then_inc(S("x_lo"), 1)

    def mix_act(act, b):
        for k in range(0, KT, 2):
            act.wait_ge(S(f"mixed_ready{b}"), k + 2 if b == 1 else k // 2 + 1)
            act.activation(XH[:, k:k + 2, :], HF[:, k:k + 2, :], ACT.Copy, scale=0.5).then_inc(S("x_hi"), 1)

    def x_ready(pe, rewrite):
        pe.wait_ge(S("x_lo"), 4 * rewrite + 4)

    L.update({k: v for k, v in locals().items() if k != "L"})
    mixers(nc, block, S, L)


def mixers(nc, block, S, L):
    (X, HF, XH, XL, Y, P, C, PC, G1W, IFW, DTW, G2W, PLW, RW, RMS, RCP, SM, SC, U, LR, DR, pp, pm, bank, ident, ones,
     col, link, Stream, pair_done, conv_started, hi_ready, lo_ready, norm_pe, norm_act, norm_dve, lo_parts,
     mix_act, x_ready, mixes, three_passes, whi, wlo, raw, arrived, split_hi, split_lo) = (
        L[k] for k in ("X HF XH XL Y P C PC G1W IFW DTW G2W PLW RW RMS RCP SM SC U LR DR pp pm bank ident ones "
                       "col link Stream pair_done conv_started hi_ready lo_ready norm_pe norm_act norm_dve lo_parts "
                       "mix_act x_ready mixes three_passes whi wlo raw arrived split_hi split_lo").split())
    eps1, eps4, one, eps16 = (SC[:, 127:128], SC[:, 126:127], SC[:, 125:126], SC[:, 124:125])

    def words(tile, start, n):
        return P[:, :, :].rearrange("p a t -> p (a t)")[:, tile * T + start:tile * T + start + n]

    def head_of(m, h):
        return C[:, CHEAD + 15 - h:CHEAD + 15 - h + m]

    def row_sel(rows, h, n=128, at=0):
        return C[at:at + rows, CIDENT + at + h:CIDENT + at + h + 1].to_broadcast([rows, n])

    def gated(r):
        if r == 0:
            return dict(nt=2, hp=2, dk=64, q=P[:, GQ:GQ + 2, :], k=P[:, GK:GK + 2, :], b=HF[:, 0:2, :], d=HF[:, 2:4, :],
                        z=HF[:, 4:6, :], A=34, o=GQ, r=GR, v=lambda v, h: words(GV + 2 * v, h * 128, 128),
                        scale=1.0 / 16, y=0, gain="gla_norm")
        h0 = 4 * (r - 1)
        return dict(nt=4, hp=1, dk=128, q=P[:, HQ + h0:HQ + h0 + 4, :], k=P[:, HK:HK + 4, :], b=P[:, HFG + h0:HFG + h0 + 4, :],
                    d=HF[:, 0:4, :], z=HF[:, 4:8, :], A=None, o=HQ + h0, r=HG + h0,
                    v=lambda v, h: words(HI + 4 * v, (h0 + h) * 128, 128), scale=1.0, y=h0, gain="hg_norm")

    def blocks(ap, half):
        return ap.rearrange("p a t -> p (a t)").rearrange("p (n w) -> p n w", w=2 * half)

    def a_words(g, h):
        at = score_slot(g, h) * 384
        return gated_a(g)[:, at:at + 384]

    def score_slot(g, h):
        tile, j = divmod(h, g["hp"])
        return j * 2 + tile if g["hp"] == 2 else h

    def gated_a(g):
        return words(g["A"], 0, 1536) if g["A"] is not None else U[:, 0:6, :].rearrange("p a t -> p (a t)")

    def level_mask(n, dt):
        m = C[:, CLEVEL + n * 128:CLEVEL + (n + 1) * 128]
        return (m.bitcast(dt) if dt != F32 else m).unsqueeze(1).unsqueeze(1).to_broadcast([128, 4, 2, 128])

    def gated_pe(pe, r, st):
        g = gated(r)
        if r == 0:
            pe.wait_ge(S("g1_copied"), 1)
            for t in range(2):
                i = pe.matmul(bank(3)[:, t * 256:t * 256 + 256], G2W[:, t * 128:t * 128 + 128], SM[0:16, 0:256], start=True, stop=True)
            i.then_inc(S("logit_ready"), 1)
        for n in range(9):
            if n == 0:
                pe.wait_ge(S("gated_inputs_ready"), r + 1)
            else:
                pe.wait_ge(S("gated_z_ready"), 2 * (8 * r + n))
            if n >= 2 or r:
                pe.wait_ge(S("scores_taken"), 9 * r + n - 1 if n >= 2 else 9 * r)
            if n <= 1 and r:
                pe.wait_ge(S("gated_y_done"), r)
            st.go(1 if n % 2 or r == 0 and n < 6 else 0)
            b0 = 1024 * (n % 2)
            for h in range(4):
                tile, j = divmod(h, g["hp"])
                rows = slice(j * g["dk"], (j + 1) * g["dk"])
                at_h = b0 + score_slot(g, h) * 256
                if n == 1:
                    i = pe.matmul(pm[:, at_h:at_h + 128], g["z"][rows, tile, 0:128],
                                  g["z"][rows, tile, 128:256], start=True, stop=True)
                    continue
                for u in range(2):
                    at = slice(u * 128, u * 128 + 128)
                    lhs, rhs = (g["k"], g["q"]) if n == 0 else (g["z"], g["z"])
                    i = pe.matmul(pm[:, at_h + u * 128:at_h + u * 128 + 128], lhs[rows, tile, at],
                                  rhs[rows, tile, at], start=True, stop=True)
            i.then_inc(S("scores_ready"), 1)
        pe.wait_ge(S("scores_taken"), 9 * r + 9)
        for h in range(4):
            o = pm[:, h * 256:h * 256 + 256]
            pe.matmul(o, g["v"](0, h), a_words(g, h)[:, 0:256], start=True, stop=False)
            i = pe.matmul(o[:, 128:256], g["v"](1, h), a_words(g, h)[:, 256:384], start=False, stop=True)
        i.then_inc(S("gated_o_ready"), 1)
        st.go(1)
        pe.wait_ge(S("gated_squares"), r + 1)
        for h in range(4):
            i = pe.matmul(bank(2)[0:4, 0:256], head_of(4, h), g["z_sq"][:, h, :] if "z_sq" in g else HF[:, 4 + h, :],
                          start=h == 0, stop=h == 3)
        i.then_inc(S("gated_sums"), 1)
        st.go(1)
        pe.wait_ge(S("gated_rsqrt"), r + 1)
        for h in range(4):
            i = pe.matmul(bank(3 + h // 2)[:, (h % 2) * 256:(h % 2) * 256 + 256], row_sel(4, h), SM[0:4, 256:512], start=True, stop=True)
        i.then_inc(S("gated_norm_spread"), 1)

    def gated_act(act, r, st):
        g = gated(r)
        n0 = g["nt"]
        if r == 0:
            act.wait_ge(S("logit_ready"), 1)
            for t in range(2):
                act.activation(HF[:, 2 + t, :], bank(3)[:, t * 256:t * 256 + 256], ACT.Identity, bias=col("gla_b_g", t))\
                   .then_inc(S("gate_logits"), 1)
        else:
            if r == 2:
                act.wait_ge(S("gated_y_done"), 2)
            act.activation(g["z"], g["q"], ACT.Tanh, scale=0.5).then_inc(S("hg_tanh"), 1)
            act.activation(g["k"], g["b"], ACT.Tanh, scale=0.5).then_inc(S("hg_tanh"), 1)
        act.wait_ge(S("gate_abs"), r + 1)
        link(act, act.activation(g["z"], g["z"], ACT.Exp))
        act.activation(g["z"], g["z"], ACT.Ln, bias=one).then_inc(S("gate_log"), 1)
        st.go(1 if r < 2 else 0)
        for n in range(8):
            act.wait_ge(S("gated_diff_ready"), 8 * r + n + 1)
            act.wait_ge(S("scores_ready"), 9 * r + n + 1)
            half = LEVELS[n]
            d, z = blocks(g["d"], half), blocks(g["z"], half)
            act.activation(z[:, :, half:], d[:, :, half:], ACT.Exp, scale=g["scale"]).then_inc(S("gated_exp"), 1)
            act.activation(z[:, :, :half], d[:, :, :half], ACT.Exp, scale=-g["scale"]).then_inc(S("gated_exp"), 1)
            st.go(1 if n % 2 == 0 or r == 0 and n < 5 else 0)
        act.wait_ge(S("gated_exp"), 2 * (8 * r + 8))
        act.activation(GD(g), P[:, g["r"]:g["r"] + 4, :], ACT.Tanh, scale=0.5).then_inc(S("gated_r_tanh"), 1)
        act.wait_ge(S("gated_o_ready"), r + 1)
        act.activation(P[:, g["o"]:g["o"] + 4, :], pm[:, 0:1024].rearrange("p (a t) -> p a t", a=4), ACT.Copy)\
           .then_inc(S("gated_o_copied"), 1)
        act.activation(HF[:, 4:8, :], pm[:, 0:1024].rearrange("p (a t) -> p a t", a=4), ACT.Square)\
           .then_inc(S("gated_squares"), 1)
        st.go(1)
        act.wait_ge(S("gated_sums"), r + 1)
        act.activation(SM[0:4, 0:256], bank(2)[0:4, 0:256], ACT.Sqrt, bias=eps4[0:4], scale=4.0 / 128).then_inc(S("gated_rms"), 1)
        st.go(1)
        act.wait_ge(S("gated_y_ready"), r + 1)
        act.activation(Y[:, g["y"]:g["y"] + 4, :], P[:, g["o"]:g["o"] + 4, :], ACT.Copy).then_inc(S("gated_y_hi"), 1)

    def GD(g):
        return HF[:, 0:4, :]

    def gated_dve(dve, r, st):
        g = gated(r)
        logits = HF[:, 2:4, :] if r == 0 else g["b"]
        if r == 0:
            dve.wait_ge(S("gate_logits"), 2)
        else:
            dve.wait_ge(S("hg_tanh"), 2 * r - 1)
            link(dve, dve.scalar_tensor_tensor(g["q"], g["z"], 1.0, g["q"], ALU.add, ALU.mult))
            dve.wait_ge(S("hg_tanh"), 2 * r)
            link(dve, dve.tensor_scalar(g["k"], g["k"], -0.25, 0.25, ALU.mult, ALU.add))
        dve.scalar_tensor_tensor(g["z"], logits, -1.0, logits, ALU.mult, ALU.min).then_inc(S("gate_abs"), 1)
        dve.wait_ge(S("gate_log"), r + 1)
        link(dve, dve.scalar_tensor_tensor(g["d"], logits, 0.0, g["z"], ALU.min, ALU.subtract))
        for t in range(g["nt"]):
            i = dve.tensor_tensor_scan(g["b"][:, t, :], C[:, CONES:CONES + 256], g["d"][:, t, :], 0.0, ALU.mult, ALU.add)
            if t < g["nt"] - 1:
                link(dve, i)
        i.then_inc(S("gated_inputs_ready"), 1)
        dve.wait_ge(S("gated_inputs_ready"), r + 1)
        A = gated_a(g).rearrange("p (h j t) -> p h j t", h=4, j=3)

        def take(n):
            dve.wait_ge(S("scores_ready"), 9 * r + n + 1)
            ps = pm[:, 1024 * (n % 2):1024 * (n % 2) + 1024].rearrange("p (h u t) -> p h u t", h=4, u=2)
            if n == 0:
                i = dve.tensor_tensor(A[:, :, 0::2, :], ps, level_mask(7, F32), ALU.mult)
            elif n == 1:
                i = dve.tensor_copy(A[:, :, 1, :], ps[:, :, 0, :])
            else:
                i = dve.copy_predicated(A[:, :, 0::2, :], level_mask(n - 2, I32), ps)
            i.then_inc(S("scores_taken"), 1)
            dve.wait_ge(S("scores_taken"), 9 * r + n + 1)

        for n in range(8):
            half = LEVELS[n]
            b, d, z, q, k = (blocks(g[x], half) for x in "bdzqk")
            if n:
                dve.wait_ge(S("gated_exp"), 2 * (8 * r + n))
            dve.tensor_tensor(d, b, b[:, :, half - 1:half].to_broadcast(list(b.shape)), ALU.subtract).then_inc(S("gated_diff_ready"), 1)
            take(n)
            st.go(1 if n % 2 == 0 or r == 0 and n < 5 else 0)
            dve.wait_ge(S("gated_exp"), 2 * (8 * r + n) + 2)
            dve.tensor_tensor(z[:, :, half:], z[:, :, half:], q[:, :, half:], ALU.mult).then_inc(S("gated_z_ready"), 1)
            dve.tensor_tensor(z[:, :, :half], z[:, :, :half], k[:, :, :half], ALU.mult).then_inc(S("gated_z_ready"), 1)
        take(8)
        dve.wait_ge(S("gated_r_tanh"), r + 1)
        link(dve, dve.scalar_tensor_tensor(GD(g), GD(g), 1.0, P[:, g["r"]:g["r"] + 4, :], ALU.add, ALU.mult))
        dve.wait_ge(S("gated_o_copied"), r + 1)
        o = P[:, g["o"]:g["o"] + 4, :]
        link(dve, dve.scalar_tensor_tensor(o, o, col(g["gain"]), GD(g), ALU.mult, ALU.mult))
        st.go(1)
        dve.wait_ge(S("gated_rms"), r + 1)
        dve.reciprocal(SM[0:4, 256:512], SM[0:4, 0:256]).then_inc(S("gated_rsqrt"), 1)
        st.go(1)
        dve.wait_ge(S("gated_norm_spread"), r + 1)
        dve.tensor_tensor(o, o, pm[:, 1536:2560].rearrange("p (a t) -> p a t", a=4), ALU.mult).then_inc(S("gated_y_ready"), 1)
        dve.wait_ge(S("gated_y_hi"), r + 1)
        dve.tensor_tensor(Y[:, 8 + g["y"]:12 + g["y"], :], o, Y[:, g["y"]:g["y"] + 4, :].bitcast(F32), ALU.subtract)\
           .then_inc(S("gated_y_done"), 1)

    def head_rows(h):
        return slice(64 * (h % 2), 64 * (h % 2) + 64), h // 2

    def moba_pe(pe, st):
        for h in range(8):
            rows, tile = head_rows(h)
            q, k = P[rows, MQ + tile, :], P[rows, MK + tile, :]
            if h >= 2:
                pe.wait_ge(S("moba_max"), 2 * (h - 1))
            for u in range(2):
                s = bank(h % 2)[:, u * 128:u * 128 + (u + 1) * 128]
                pe.matmul(s, q[:, u * 128:u * 128 + 128], k[:, 0:(u + 1) * 128], start=True, stop=False)
                pe.matmul(s, row_sel(8, h), C[0:8, CALIBI:CALIBI + (u + 1) * 128], start=False, stop=False)
                i = pe.matmul(s[:, u * 128:u * 128 + 128], ident, C[:, CMASKT:CMASKT + 128], start=False, stop=True)
            i.then_inc(S("moba_scores"), 1)
            st.go(1 if h % 2 else 0)
        pe.wait_ge(S("moba_max"), 16)
        for u in range(2):
            i = pe.matmul(bank(2)[0:8, u * 128:u * 128 + 128], SC[:, 72 + 8 * u:80 + 8 * u], ident, start=True, stop=True)
        i.then_inc(S("moba_max_rows"), 1)
        pe.wait_ge(S("moba_max_copied"), 1)
        for h in range(9):
            if h < 8:
                rows, tile = head_rows(h)
                q, k = P[rows, MQ + tile, :], P[rows, MK + tile, :]
                if h >= 2:
                    pe.wait_ge(S("moba_exp"), 2 * (h - 1))
                for v in range(2):
                    s = bank(h % 2)[:, 0:256] if v == 0 else bank(h % 2)[:, 256:384]
                    pe.matmul(s, k[:, v * 128:v * 128 + 128], q[:, v * 128:256], start=True, stop=False)
                    pe.matmul(s, row_sel(8, h), SM[0:8, v * 128:256], start=False, stop=False)
                    i = pe.matmul(s[:, 0:128], ident, C[:, CMASK:CMASK + 128], start=False, stop=True)
                i.then_inc(S("moba_scores_t"), 1)
                st.go(1)
            if h:
                moba_values(pe, h - 1)
        pe.wait_ge(S("moba_recip"), 1)
        pe.wait_ge(S("moba_o_copied"), 2)
        for h in range(8):
            rows, t = head_rows(h)
            i = pe.matmul(bank(t // 2)[rows, (t % 2) * 256:(t % 2) * 256 + 256], row_sel(8, h, 64), SM[0:8, 512:768],
                          start=True, stop=True)
        i.then_inc(S("moba_spread"), 1)

    def moba_values(pe, h):
        rows, tile = head_rows(h)
        w = words(4, (h % 2) * 384, 384)
        pe.wait_ge(S("moba_exp"), 2 * h + 2)
        pe.matmul(bank(2)[0:8, 0:256], head_of(8, h), w[:, 0:256], start=h == 0, stop=False)
        pe.matmul(bank(2)[0:8, 128:256], head_of(8, h), w[:, 256:384], start=False, stop=h == 7).then_inc(S("moba_den"), 1)
        o = bank(3 + tile // 2)[rows, (tile % 2) * 256:(tile % 2) * 256 + 256]
        pe.matmul(o, words(MV, h * 64, 64), w[:, 0:256], start=True, stop=False)
        pe.matmul(o[:, 128:256], words(MV + 2, h * 64, 64), w[:, 256:384], start=False, stop=True).then_inc(S("moba_o"), 1)

    def moba_act(act, st):
        st.go(2)
        for h in range(4):
            st.go(1 if h % 2 else 0)
        act.wait_ge(S("moba_max_rows"), 1)
        act.activation(SM[0:8, 0:256], bank(2)[0:8, 0:256], ACT.Copy).then_inc(S("moba_max_copied"), 1)
        for h in range(8):
            w = words(4, (h % 2) * 384, 384)
            act.wait_ge(S("moba_scores_t"), h + 1)
            if h >= 2:
                act.wait_ge(S("moba_o"), h - 1)
            for v in range(2):
                s = bank(h % 2)[:, 0:256] if v == 0 else bank(h % 2)[:, 256:384]
                act.activation(w[:, 0:256] if v == 0 else w[:, 256:384], s, ACT.Exp,
                               bias=C[:, CALCOL + v * 8 + h:CALCOL + v * 8 + h + 1]).then_inc(S("moba_exp"), 1)
            st.go(1)
        act.wait_ge(S("moba_o"), 8)
        for b in range(2):
            act.activation(P[:, 8 + 2 * b:10 + 2 * b, :], bank(3 + b).rearrange("p (a t) -> p a t", a=2), ACT.Copy)\
               .then_inc(S("moba_o_copied"), 1)
        act.wait_ge(S("moba_y"), 1)
        act.activation(Y[:, 16:20, :], P[:, 8:12, :], ACT.Copy).then_inc(S("moba_y_hi"), 1)
        act.wait_ge(S("pool_mm"), 1)
        for g in range(4):
            act.activation(P[:, g, :], pm[:, 1536 + g * 256:1792 + g * 256], ACT.Copy, scale=col("pool_scale", g))\
               .then_inc(S("pool_y"), 1)
        act.wait_ge(S("pool_y"), 4)
        act.activation(Y[:, 4:8, :], P[:, 0:4, :], ACT.Copy).then_inc(S("pool_y_hi"), 1)

    def moba_dve(dve, st):
        for h in range(8):
            dve.wait_ge(S("moba_scores"), h + 1)
            for u in range(2):
                dve.tensor_reduce(SC[:, 72 + 8 * u + h:73 + 8 * u + h], bank(h % 2)[:, u * 128:u * 128 + (u + 1) * 128],
                                  AX.X, ALU.max, negate=True).then_inc(S("moba_max"), 1)
            st.go(1 if h % 2 else 0)
        for g in range(4):
            u, a = P[:, PU + g, :], P[:, g, :]
            link(dve, dve.tensor_copy(a, u))
            for n in range(g + 1):
                src, dst = (P[:, g, :], P[:, 7, :]) if n % 2 == 0 else (P[:, 7, :], P[:, g, :])
                lag = 1 << n
                link(dve, dve.tensor_tensor(dst[:, lag:], src[:, lag:], src[:, :T - lag], ALU.add))
                link(dve, dve.tensor_copy(dst[:, :lag], src[:, :lag]))
            s = P[:, 7, :] if g % 2 == 0 else P[:, g, :]
            link(dve, dve.tensor_tensor(s[:, 0:16], s[:, 0:16], C[:, CINV + 16 * g:CINV + 16 * g + 16], ALU.mult))
            link(dve, dve.tensor_scalar(s[:, 16:], s[:, 16:], 1.0 / (2 << g), None, ALU.mult))
            dve.tensor_tensor(u, s, u, ALU.subtract).then_inc(S("pool_p"), 1)
            dve.wait_ge(S("pool_p"), g + 1)
            st.go(2)
        dve.wait_ge(S("moba_den"), 8)
        dve.reciprocal(SM[0:8, 512:768], bank(2)[0:8, 0:256]).then_inc(S("moba_recip"), 1)
        dve.wait_ge(S("moba_spread"), 1)
        o = P[:, 8:12, :]
        dve.tensor_tensor(o, o, pm[:, 0:1024].rearrange("p (a t) -> p a t", a=4), ALU.mult).then_inc(S("moba_y"), 1)
        dve.wait_ge(S("moba_y_hi"), 1)
        dve.tensor_tensor(Y[:, 24:28, :], o, Y[:, 16:20, :].bitcast(F32), ALU.subtract).then_inc(S("y1_ready"), 1)
        dve.wait_ge(S("pool_y_hi"), 1)
        dve.tensor_tensor(Y[:, 12:16, :], P[:, 0:4, :], Y[:, 4:8, :].bitcast(F32), ALU.subtract).then_inc(S("y1_ready"), 1)

    def pool_pe(pe, st):
        pe.wait_ge(S("pool_p"), 4)
        pe.wait_ge(S("moba_o_copied"), 2)
        for g in range(4):
            i = pe.matmul(pm[:, 1536 + g * 256:1792 + g * 256], PLW[:, g * 128:g * 128 + 128], P[:, PU + g, :], start=True, stop=True)
        i.then_inc(S("pool_mm"), 1)

    def rows_pe(pe, st):
        for j in range(2):
            for k in range(KT):
                i = pe.matmul(bank(4)[32:36, j * 256:j * 256 + 256], IFW[:, k * 8 + 4 * j:k * 8 + 4 * j + 4], HF[:, k, :], start=k == 0, stop=k == KT - 1)
        for k in range(KT):
            i = pe.matmul(bank(3)[0:16, 0:256], DTW[:, k * 16:k * 16 + 16], HF[:, k, :], start=k == 0, stop=k == KT - 1)
        i.then_inc(S("rows_projected"), 1)
        st.go(3)
        pe.wait_ge(S("rows_ready"), 1)
        for v in range(2):
            at = slice(v * 128, v * 128 + 128)
            pe.matmul(bank(2)[:, v * 4:v * 4 + 4], LR[:, 2, at], C[32:36, CIDENT + 32:CIDENT + 36], start=True, stop=True)
            pe.matmul(bank(3)[:, v * 16:16 + v * 16], DR[:, 2, at], C[0:16, CIDENT:CIDENT + 16], start=True, stop=True)
            i = pe.matmul(bank(3)[:, 32 + v * 16:48 + v * 16], DR[:, 0, at], C[0:16, CIDENT:CIDENT + 16], start=True, stop=True)
        i.then_inc(S("columns_ready"), 1)

    def rows_act(act, st):
        act.wait_ge(S("rows_projected"), 1)
        act.activation(LR[:, 0, :], bank(4)[32:36, 0:256], ACT.Identity, bias=RW[32:36, 0:1]).then_inc(S("rows_biased"), 1)
        act.activation(LR[:, 1, :], bank(4)[32:36, 256:512], ACT.Identity, bias=RW[32:36, 1:2]).then_inc(S("rows_biased"), 1)
        act.activation(DR[:, 0, :], bank(3)[0:16, 0:256], ACT.Identity, bias=RW[0:16, 2:3]).then_inc(S("rows_biased"), 1)
        act.activation(RW[0:16, 4:5], RW[0:16, 3:4], ACT.Exp).then_inc(S("rows_biased"), 1)
        act.wait_ge(S("rows_abs"), 2)
        link(act, act.activation(LR[:, 4, :], LR[:, 4, :], ACT.Exp))
        link(act, act.activation(DR[:, 3, :], DR[:, 3, :], ACT.Exp))
        act.activation(LR[:, 4, :], LR[:, 4, :], ACT.Ln, bias=one[32:36]).then_inc(S("rows_log"), 1)
        act.activation(DR[:, 3, :], DR[:, 3, :], ACT.Ln, bias=one[0:16]).then_inc(S("rows_log"), 1)
        st.go(2)
        act.wait_ge(S("columns_ready"), 1)
        act.activation(SC[:, 0:8], bank(2)[:, 0:8], ACT.Copy).then_inc(S("columns_copied"), 1)
        act.activation(SC[:, 8:72], bank(3)[:, 0:64], ACT.Copy).then_inc(S("columns_copied"), 1)
        act.activation(LR[:, 5, :], LR[:, 5, :], ACT.Exp, scale=-1.0).then_inc(S("exp_minus_m"), 1)

    def rows_dve(dve, st):
        dve.wait_ge(S("rows_biased"), 4)
        dve.scalar_tensor_tensor(LR[:, 4, :], LR[:, 1, :], -1.0, LR[:, 1, :], ALU.mult, ALU.min).then_inc(S("rows_abs"), 1)
        dve.scalar_tensor_tensor(DR[:, 3, :], DR[:, 0, :], -1.0, DR[:, 0, :], ALU.mult, ALU.min).then_inc(S("rows_abs"), 1)
        st.go(1)
        dve.wait_ge(S("rows_log"), 2)
        link(dve, dve.scalar_tensor_tensor(LR[:, 4, :], LR[:, 1, :], 0.0, LR[:, 4, :], ALU.min, ALU.subtract))
        link(dve, dve.tensor_tensor_scan(LR[:, 1, :], C[32:36, CONES:CONES + 256], LR[:, 4, :], 0.0, ALU.mult, ALU.add))
        link(dve, dve.tensor_tensor(LR[:, 2, :], LR[:, 0, :], LR[:, 1, :], ALU.subtract))
        link(dve, dve.memset(LR[:, 0, :], 0.0))
        link(dve, dve.tensor_tensor_scan(LR[:, 3, :], LR[:, 2, :], LR[:, 0, :], 0.0, ALU.max, ALU.add))
        link(dve, dve.tensor_tensor(LR[:, 5, :], LR[:, 1, :], LR[:, 3, :], ALU.add))
        link(dve, dve.tensor_scalar(LR[:, 3, :], LR[:, 3, :], -1.0, None, ALU.mult))
        link(dve, dve.scalar_tensor_tensor(DR[:, 0, :], DR[:, 0, :], 0.0, DR[:, 3, :], ALU.max, ALU.add))
        link(dve, dve.tensor_scalar(DR[:, 3, :], DR[:, 0, :], RW[0:16, 4:5], -1.0, ALU.mult, ALU.mult))
        link(dve, dve.tensor_tensor_scan(DR[:, 1, :], C[0:16, CONES:CONES + 256], DR[:, 3, :], 0.0, ALU.mult, ALU.add))
        dve.tensor_scalar(DR[:, 2, :], DR[:, 1, :], -1.0, None, ALU.mult).then_inc(S("rows_ready"), 1)
        st.go(1)

    def decay_matmuls(pe, dst, rows, h, src, at=0):
        for v in range(2):
            s = dst[:, 0:256] if v == 0 else dst[:, 256:384]
            pe.matmul(s, row_sel(rows, h, at=at), src[:, v * 128:256], start=True, stop=False)
            i = pe.matmul(s[:, 0:128], ident, C[:, CMASK:CMASK + 128], start=False, stop=True)
        return i

    EW = 16

    def mlstm_pe(pe, st):
        for h in range(5):
            if h < 4:
                if h == 0:
                    pe.wait_ge(S("lm_silu"), 2)
                    pe.wait_ge(S("columns_copied"), 2)
                else:
                    pe.wait_ge(S("lm_w"), 2 * h)
                q, k = P[:, LQ + h, :], P[:, LK + h, :]
                pe.matmul(bank(0)[:, 0:256], k[:, 0:128], q, start=True, stop=True)
                pe.matmul(bank(0)[:, 256:384], k[:, 128:256], q[:, 128:256], start=True, stop=True)
                decay_matmuls(pe, bank(1), 4, h, LR[:, 3, :], 32).then_inc(S("lm_scores"), 1)
                st.go(1)
            if h:
                n = h - 1
                w = words(EW, 768 + (n % 2) * 384, 384)
                pe.wait_ge(S("lm_w"), 2 * n + 2)
                if n >= 2:
                    pe.wait_ge(S("lm_h_copied"), 2 * (n - 1))
                pe.matmul(bank(2)[32:36, 0:256], head_of(4, n), w[:, 0:256], start=n == 0, stop=False, skip_group_check=True)
                pe.matmul(bank(2)[32:36, 128:256], head_of(4, n), w[:, 256:384], start=False, stop=n == 3, skip_group_check=True)
                for j in range(2):
                    o = bank(3 + n % 2)[:, j * 256:j * 256 + 256]
                    at = n * 256 + j * 128
                    pe.matmul(o, words(LV, at, 128), w[:, 0:256], start=True, stop=False)
                    i = pe.matmul(o[:, 128:256], words(LV + 4, at, 128), w[:, 256:384], start=False, stop=True)
                i.then_inc(S("lm_h"), 1)
                st.go(1)
                pe.wait_ge(S("lm_h_copied"), 2 * n + 2)
                for j in range(2):
                    i = pe.matmul(bank(2)[32:36, 256:512], head_of(4, n), P[:, EW + 6 + j, :], start=False,
                                  stop=n == 3 and j == 1, skip_group_check=True)
                i.then_inc(S("lm_sums"), 1)
        st.go(1)
        pe.wait_ge(S("lm_comb"), 1)
        for h in range(4):
            i = pe.matmul(pm[:, h * 256:h * 256 + 256], row_sel(4, h, at=32), LR[:, 2, :], start=True, stop=True)
        i.then_inc(S("lm_spread"), 1)

    def mlstm_act(act, st):
        for b in range(2):
            if b == 0:
                act.wait_ge(S("gated_y_done"), 3)
            act.activation(HF[:, 4 * b:4 * b + 4, :], P[:, LQ + 4 * b:LQ + 4 * b + 4, :], ACT.Tanh, scale=0.5).then_inc(S("lm_tanh"), 1)
        for h in range(4):
            st.go(1)
            e = words(EW, (h % 2) * 384, 384)
            act.wait_ge(S("lm_scores"), h + 1)
            if h >= 2:
                act.wait_ge(S("lm_w"), 2 * (h - 1))
            for v in range(2):
                at = slice(0, 256) if v == 0 else slice(256, 384)
                act.activation(e[:, at], bank(1)[:, at], ACT.Exp, bias=SC[:, v * 4 + h:v * 4 + h + 1]).then_inc(S("lm_exp"), 1)
            st.go(1)
            act.wait_ge(S("lm_h"), h + 1)
            if h == 0:
                act.wait_ge(S("lm_silu"), 2)
            else:
                act.wait_ge(S("lm_sums"), h)
            o = bank(3 + h % 2).rearrange("p (a t) -> p a t", a=2)
            act.activation(HF[:, 2 * h:2 * h + 2, :], o, ACT.Copy).then_inc(S("lm_h_copied"), 1)
            act.activation(P[:, EW + 6:EW + 8, :], o, ACT.Square).then_inc(S("lm_h_copied"), 1)
        act.wait_ge(S("lm_ms"), 1)
        act.activation(LR[:, 1, :], LR[:, 1, :], ACT.Sqrt, bias=eps4[32:36], scale=4.0 / 256).then_inc(S("lm_rms"), 1)
        st.go(1)
        for b in range(2):
            act.wait_ge(S("lm_y"), b + 1)
            act.activation(Y[:, 16 + 4 * b:20 + 4 * b, :], HF[:, 4 * b:4 * b + 4, :], ACT.Copy).then_inc(S("lm_y_hi"), 1)

    def mlstm_dve(dve, st):
        for b in range(2):
            dve.wait_ge(S("lm_tanh"), b + 1)
            x = P[:, LQ + 4 * b:LQ + 4 * b + 4, :]
            dve.scalar_tensor_tensor(x, HF[:, 4 * b:4 * b + 4, :], 1.0, x, ALU.add, ALU.mult).then_inc(S("lm_silu"), 1)
        for h in range(4):
            st.go(1)
            e, w = words(EW, (h % 2) * 384, 384), words(EW, 768 + (h % 2) * 384, 384)
            if h >= 2:
                dve.wait_ge(S("lm_h"), h - 1)
            for v in range(2):
                at = slice(0, 256) if v == 0 else slice(256, 384)
                dve.wait_ge(S("lm_exp"), 2 * h + v + 1)
                dve.scalar_tensor_tensor(w[:, at], bank(0)[:, at], 0.25 * 128 ** -0.5, e[:, at], ALU.mult, ALU.mult).then_inc(S("lm_w"), 1)
            st.go(1)
        dve.wait_ge(S("lm_sums"), 4)
        dve.wait_ge(S("exp_minus_m"), 1)
        a, b, c = (LR[:, n, :] for n in range(3))
        link(dve, dve.tensor_copy(a, bank(2)[32:36, 0:256]))
        link(dve, dve.scalar_tensor_tensor(a, a, -1.0, a, ALU.mult, ALU.max))
        link(dve, dve.tensor_tensor(a, a, LR[:, 5, :], ALU.max))
        link(dve, dve.reciprocal(a, a))
        link(dve, dve.tensor_tensor(b, bank(2)[32:36, 256:512], a, ALU.mult))
        dve.tensor_tensor(b, b, a, ALU.mult).then_inc(S("lm_ms"), 1)
        dve.wait_ge(S("lm_rms"), 1)
        link(dve, dve.reciprocal(c, b))
        dve.tensor_tensor(c, c, a, ALU.mult).then_inc(S("lm_comb"), 1)
        st.go(1)
        dve.wait_ge(S("lm_spread"), 1)
        for h in range(4):
            for j in range(2):
                t = HF[:, 2 * h + j, :]
                link(dve, dve.scalar_tensor_tensor(t, t, col("ml_norm", j), pm[:, h * 256:h * 256 + 256], ALU.mult, ALU.mult))
            if h % 2:
                b = h // 2
                t = HF[:, 4 * b:4 * b + 4, :]
                dve.scalar_tensor_tensor(t, P[:, LO + 4 * b:LO + 4 * b + 4, :], 1.0, t, ALU.add, ALU.mult).then_inc(S("lm_y"), 1)
        for b in range(2):
            dve.wait_ge(S("lm_y_hi"), b + 1)
            dve.tensor_tensor(Y[:, 24 + 4 * b:28 + 4 * b, :], HF[:, 4 * b:4 * b + 4, :], Y[:, 16 + 4 * b:20 + 4 * b, :].bitcast(F32),
                              ALU.subtract).then_inc(S("lm_y_done"), 1)

    TMP, CB, MW = 24, 48, 8

    def cb_words(g):
        return words(CB, g * 384, 384) if g < 3 else words(MW, 1536, 384)

    def ssd_pe(pe, st):
        pe.wait_ge(S("mb_silu"), 4)
        for g in range(4):
            if g >= 2:
                pe.wait_ge(S("mb_cb"), g - 1)
            b = bank(g % 2)
            pe.matmul(b[:, 0:256], P[:, XB + g, 0:128], P[:, XC + g, :], start=True, stop=True)
            pe.matmul(b[:, 256:384], P[:, XB + g, 128:256], P[:, XC + g, 128:256], start=True, stop=True).then_inc(S("mb_bc"), 1)
        for n in range(4):
            v, q = divmod(n, 2)
            if n >= 2:
                pe.wait_ge(S("mb_xt"), n - 1)
            for j in range(4):
                i = pe.matmul(bank(2 + n % 2)[:, j * 128:j * 128 + 128], P[:, XS + 4 * q + j, v * 128:v * 128 + 128], ident, start=True, stop=True)
            i.then_inc(S("mb_xtp"), 1)
        pe.wait_ge(S("mb_xt"), 4)
        pe.wait_ge(S("mb_cb"), 4)
        for h in range(17):
            if h < 16:
                if h >= 2:
                    pe.wait_ge(S("mb_exp"), 2 * (h - 1))
                decay_matmuls(pe, bank(h % 2), 16, h, DR[:, 1, :]).then_inc(S("mb_decay"), 1)
                st.go(1)
            if h:
                n = h - 1
                w = words(MW, 768 + (n % 2) * 384, 384)
                pe.wait_ge(S("mb_w"), 2 * n + 2)
                if n >= 4 and n % 2 == 0:
                    pe.wait_ge(S("mb_y"), n // 2 - 1)
                o = bank(2 + (n // 2) % 2)[64 * (n % 2):64 * (n % 2) + 64, 0:256]
                pe.matmul(o, words(TMP, n * 64, 64), w[:, 0:256], start=True, stop=False)
                pe.matmul(o[:, 128:256], words(TMP + 4, n * 64, 64), w[:, 256:384], start=False, stop=True).then_inc(S("mb_o"), 1)
        for t in range(8):
            if t % 4 == 0:
                pe.wait_ge(S("mb_squares"), t // 4 + 1)
            i = pe.matmul(bank(4)[0:4, 0:256], head_of(4, t // 2), P[:, TMP + t, :], start=t == 0, stop=t == 7)
        i.then_inc(S("mb_sums"), 1)
        st.go(1)
        pe.wait_ge(S("mb_rsqrt"), 1)
        for g in range(4):
            i = pe.matmul(pm[:, g * 256:g * 256 + 256], row_sel(4, g), SM[0:4, 256:512], start=True, stop=True)
        i.then_inc(S("mb_spread"), 1)

    def ssd_act(act, st):
        for n, at in enumerate((XB, XS, XZ)):
            if n == 0:
                act.wait_ge(S("lm_y_done"), 2)
            else:
                act.wait_ge(S("mb_silu"), 2 * n)
            for b in range(2):
                act.activation(P[:, TMP + 4 * b:TMP + 4 * b + 4, :], P[:, at + 4 * b:at + 4 * b + 4, :], ACT.Tanh, scale=0.5).then_inc(S("mb_tanh"), 1)
        for g in range(4):
            act.wait_ge(S("mb_bc"), g + 1)
            act.activation(cb_words(g), bank(g % 2)[:, 0:384], ACT.Copy, scale=0.25).then_inc(S("mb_cb"), 1)
        act.wait_ge(S("mb_silu"), 6)
        for n in range(4):
            v, q = divmod(n, 2)
            act.wait_ge(S("mb_xtp"), n + 1)
            act.activation(words(TMP, v * 1024 + q * 512, 512), bank(2 + n % 2), ACT.Copy).then_inc(S("mb_xt"), 1)
        for h in range(16):
            e = words(MW, (h % 2) * 384, 384)
            act.wait_ge(S("mb_decay"), h + 1)
            if h >= 2:
                act.wait_ge(S("mb_w"), 2 * (h - 1))
            for v in range(2):
                at = slice(0, 256) if v == 0 else slice(256, 384)
                act.activation(e[:, at], bank(h % 2)[:, at], ACT.Exp, bias=SC[:, 8 + v * 16 + h:9 + v * 16 + h]).then_inc(S("mb_exp"), 1)
            st.go(1)
        for b in range(2):
            act.wait_ge(S("mb_u"), b + 1)
            act.activation(P[:, TMP + 4 * b:TMP + 4 * b + 4, :], P[:, XS + 4 * b:XS + 4 * b + 4, :], ACT.Square).then_inc(S("mb_squares"), 1)
        act.wait_ge(S("mb_sums"), 1)
        act.activation(SM[0:4, 0:256], bank(4)[0:4, 0:256], ACT.Sqrt, bias=eps16[0:4], scale=1.0 / 256).then_inc(S("mb_rms"), 1)
        st.go(1)
        act.wait_ge(pair_done, Y0_READ)
        for b in range(2):
            act.wait_ge(S("mb_yn"), b + 1)
            act.activation(Y[:, 4 * b:4 * b + 4, :], P[:, XS + 4 * b:XS + 4 * b + 4, :], ACT.Copy).then_inc(S("mb_y_hi"), 1)

    def ssd_dve(dve, st):
        for n, at in enumerate((XB, XS, XZ)):
            for b in range(2):
                dve.wait_ge(S("mb_tanh"), 2 * n + b + 1)
                x = P[:, at + 4 * b:at + 4 * b + 4, :]
                dve.scalar_tensor_tensor(x, P[:, TMP + 4 * b:TMP + 4 * b + 4, :], 1.0, x, ALU.add, ALU.mult).then_inc(S("mb_silu"), 1)
        for h in range(17):
            if h < 16:
                e, w = words(MW, (h % 2) * 384, 384), words(MW, 768 + (h % 2) * 384, 384)
                if h == 0:
                    dve.wait_ge(S("mb_cb"), 4)
                if h >= 2:
                    dve.wait_ge(S("mb_o"), h - 1)
                for v in range(2):
                    at = slice(0, 256) if v == 0 else slice(256, 384)
                    dve.wait_ge(S("mb_exp"), 2 * h + v + 1)
                    dve.scalar_tensor_tensor(w[:, at], e[:, at], SC[:, 40 + v * 16 + h:41 + v * 16 + h],
                                             cb_words(h // 4)[:, at], ALU.mult, ALU.mult).then_inc(S("mb_w"), 1)
                st.go(1)
            if h and h % 2 == 0:
                t = h // 2 - 1
                dve.wait_ge(S("mb_o"), h)
                x = P[:, XS + t, :]
                dve.scalar_tensor_tensor(x, x, col("mb_d", t), bank(2 + t % 2)[:, 0:256], ALU.mult, ALU.add).then_inc(S("mb_y"), 1)
        dve.wait_ge(S("mb_y"), 8)
        for b in range(2):
            x = P[:, XS + 4 * b:XS + 4 * b + 4, :]
            dve.tensor_tensor(x, x, P[:, XZ + 4 * b:XZ + 4 * b + 4, :], ALU.mult).then_inc(S("mb_u"), 1)
        dve.wait_ge(S("mb_rms"), 1)
        dve.reciprocal(SM[0:4, 256:512], SM[0:4, 0:256]).then_inc(S("mb_rsqrt"), 1)
        st.go(1)
        dve.wait_ge(S("mb_spread"), 1)
        for t in range(8):
            x = P[:, XS + t, :]
            i = dve.scalar_tensor_tensor(x, x, col("mb_norm", t), pm[:, (t // 2) * 256:(t // 2) * 256 + 256], ALU.mult, ALU.mult)
            if t % 4 == 3:
                i.then_inc(S("mb_yn"), 1)
            else:
                link(dve, i)
        dve.wait_ge(S("mb_yn"), 2)
        for b in range(2):
            dve.wait_ge(S("mb_y_hi"), b + 1)
            dve.tensor_tensor(Y[:, 8 + 4 * b:12 + 4 * b, :], P[:, XS + 4 * b:XS + 4 * b + 4, :], Y[:, 4 * b:4 * b + 4, :].bitcast(F32),
                              ALU.subtract).then_inc(S("mb_y_done"), 1)

    Y0_READ = BLK2 + 12 + 12 + 16 + 4 + 4
    L.update({k: v for k, v in locals().items() if k != "L"})
    feed_forward(nc, block, S, L)


def feed_forward(nc, block, S, L):
    (X, HF, XH, XL, Y, P, C, PC, SM, SC, pp, pm, bank, col, link, Stream, pair_done, hi_ready, lo_ready, norm_pe,
     norm_act, norm_dve, lo_parts, mix_act, x_ready, mixes, three_passes, whi, wlo, raw, split_hi, split_lo,
     wait_evac) = (
        L[k] for k in ("X HF XH XL Y P C PC SM SC pp pm bank col link Stream pair_done hi_ready lo_ready norm_pe "
                       "norm_act norm_dve lo_parts mix_act x_ready mixes three_passes whi wlo raw split_hi split_lo "
                       "wait_evac").split())
    moba_pe, moba_act, moba_dve, pool_pe, gated_pe, gated_act, gated_dve = (
        L[k] for k in "moba_pe moba_act moba_dve pool_pe gated_pe gated_act gated_dve".split())
    rows_pe, rows_act, rows_dve, mlstm_pe, mlstm_act, mlstm_dve, ssd_pe, ssd_act, ssd_dve = (
        L[k] for k in "rows_pe rows_act rows_dve mlstm_pe mlstm_act mlstm_dve ssd_pe ssd_act ssd_dve".split())
    G1W = L["G1W"]

    F0 = [FFN1, FFN2]

    def up_pe(pe, b, p, slot, g):
        pe.wait_ge(lo_ready, p + 1)
        if not (isinstance(g, int) and g < 2):
            pe.wait_ge(S("up_taken" if b else "up_product"), g - 1)
        for half in range(2):
            for k in range(KT):
                at = k * 256 + half * 128
                done = three_passes(pe, pp[slot][:, half * 256:half * 256 + 256], [u[:, slot, at:at + 128] for u in (whi, wlo)],
                                    [u[:, k, :] for u in (XH, XL)], k == 0, k == KT - 1)
        done.then_inc(pair_done, 1)

    def down_pe(pe, b, p, slot, j, parity):
        pe.wait_ge(lo_ready, p + 1)
        pe.wait_ge(S("hidden_ready"), 2 * j + (FT * b + 2))
        first = isinstance(j, int) and j == 0
        last = isinstance(j, int) and j == FT // 2 - 1
        for kk in range(2):
            y = [Y[:, 4 * part + 2 * parity + kk, :] for part in range(2)]
            for m in range(KT):
                at = kk * 1024 + m * 128
                for n, (a, c) in enumerate(((whi, 0), (whi, 1), (wlo, 0))):
                    done = pe.matmul(pm[:, 512 + m * 256:768 + m * 256], a[:, slot, at:at + 128], y[c],
                                     start=first and kk == 0 and n == 0 and m % 2 == 0,
                                     stop=last and kk == 1 and n == 2, skip_group_check=True)
        done.then_inc(pair_done, 1)

    def ffn_pe(pe, b):
        f = F0[b]
        for g in range(2):
            up_pe(pe, b, f + g, (f + g) % RING, g)
        up_pe(pe, b, f + 2, (f + 2) % RING, 2)
        down_pe(pe, b, f + 3, (f + 3) % RING, 0, 0)
        up_pe(pe, b, f + 4, (f + 4) % RING, 3)
        with pe.Fori(0, 4) as i:
            p, s = i * 6 + (f + 5), f + 5
            up_pe(pe, b, p, s % RING, i * 4 + 4)
            down_pe(pe, b, p + 1, (s + 1) % RING, i * 2 + 1, 1)
            up_pe(pe, b, p + 2, (s + 2) % RING, i * 4 + 5)
            up_pe(pe, b, p + 3, (s + 3) % RING, i * 4 + 6)
            down_pe(pe, b, p + 4, (s + 4) % RING, i * 2 + 2, 0)
            up_pe(pe, b, p + 5, (s + 5) % RING, i * 4 + 7)
        up_pe(pe, b, f + 29, (f + 29) % RING, 20)
        down_pe(pe, b, f + 30, (f + 30) % RING, 9, 1)
        up_pe(pe, b, f + 31, (f + 31) % RING, 21)
        down_pe(pe, b, f + 32, (f + 32) % RING, 10, 0)

    def temps(par):
        return [P[:, 16 + 4 * par + n, :] for n in range(4)]

    def fcol(name, k):
        return PC[:, COLS[name] + k:COLS[name] + k + 1] if isinstance(k, int) else PC[:, bass.ds(k + COLS[name], 1)]

    def act_turn(act, b, p, slot, turn, prev):
        if prev is not None:
            g, ps_slot, par = prev
            n = g + (FT * b + 1)
            th, pr, cg, cu = temps(par % 2)
            gate, value = pp[ps_slot][:, 0:256], pp[ps_slot][:, 256:512]
            act.wait_ge(pair_done, p)
            if b == 0:
                act.activation(th, gate, ACT.Tanh, scale=0.5).then_inc(S("up_tanh"), 1)
            else:
                act.activation(cg, gate, ACT.Identity, bias=fcol("ffn_conv_b", g), scale=fcol("ffn_conv_w", g + 88)).then_inc(S("up_conv"), 1)
                act.activation(cu, value, ACT.Identity, bias=fcol("ffn_conv_b", g + 22), scale=fcol("ffn_conv_w", g + 110)).then_inc(S("up_conv"), 1)
        if turn is not None:
            split_hi(act, p + 2, slot, turn)
        if prev is not None:
            if b:
                act.wait_ge(S("up_taken"), g + 1)
                act.activation(th, cg, ACT.Tanh, scale=0.5).then_inc(S("up_tanh"), 1)
            act.wait_ge(S("up_product"), n)
            act.activation(Y[:, par, :], pr, ACT.Copy).then_inc(S("hidden_hi"), 1)

    def dve_turn(dve, b, p, slot, turn, prev):
        if prev is not None:
            g, ps_slot, par = prev
            n = g + (FT * b + 1)
            th, pr, cg, cu = temps(par % 2)
            gate, value = pp[ps_slot][:, 0:256], pp[ps_slot][:, 256:512]
            if b == 0:
                dve.wait_ge(S("up_tanh"), n)
                dve.scalar_tensor_tensor(pr, th, 1.0, gate, ALU.add, ALU.mult).then_inc(S("up_gated"), 1)
                dve.wait_ge(S("up_gated"), n)
                dve.scalar_tensor_tensor(pr, pr, 0.5, value, ALU.mult, ALU.mult).then_inc(S("up_product"), 1)
            else:
                dve.wait_ge(S("up_conv"), 2 * g + 2)
                for k in (1, 0):
                    lag = 2 - k
                    for c, src, off in ((cg, gate, 0), (cu, value, 22)):
                        i = dve.scalar_tensor_tensor(c[:, lag:], src[:, 0:256 - lag], fcol("ffn_conv_w", g + (44 * k + off)),
                                                     c[:, lag:], ALU.mult, ALU.add)
                        if k == 0 and off:
                            i.then_inc(S("up_taken"), 1)
                            dve.wait_ge(S("up_taken"), g + 1)
                        else:
                            i.then_inc(S("up_taps"), 1)
                            dve.wait_ge(S("up_taps"), 3 * g + (1 + (0 if k else 2) + (1 if off else 0)))
        if turn is not None:
            split_lo(dve, p + 2, slot)
        if prev is not None:
            if b:
                dve.wait_ge(S("up_tanh"), n)
                dve.scalar_tensor_tensor(pr, th, 1.0, cg, ALU.add, ALU.mult).then_inc(S("up_gated"), 1)
                dve.wait_ge(S("up_gated"), n)
                dve.scalar_tensor_tensor(pr, pr, 0.5, cu, ALU.mult, ALU.mult).then_inc(S("up_product"), 1)
            dve.wait_ge(S("hidden_hi"), n)
            dve.tensor_tensor(Y[:, 4 + par, :], pr, Y[:, par, :].bitcast(F32), ALU.subtract).then_inc(S("hidden_ready"), 1)

    def ffn_side(eng, b, turn_fn):
        f = F0[b]

        def turn(p, n, g=None):
            at = f + n + 2
            loaded = at // RING if isinstance(p, int) else None
            prev = None if g is None else (g, (f + n - 1) % RING, g % 4)
            turn_fn(eng, b, p, at % RING, loaded if at < NPAIRS else None, prev)

        turn(f, 0)
        turn(f + 1, 1, 0)
        turn(f + 2, 2, 1)
        turn(f + 3, 3, 2)
        turn(f + 4, 4)
        with eng.Fori(0, 4) as i:
            for j, g in enumerate((3, 4, None, 5, 6, None)):
                n = 5 + j
                at = f + n + 2
                prev = None if g is None else (i * 4 + g, (f + n - 1) % RING, g % 4)
                turn_fn(eng, b, i * 6 + (f + n), at % RING, i * 2 + at // RING, prev)
        turn(f + 29, 29, 19)
        turn(f + 30, 30, 20)
        turn(f + 31, 31)
        turn(f + 32, 32, 21)

    def acc(q):
        return pm[:, 512 + q * 512:1024 + q * 512].rearrange("p (a t) -> p a t", a=2)

    @block.tensor
    def _(pe):
        st = Stream(pe, "pe")
        pe.wait_ge(S("consts_loaded"), 16)
        norm_pe(pe, 0)
        pe.wait_ge(S("norm_tiles"), 8)
        for w in ("G1W", "G2W", "PLW", "IFW", "DTW"):
            pe.wait_ge(S(f"loaded_{w}"), 16)
        for k in range(KT):
            i = pe.matmul(bank(4)[0:16, 0:256], G1W[:, k * 16:k * 16 + 16], HF[:, k, :], start=k == 0, stop=k == KT - 1)
        i.then_inc(S("g1_ready"), 1)
        x_ready(pe, 0)
        st.window(0, 6)
        st.finish()
        st.window(6, 6)
        wait_evac(pe, 5)
        gated_pe(pe, 0, st)
        st.finish()
        st.window(12, 14)
        wait_evac(pe, 11)
        moba_pe(pe, st)
        pool_pe(pe, st)
        st.finish()
        st.window(26, 6)
        pe.wait_ge(S("gated_y_done"), 1)
        pe.wait_ge(S("y1_ready"), 2)
        st.finish()
        x_ready(pe, 1)
        st.window(32, 4)
        st.finish()
        norm_pe(pe, 1)
        norm_pe(pe, 2)
        x_ready(pe, 2)
        ffn_pe(pe, 0)
        norm_pe(pe, 3)
        norm_pe(pe, 4)
        st.p = BLK2
        st.window(BLK2, 12)
        x_ready(pe, 3)
        rows_pe(pe, st)
        st.finish()
        st.window(BLK2 + 12, 12)
        wait_evac(pe, BLK2 + 11)
        gated_pe(pe, 1, st)
        gated_pe(pe, 2, st)
        st.finish()
        st.window(BLK2 + 24, 16)
        wait_evac(pe, BLK2 + 23)
        mlstm_pe(pe, st)
        st.finish()
        st.window(BLK2 + 40, 20)
        wait_evac(pe, BLK2 + 39)
        pe.wait_ge(S("gated_y_done"), 3)
        pe.wait_ge(S("lm_y_done"), 2)
        ssd_pe(pe, st)
        st.finish()
        st.window(BLK2 + 60, 4)
        pe.wait_ge(S("mb_y_done"), 2)
        st.finish()
        x_ready(pe, 4)
        st.window(BLK2 + 64, 4)
        st.finish()
        norm_pe(pe, 5)
        x_ready(pe, 5)
        ffn_pe(pe, 1)
        norm_pe(pe, 6)

    @block.scalar
    def _(act):
        st = Stream(act, "act")
        act.wait_ge(S("x_loaded"), 16)
        act.wait_ge(S("cols_loaded"), 16)
        act.wait_ge(S("scalars_set"), 4)
        norm_act(act, 0, X, 0)
        st.start()
        act.wait_ge(S("g1_ready"), 1)
        act.activation(SM[0:16, 0:256], bank(4)[0:16, 0:256], ACT.Copy).then_inc(S("g1_copied"), 1)
        st.window(0, 6)
        st.finish()
        st.window(6, 6)
        wait_evac(act, 5)
        gated_act(act, 0, st)
        st.finish()
        st.window(12, 14)
        wait_evac(act, 11)
        moba_act(act, st)
        st.finish()
        st.window(26, 6)
        st.finish()
        mix_act(act, 1)
        st.window(32, 4)
        st.finish()
        wait_evac(act, 35)
        norm_act(act, 1, P[:, OUT:OUT + 8, :], None)
        act.wait_ge(S("x_updated"), 8)
        norm_act(act, 2, X, 1)
        ffn_side(act, 0, act_turn)
        act.wait_ge(pair_done, BLK2)
        for q in range(4):
            act.activation(P[:, OUT + 2 * q:OUT + 2 * q + 2, :], acc(q), ACT.Copy).then_inc(S("ffn_out"), 1)
        act.wait_ge(S("ffn_out"), 4)
        norm_act(act, 3, P[:, OUT:OUT + 8, :], None)
        act.wait_ge(S("x_updated"), 16)
        norm_act(act, 4, X, 2)
        st.p = BLK2
        st.window(BLK2, 12)
        rows_act(act, st)
        st.finish()
        st.window(BLK2 + 12, 12)
        wait_evac(act, BLK2 + 11)
        gated_act(act, 1, st)
        gated_act(act, 2, st)
        st.finish()
        st.window(BLK2 + 24, 16)
        wait_evac(act, BLK2 + 23)
        mlstm_act(act, st)
        st.finish()
        st.window(BLK2 + 40, 20)
        wait_evac(act, BLK2 + 39)
        ssd_act(act, st)
        st.finish()
        st.window(BLK2 + 60, 4)
        st.finish()
        mix_act(act, 2)
        st.window(BLK2 + 64, 4)
        st.finish()
        wait_evac(act, BLK2 + 67)
        norm_act(act, 5, X, 3)
        ffn_side(act, 1, act_turn)
        act.wait_ge(S("x_final"), 4)
        norm_act(act, 6, X, None)

    @block.vector
    def _(dve):
        st = Stream(dve, "dve")
        for n, v in ((127, EPS), (126, 4 * EPS), (125, 1.0), (124, 16 * EPS)):
            dve.memset(SC[:, n:n + 1], v).then_inc(S("scalars_set"), 1)
        dve.wait_ge(S("consts_loaded"), 16)
        dve.wait_ge(S("cols_loaded"), 16)
        dve.wait_ge(S("x_loaded"), 16)
        norm_dve(dve, 0, X, "norm_mix_pre", 0)
        st.start()
        st.window(0, 6)
        st.finish()
        st.window(6, 6)
        wait_evac(dve, 5)
        gated_dve(dve, 0, st)
        st.finish()
        st.window(12, 14)
        wait_evac(dve, 11)
        moba_dve(dve, st)
        st.finish()
        st.window(26, 6)
        wait_evac(dve, 25)
        st.finish()
        lo_parts(dve, 4 * mixes[1], 0.5)
        st.window(32, 4)
        st.finish()
        norm_dve(dve, 1, P[:, OUT:OUT + 8, :], "norm_mix_post", None)
        norm_dve(dve, 2, X, "norm_ffn_pre", 1)
        ffn_side(dve, 0, dve_turn)
        norm_dve(dve, 3, P[:, OUT:OUT + 8, :], "norm_ffn_post", None)
        norm_dve(dve, 4, X, "norm1_g", 2)
        st.p = BLK2
        st.window(BLK2, 12)
        dve.wait_ge(S("loaded_RW"), 16)
        rows_dve(dve, st)
        st.finish()
        st.window(BLK2 + 12, 12)
        wait_evac(dve, BLK2 + 11)
        gated_dve(dve, 1, st)
        gated_dve(dve, 2, st)
        st.finish()
        st.window(BLK2 + 24, 16)
        wait_evac(dve, BLK2 + 23)
        mlstm_dve(dve, st)
        st.finish()
        st.window(BLK2 + 40, 20)
        wait_evac(dve, BLK2 + 39)
        ssd_dve(dve, st)
        st.finish()
        st.window(BLK2 + 60, 4)
        st.finish()
        lo_parts(dve, 4 * mixes[2], 0.5)
        st.window(BLK2 + 64, 4)
        st.finish()
        norm_dve(dve, 5, X, "norm2_g", 3)
        ffn_side(dve, 1, dve_turn)
        dve.wait_ge(pair_done, NPAIRS)
        for q in range(4):
            dve.tensor_tensor(X[:, 2 * q:2 * q + 2, :], X[:, 2 * q:2 * q + 2, :], acc(q), ALU.add).then_inc(S("x_final"), 1)
        norm_dve(dve, 6, X, "final_g", None, P[:, 8:16, :], "result_ready")


def pair_columns(w, cols):
    return w[:, cols].reshape(KT, 128, 256).transpose(1, 0, 2).reshape(128, PW)


def weight_stream(i):
    s = np.empty((NPAIRS, 128, PW), np.float32)
    n = 0

    def put(a):
        nonlocal n
        s[n] = a
        n += 1

    def span(w, start, width):
        for c in range(start, start + width, 256):
            put(pair_columns(w, slice(c, c + 256)))

    w = i["w_in"][0]
    q, k, v, g1, r, u, mq, mk, mv, gates = np.cumsum([0, 256, 256, 512, 16, 512, 512, 512, 512, 512]).tolist()
    for start, width in ((q, 256), (k, 256), (r, 512), (v, 512), (mq, 512), (mk, 512), (mv, 512), (u, 512), (gates, 3072)):
        span(w, start, width)
    branches = [i[f"w_branch_{x}"][0] for x in "abc"]
    for j in range(6):
        groups = [divmod(4 * j + g, 3) for g in range(4)]
        put(np.concatenate([branches[br][:, m * 128:m * 128 + 128].reshape(4, 128, 128).transpose(1, 0, 2).reshape(128, 512)
                            for m, br in groups], 1))
    span(i["w_out"][0], 0, 1024)

    def ffn(gate, up, down):
        def one(g):
            put(np.concatenate([gate[:, g * 128:g * 128 + 128].reshape(KT, 128, 128),
                                up[:, g * 128:g * 128 + 128].reshape(KT, 128, 128)], 2).transpose(1, 0, 2).reshape(128, PW))

        def two(j):
            put(down[j * 256:j * 256 + 256].reshape(2, 128, 1024).transpose(1, 0, 2).reshape(128, PW))

        one(0)
        one(1)
        for j in range(1, 11):
            one(2 * j)
            two(j - 1)
            one(2 * j + 1)
        two(10)

    ffn(i["ffn_w_gate"][0], i["ffn_w_up"][0], i["ffn_w_down"][0])
    w = i["w_in_2"][0]
    hq, hf, hi, hg, lqk, lv, lif, lo, z, xbc, dt, gates = np.cumsum(
        [0, 1024, 1024, 1024, 1024, 1024, 1024, 8, 1024, 1024, 2048, 16]).tolist()
    for start, width in ((hq, 1024), (hf, 1024), (hi, 1024), (hg, 1024), (lqk, 1024), (lv, 1024), (lo, 1024), (xbc, 2048), (z, 1024)):
        span(w, start, width)
    for b, name in enumerate(("w_br_hg_2", "w_br_ml_2", "w_br_mb_2")):
        span(w, gates + 1024 * b, 1024)
        span(i[name][0], 0, 1024)
    span(i["w_out_2"][0], 0, 1024)
    up = i["w_up_2"][0]
    ffn(up[:, :FF], up[:, FF:], i["w_down_2"][0])
    assert n == NPAIRS, n
    return s


def channel_columns(i):
    def cols(v):
        return np.asarray(v).reshape(-1, 128).T

    parts = [cols(i[k][0]) for k in ("norm_mix_pre", "norm_mix_post", "norm_ffn_pre", "norm_ffn_post", "gla_b_g", "gla_norm",
                                     "pool_scale", "norm1_g_2", "hg_norm_g_2", "ml_norm_g_2")]
    parts += [cols(np.repeat(i["mb_d_2"][0], 64)), cols(i["mb_norm_g_2"][0]), cols(i["norm2_g_2"][0]), cols(i["final_g_2"])]
    parts += [cols(np.concatenate([i["ml_conv_b_2"][0], i["mb_conv_b_2"][0]]))]
    parts += [cols(np.concatenate([i["ml_conv_w_2"][0][k], i["mb_conv_w_2"][0][k]])) for k in range(4)]
    parts += [cols(i["ffn_conv_b_2"][0])] + [cols(i["ffn_conv_w_2"][0][k]) for k in range(3)]
    return np.ascontiguousarray(np.concatenate(parts, 1))


def kernel(**inputs):
    import concourse.bacc as bacc
    from concourse.bass_utils import run_bass_kernel_spmd

    i = {k: np.asarray(v) for k, v in inputs.items()}

    def small(w):
        return np.ascontiguousarray(w.reshape(KT, 128, -1).transpose(1, 0, 2).reshape(128, -1))

    head_rows = np.zeros((36, 8), np.float32)
    head_rows[32:36, 0], head_rows[32:36, 1] = i["ml_gate_b_2"][0][:4], i["ml_gate_b_2"][0][4:]
    head_rows[0:16, 2], head_rows[0:16, 3] = i["mb_dt_bias_2"][0], i["mb_a_log_2"][0]
    w1, w2 = i["w_in"][0], i["w_in_2"][0]
    arrays = {
        "stream": weight_stream(i),
        "xT": small(i["x"][0].T).reshape(128, KT, T),
        "cols": channel_columns(i),
        "consts": constants(),
        "g1w": small(w1[:, 1024:1040]),
        "g2w": np.ascontiguousarray(i["gla_w_g2"][0]),
        "poolw": np.ascontiguousarray(i["pool_w"][0].transpose(1, 0, 2).reshape(128, 512)),
        "ifw": small(w2[:, 6144:6152]),
        "dtw": small(w2[:, 10248:10264]),
        "rows": head_rows,
    }
    nc = bacc.Bacc("TRN2", target_bir_lowering=False, num_devices=1)
    aps = [nc.dram_tensor(k, a.shape, F32, kind="ExternalInput").ap() for k, a in arrays.items()]
    out = nc.dram_tensor("out", (128, KT, T), F32, kind="ExternalOutput").ap()
    build(nc, *aps, out)
    r = run_bass_kernel_spmd(nc, [arrays], core_ids=[0]).results[0]["out"]
    return np.ascontiguousarray(r.reshape(128, KT, T).transpose(2, 1, 0).reshape(1, T, D))
```

```python
import concourse.bass as bass
from concourse import mybir
from contextlib import ExitStack
import numpy as np

F32 = mybir.dt.float32
F32R = mybir.dt.float32r
I32 = mybir.dt.int32
ACT = mybir.ActivationFunctionType
ALU = mybir.AluOpType
AX = mybir.AxisListType

T = 256
D = 1024
KT = D // 128
FF = 2816
FT = FF // 128
PW = 2048
EPS = 1e-6
NEG = -1e30
RING = 3
LEVELS = [128, 64, 32, 16, 8, 4, 2, 1]

GQ, GK, GR, GV = 0, 2, 4, 8
MQ, MK, MV = 12, 16, 20
PU, GATE1 = 24, 28
HQ, HFG, HI, HG, HK = 0, 8, 16, 24, 48
LQ, LK, LV, LO = 32, 36, 40, 24
XS, XB, XC, XZ = 0, 8, 12, 16
GATE2 = [32, 40, 32]
SQ = 40
RMS_T, RCP_T = 38, 39
MASKS = 52
OUT = 0
POOL_TILES = 53

PAIRS1 = (
    [("B", "copy", GQ, 0.125)] + [("B", "copy", GK, 1.0)]
    + [("B", "copy", GR + 2 * j, 1.0) for j in range(2)]
    + [("A", "copyA", GV + j, 2) for j in range(2)]
    + [("B", "copy", MQ + 2 * j, 0.125) for j in range(2)]
    + [("B", "copy", MK + 2 * j, 1.0) for j in range(2)]
    + [("A", "copyA", MV + j, 2) for j in range(2)]
    + [("B", "copy", PU + 2 * j, 1.0) for j in range(2)]
    + [("B", "tanh", GATE1 + 2 * j, 0.5) for j in range(12)]
    + [("BR1", "mix1", j, 0) for j in range(6)]
    + [("B", "copy", OUT + 2 * j, 1.0) for j in range(4)]
)
PAIRS2 = (
    [("B", "copy", HQ + 2 * j, 1.0) for j in range(4)]
    + [("B", "copy", HFG + 2 * j, 1.0) for j in range(4)]
    + [("A", "copyA", HI + j, 4) for j in range(4)]
    + [("B", "copy", HG + 2 * j, 1.0) for j in range(4)]
    + [("B", "conv", LQ + 2 * j, 2 * j) for j in range(4)]
    + [("A", "copyA", LV + j, 4) for j in range(4)]
    + [("B", "tanh", LO + 2 * j, 0.5) for j in range(4)]
    + [("B", "conv", XS + 2 * j, 8 + 2 * j) for j in range(8)]
    + [("B", "copy", XZ + 2 * j, 1.0) for j in range(4)]
    + [("B", "tanh", GATE2[0] + 2 * j, 0.5) for j in range(4)]
    + [("Y0", "mix2", j, 0) for j in range(4)]
    + [("B", "tanh", GATE2[1] + 2 * j, 0.5) for j in range(4)]
    + [("Y1", "mix2", j, 1) for j in range(4)]
    + [("B", "tanh", GATE2[2] + 2 * j, 0.5) for j in range(4)]
    + [("Y0", "mix2", j, 2) for j in range(4)]
    + [("B", "resid", 2 * j, 0) for j in range(4)]
)
N1, N2, NF = len(PAIRS1), len(PAIRS2), FT + FT // 2
FFN1 = N1
BLK2 = N1 + NF
FFN2 = BLK2 + N2
NPAIRS = FFN2 + NF
PAIR = dict(enumerate(PAIRS1)) | {BLK2 + n: s for n, s in enumerate(PAIRS2)}


def taken(p):
    who = "act_taken" if PAIR[p][1] in ("copy", "tanh", "copyA") else "dve_taken"
    act = ("copy", "tanh", "copyA")
    return who, sum((PAIR[x][1] in act) == (who == "act_taken") for x in PAIR if x <= p)


COLS = {}
_n = 0
for _name, _k in (("norm_mix_pre", KT), ("norm_mix_post", KT), ("norm_ffn_pre", KT), ("norm_ffn_post", KT),
                  ("gla_b_g", 2), ("gla_norm", 1), ("pool_scale", 4), ("norm1_g", KT), ("hg_norm", 1),
                  ("ml_norm", 2), ("mb_d", KT), ("mb_norm", KT), ("norm2_g", KT), ("final_g", KT),
                  ("conv_b", 24), ("conv_w", 96), ("ffn_conv_b", 44), ("ffn_conv_w", 132)):
    COLS[_name] = _n
    _n += _k
NCOLS = _n

CIDENT, CONES, CLEVEL = 0, 128, 384
CALIBI = CLEVEL + 8 * 128
CALCOL, CHEAD, CINV = CALIBI + 256, CALIBI + 272, CALIBI + 303
NCONST = CINV + 64


def constants():
    c = np.zeros((128, NCONST), np.float32)
    s, t = np.arange(128)[:, None], np.arange(128)[None, :]
    c[:, CIDENT:CIDENT + 128] = np.eye(128)
    c[:, CONES:CONES + 256] = 1.0
    for n, half in enumerate(LEVELS[1:]):
        same = (s // (2 * half)) == (t // (2 * half))
        c[:, CLEVEL + n * 128:CLEVEL + (n + 1) * 128] = same & (s % (2 * half) < half) & (t % (2 * half) >= half)
    c[:, CLEVEL + 7 * 128:CLEVEL + 8 * 128] = s == t
    slope = 2.0 ** -(np.arange(8) + 1.0)
    c[:8, CALIBI:CALIBI + 256] = slope[:, None] * np.arange(256)[None, :]
    for v in range(2):
        c[:, CALCOL + v * 8:CALCOL + v * 8 + 8] = slope[None, :] * (np.arange(128)[:, None] + 128 * v)
    c[:, CHEAD + 15] = 1.0
    for g, w in enumerate((2, 4, 8, 16)):
        c[:, CINV + 16 * g:CINV + 16 * g + 16] = 1.0 / np.minimum(np.arange(16) + 1, w)
    return c


def causal_masks():
    s, t = np.arange(128)[:, None], np.arange(128)[None, :]
    return np.concatenate([np.where(s <= t, 0.0, NEG), np.where(t <= s, 0.0, NEG)], 1).astype(np.float32)


def build(nc, stream, xT, cols, consts, masks, g1w, g2w, poolw, ifw, dtw, rows, out):
    ctx = ExitStack()
    with ctx:
        def sb(name, shape, dt=F32):
            return ctx.enter_context(nc.sbuf_tensor(name, shape, dt))

        sems = {}

        def S(name):
            if name not in sems:
                sems[name] = ctx.enter_context(nc.semaphore(name))
            return sems[name]

        raw = sb("raw", [128, RING, PW])
        whi = sb("whi", [128, RING, PW], F32R)
        wlo = sb("wlo", [128, RING, PW], F32R)
        X = sb("X", [128, KT, T])
        HF = sb("HF", [128, KT, T])
        XH = sb("XH", [128, KT, T], F32R)
        XL = sb("XL", [128, KT, T], F32R)
        y_at = nc.sbuf_base
        Y = sb("Y", [128, 32, T], F32R)
        U = nc.alloc_sbuf_tensor_at("U", [128, 16, T], F32, offset=y_at + 16 * T * 4)
        P = sb("P", [128, POOL_TILES, T])
        C = sb("C", [128, NCONST])
        CR = sb("CR", [128, 384], F32R)
        PC = sb("PC", [128, NCOLS])
        G1W = sb("G1W", [128, KT * 16])
        IFW = sb("IFW", [128, KT * 8])
        DTW = sb("DTW", [128, KT * 16])
        RW = sb("RW", [36, 8])
        SC = sb("SC", [128, 128])
        R = sb("R", [36, 7 * T])
        SM = R[0:16, 0:3 * T]
        LR = R[32:36, 0:6 * T].rearrange("p (a t) -> p a t", a=6)
        DR = R[0:16, 3 * T:7 * T].rearrange("p (a t) -> p a t", a=4)
        RMS, RCP = P[:, RMS_T, :], P[:, RCP_T, :]
        G2W, PLW = U[0:16, 4:5, :].rearrange("p a t -> p (a t)"), U[:, 6:8, :].rearrange("p a t -> p (a t)")
        pp = [ctx.enter_context(nc.psum_tensor(f"pp{i}", [128, 512], F32)) for i in range(RING)]
        pm = ctx.enter_context(nc.psum_tensor("pm", [128, 5 * 512], F32))

        arrived = [S(f"weights_arrived{i}") for i in range(RING)]
        hi_ready, lo_ready, pair_done = (S(n) for n in ("hi_ready", "lo_ready", "pair_done"))
        conv_started = S("conv_started")
        ident = C[:, CIDENT:CIDENT + 128]
        ones = C[:, CONES:CONES + 128]

        def col(name, i=0):
            return PC[:, COLS[name] + i:COLS[name] + i + 1]

        block = ctx.enter_context(nc.Block())
        self = dict(locals())

        @block.sync
        def _(sp):
            def load(p, slot):
                src = stream[p] if isinstance(p, int) else stream[bass.ds(p, 1), :, :].rearrange("a p n -> p (a n)")
                sp.dma_start(raw[:, slot, :], src).then_inc(arrived[slot], 16)

            sp.dma_start(X[:, :, :], xT).then_inc(S("x_loaded"), 16)
            sp.dma_start(C[:, 0:CLEVEL], consts[:, 0:CLEVEL]).then_inc(S("consts_loaded"), 16)
            sp.dma_start(PC[:, :], cols).then_inc(S("cols_loaded"), 16)
            for p in range(RING):
                load(p, p)
            sp.dma_start(C[:, CLEVEL:], consts[:, CLEVEL:]).then_inc(S("tables_loaded"), 16)
            sp.dma_start(P[:, MASKS, :], masks).then_inc(S("masks_loaded"), 16)
            for name, dst, src in (("G1W", G1W, g1w), ("G2W", G2W, g2w), ("PLW", PLW, poolw), ("IFW", IFW, ifw),
                                   ("DTW", DTW, dtw), ("RW", RW, rows)):
                sp.dma_start(dst[:, :], src).then_inc(S(f"loaded_{name}"), 16)
            whole = (NPAIRS - RING) // RING
            with sp.Fori(1, 1 + whole) as i:
                for slot in range(RING):
                    sp.wait_ge(lo_ready, i * RING + (slot + 1 - RING))
                    load(i * RING + slot, slot)
            for p in range(RING * (1 + whole), NPAIRS):
                sp.wait_ge(lo_ready, p - RING + 1)
                load(p, p % RING)
            sp.wait_ge(S("result_ready"), 8)
            sp.dma_start(out, P[:, 8:16, :]).then_inc(S("result_stored"), 16)
            sp.wait_ge(S("result_stored"), 16)

        parts = {}
        for engine in ("tensor", "scalar", "vector", "gpsimd"):
            parts[engine] = engine
        program(nc, block, S, self)


def program(nc, block, S, L):
    raw, whi, wlo, X, HF, XH, XL, Y, P, C, PC = (L[k] for k in "raw whi wlo X HF XH XL Y P C PC".split())
    G1W, IFW, DTW, G2W, PLW, RW, RMS, RCP, SM, SC = (L[k] for k in "G1W IFW DTW G2W PLW RW RMS RCP SM SC".split())
    pp, pm, arrived, hi_ready, lo_ready, pair_done, conv_started = (
        L[k] for k in "pp pm arrived hi_ready lo_ready pair_done conv_started".split())
    ident, ones, col = L["ident"], L["ones"], L["col"]

    def bank(n):
        return pm[:, n * 512:(n + 1) * 512]

    def split_hi(act, p, slot, turn):
        act.wait_ge(arrived[slot], turn * 16 + 16)
        if not isinstance(p, int) or p >= RING:
            act.wait_ge(pair_done, p - (RING - 1))
        act.activation(whi[:, slot, :], raw[:, slot, :], ACT.Copy).then_inc(hi_ready, 1)

    def split_lo(dve, p, slot):
        dve.wait_ge(hi_ready, p + 1)
        if not isinstance(p, int) or p >= RING:
            dve.wait_ge(pair_done, p - (RING - 1))
        dve.tensor_tensor(wlo[:, slot, :], raw[:, slot, :], whi[:, slot, :].bitcast(F32), ALU.subtract).then_inc(lo_ready, 1)

    def three_passes(pe, dst, lhs, rhs, first, last, **kw):
        for n, (a, b) in enumerate(((lhs[0], rhs[0]), (lhs[0], rhs[1]), (lhs[1], rhs[0]))):
            done = pe.matmul(dst, a, b, start=first and n == 0, stop=last and n == 2, **kw)
        return done

    def x_tiles_ready(pe, rewrite, k):
        if rewrite is not None and k % 2 == 0:
            pe.wait_ge(S("x_lo"), 4 * rewrite + k // 2 + 1)

    def pair_matmuls(pe, p, slot, form, rewrite=None):
        pe.wait_ge(lo_ready, p + 1)
        w = [t[:, slot, :] for t in (whi, wlo)]
        if form == "BR1":
            q = p - (FFN1 - 10)
            for g in range(4):
                br = (4 * q + g) % 3
                dst = (pp[slot][:, g * 256:g * 256 + 256] if g < 2
                       else bank(slot)[:, (g - 2) * 256:(g - 2) * 256 + 256])
                for k in range(4):
                    y = [Y[:, 8 * part + br * 4 + k if br < 2 else 16 + 8 * part + k, :] for part in range(2)]
                    at = (g * 4 + k) * 128
                    done = three_passes(pe, dst, [u[:, at:at + 128] for u in w], y, k == 0, k == 3)
            done.then_inc(pair_done, 1)
            return
        x = [XH, XL]
        base = 0
        if form in ("Y0", "Y1"):
            x, base = None, 16 * (form == "Y1")
        for half in range(2):
            for k in range(KT):
                dst = pp[slot][:, half * 256:half * 256 + 256]
                if half == 0:
                    x_tiles_ready(pe, rewrite, k)
                if form == "A":
                    lhs = [u[:, k, half * 128:half * 128 + 128] for u in x]
                    rhs = [u[:, k * 256:k * 256 + 256] for u in w]
                else:
                    at = k * 256 + half * 128
                    lhs = [u[:, at:at + 128] for u in w]
                    rhs = ([u[:, k, :] for u in x] if x else [Y[:, base + 8 * part + k, :] for part in range(2)])
                done = three_passes(pe, dst, lhs, rhs, k == 0, k == KT - 1)
        done.then_inc(pair_done, 1)

    def evac_act(act, p, spec):
        form, kind, at, arg = spec
        ps = pp[p % RING]
        if kind in ("copy", "tanh", "copyA", "conv"):
            act.wait_ge(pair_done, p + 1)
        if kind == "copy":
            act.activation(P[:, at:at + 2, :], ps[:, :].rearrange("p (a t) -> p a t", a=2), ACT.Copy,
                           scale=arg).then_inc(S("act_taken"), 1)
        elif kind == "tanh":
            act.activation(P[:, at:at + 2, :], ps[:, :].rearrange("p (a t) -> p a t", a=2), ACT.Tanh,
                           scale=arg).then_inc(S("act_taken"), 1)
        elif kind == "copyA":
            act.activation(P[:, at:at + arg + 1:arg, :], ps[:, :].rearrange("p (a t) -> p a t", a=2),
                           ACT.Copy).then_inc(S("act_taken"), 1)
        elif kind == "conv":
            for h in range(2):
                act.activation(P[:, at + h, :], ps[:, h * 256:h * 256 + 256], ACT.Identity,
                               bias=col("conv_b", arg + h), scale=col("conv_w", 72 + arg + h)).then_inc(conv_started, 1)

    dve_count = {"conv": 0, "mix": 0}

    def evac_dve(dve, p, spec):
        form, kind, at, arg = spec
        ps = pp[p % RING]
        own = (S("dve_taken"), taken(p)[1])
        if kind == "conv":
            dve_count["conv"] += 2
            dve.wait_ge(conv_started, dve_count["conv"])
            before = [None, None]
            for k in (2, 1, 0):
                lag = 3 - k
                for h in range(2):
                    if before[h]:
                        settled(dve, before[h])
                    i = dve.scalar_tensor_tensor(P[:, at + h, lag:], ps[:, h * 256:h * 256 + 256 - lag],
                                                 col("conv_w", 24 * k + arg + h), P[:, at + h, lag:],
                                                 ALU.mult, ALU.add)
                    if (k, h) == (0, 1):
                        i.then_inc(S("dve_taken"), 1)
                    else:
                        before[h] = mark(dve, i)
            settled(dve, before[0])
            dve.wait_ge(*own)
        elif kind == "mix2":
            dve.wait_ge(pair_done, p + 1)
            g = GATE2[arg] + 2 * at
            flat = ps[:, :].rearrange("p (a t) -> p a t", a=2)
            dst = HF[:, 2 * at:2 * at + 2, :] if arg == 0 else P[:, g:g + 2, :]
            dve.scalar_tensor_tensor(dst, P[:, g:g + 2, :], 1.0, flat, ALU.add, ALU.mult).then_inc(S("dve_taken"), 1)
            if arg:
                dve.wait_ge(*own)
                i = dve.tensor_tensor(HF[:, 2 * at:2 * at + 2, :], HF[:, 2 * at:2 * at + 2, :], P[:, g:g + 2, :], ALU.add)
                if arg == 2:
                    i.then_inc(S("mixed_ready2"), 1)
                else:
                    link(dve, i)
        elif kind == "mix1":
            dve.wait_ge(pair_done, p + 1)
            groups = [divmod(4 * at + g, 3) for g in range(4)]
            for g, (m, br) in enumerate(groups):
                src = (ps[:, g * 256:g * 256 + 256] if g < 2
                       else bank(p % RING)[:, (g - 2) * 256:(g - 2) * 256 + 256])
                gt = GATE1 + 8 * br + m
                i = dve.scalar_tensor_tensor(P[:, gt, :] if br else HF[:, m, :], P[:, gt, :], 1.0, src, ALU.add, ALU.mult)
                if g == 3:
                    i.then_inc(S("dve_taken"), 1)
                else:
                    last = mark(dve, i)
            settled(dve, last)
            for g, (m, br) in enumerate(groups):
                if g == 3:
                    dve.wait_ge(*own)
                if br:
                    i = dve.tensor_tensor(HF[:, m, :], HF[:, m, :], P[:, GATE1 + 8 * br + m, :], ALU.add)
                    if br == 2:
                        i.then_inc(S("mixed_ready1"), 1)
                    else:
                        link(dve, i)
        elif kind == "resid":
            dve.wait_ge(pair_done, p + 1)
            dve.tensor_tensor(X[:, at:at + 2, :], X[:, at:at + 2, :],
                              ps[:, :].rearrange("p (a t) -> p a t", a=2), ALU.add).then_inc(S("dve_taken"), 1)

    def wait_evac(eng, p):
        found = {}
        for x in PAIR:
            if x <= p:
                who, n = taken(x)
                found[who] = n
        for who, n in found.items():
            eng.wait_ge(S(who), n)

    chains = {}

    def mark(eng, ins):
        name = "chain_" + chains["names"][id(eng)]
        chains[name] = chains.get(name, 0) + 1
        ins.then_inc(S(name), 1)
        return chains[name]

    def settled(eng, n):
        eng.wait_ge(S("chain_" + chains["names"][id(eng)]), n)

    def link(eng, ins):
        settled(eng, mark(eng, ins))

    class Stream:

        def __init__(self, eng, who):
            self.eng, self.who, self.p = eng, who, 0
            chains.setdefault("names", {})[id(eng)] = who

        def start(self):
            for p in range(2):
                if self.who == "act":
                    split_hi(self.eng, p, p, 0)
                elif self.who == "dve":
                    split_lo(self.eng, p, p)

        def ahead(self, p):
            if p + 2 < NPAIRS:
                if self.who == "act":
                    split_hi(self.eng, p + 2, (p + 2) % RING, (p + 2) // RING)
                elif self.who == "dve":
                    split_lo(self.eng, p + 2, (p + 2) % RING)

        def evac(self, p):
            if p in PAIR:
                if self.who == "act":
                    evac_act(self.eng, p, PAIR[p])
                elif self.who == "dve":
                    evac_dve(self.eng, p, PAIR[p])

        def go(self, n=1):
            for _ in range(n):
                p = self.p
                if p >= self.stop:
                    return
                if self.who == "pe":
                    if p - RING in PAIR:
                        who, n = taken(p - RING)
                        self.eng.wait_ge(S(who), n)
                    pair_matmuls(self.eng, p, p % RING, PAIR[p][0], self.rewrite)
                    self.rewrite = None
                else:
                    self.ahead(p)
                    if p > self.first:
                        self.evac(p - 1)
                self.p += 1

        def window(self, first, n, rewrite=None):
            assert self.p == first, (self.p, first)
            self.first, self.stop, self.rewrite = first, first + n, rewrite

        def finish(self):
            self.go(self.stop - self.p)
            if self.who != "pe":
                self.evac(self.stop - 1)

    def norm_pe(pe, n):
        for k in range(KT):
            if k % 2 == 0:
                pe.wait_ge(S("norm_squares"), 4 * n + k // 2 + 1)
            i = pe.matmul(bank(0)[:, 0:256], ones, P[:, SQ + k, :], start=k == 0, stop=k == KT - 1)
        i.then_inc(S("norm_sums"), 1)

    def load_sqrt(act):
        link(act, act.activation(SC[:, 123:124], SC[:, 125:126], ACT.Sqrt))

    def norm_act(act, n, src, split, updated=None, between=None):
        for k in range(0, KT, 2):
            if updated is not None:
                act.wait_ge(S("x_updated"), updated + k + 2)
            act.activation(P[:, SQ + k:SQ + k + 2, :], src[:, k:k + 2, :], ACT.Square).then_inc(S("norm_squares"), 1)
        if between:
            between()
        load_sqrt(act)
        act.wait_ge(S("norm_sums"), n + 1)
        act.activation(RMS[:, :], bank(0)[:, 0:256], ACT.Sqrt, bias=SC[:, 127:128], scale=1.0 / D).then_inc(S("norm_rms"), 1)
        if split is not None:
            for k in range(0, KT, 2):
                act.wait_ge(S("norm_tiles"), 8 * split + k + 2)
                act.activation(XH[:, k:k + 2, :], HF[:, k:k + 2, :], ACT.Copy).then_inc(S("x_hi"), 1)

    def norm_dve(dve, n, src, gain, split, dst=None, done=None):
        dve.wait_ge(S("norm_rms"), n + 1)
        link(dve, dve.reciprocal(RCP[:, :], RMS[:, :]))
        if split is not None:
            for k in range(KT + 2):
                if k < KT:
                    dve.scalar_tensor_tensor(HF[:, k, :], src[:, k, :], col(gain, k), RCP[:, :], ALU.mult, ALU.mult)\
                       .then_inc(S("norm_tiles"), 1)
                if k % 2 and k > 2:
                    lo_part(dve, 4 * splits[split], k - 3)
        elif done:
            for k in range(KT):
                dve.scalar_tensor_tensor(dst[:, k, :], src[:, k, :], col(gain, k), RCP[:, :], ALU.mult, ALU.mult)\
                   .then_inc(S(done), 1)
        else:
            before = 8 * (n == 3)
            for k in range(KT + 1):
                if k < KT:
                    dve.scalar_tensor_tensor(src[:, k, :], src[:, k, :], col(gain, k), RCP[:, :], ALU.mult, ALU.mult)\
                       .then_inc(S("post_scaled"), 1)
                if k:
                    dve.wait_ge(S("post_scaled"), before + k)
                    dve.tensor_tensor(X[:, k - 1, :], X[:, k - 1, :], src[:, k - 1, :], ALU.add).then_inc(S("x_updated"), 1)

    splits = {0: 0, 1: 2, 2: 3, 3: 5}
    mixes = {1: 1, 2: 4}

    def lo_part(dve, base, k, scale=1.0):
        dve.wait_ge(S("x_hi"), base + k // 2 + 1)
        dve.scalar_tensor_tensor(XL[:, k:k + 2, :], HF[:, k:k + 2, :], scale, XH[:, k:k + 2, :].bitcast(F32),
                                 ALU.mult, ALU.subtract).then_inc(S("x_lo"), 1)

    def lo_parts(dve, base, scale=1.0):
        for k in range(0, KT, 2):
            lo_part(dve, base, k, scale)

    def mix_act(act, b):
        for k in range(0, KT, 2):
            act.wait_ge(S(f"mixed_ready{b}"), k + 2 if b == 1 else k // 2 + 1)
            act.activation(XH[:, k:k + 2, :], HF[:, k:k + 2, :], ACT.Copy, scale=0.5).then_inc(S("x_hi"), 1)

    def x_ready(pe, rewrite):
        pe.wait_ge(S("x_lo"), 4 * rewrite + 4)

    L.update({k: v for k, v in locals().items() if k != "L"})
    mixers(nc, block, S, L)


def mixers(nc, block, S, L):
    (X, HF, XH, XL, Y, P, C, PC, G1W, IFW, DTW, G2W, PLW, RW, RMS, RCP, SM, SC, U, CR, LR, DR, pp, pm, bank, ident, ones,
     col, link, load_sqrt, Stream, pair_done, conv_started, hi_ready, lo_ready, norm_pe, norm_act, norm_dve, lo_parts,
     mix_act, x_ready, mixes, three_passes, whi, wlo, raw, arrived, split_hi, split_lo) = (
        L[k] for k in ("X HF XH XL Y P C PC G1W IFW DTW G2W PLW RW RMS RCP SM SC U CR LR DR pp pm bank ident ones "
                       "col link load_sqrt Stream pair_done conv_started hi_ready lo_ready norm_pe norm_act norm_dve lo_parts "
                       "mix_act x_ready mixes three_passes whi wlo raw arrived split_hi split_lo").split())
    eps1, eps4, one, eps16 = (SC[:, 127:128], SC[:, 126:127], SC[:, 125:126], SC[:, 124:125])

    def words(tile, start, n):
        return P[:, :, :].rearrange("p a t -> p (a t)")[:, tile * T + start:tile * T + start + n]

    def head_of(m, h):
        return C[:, CHEAD + 15 - h:CHEAD + 15 - h + m]

    def row_sel(rows, h, n=128, at=0):
        return C[at:at + rows, CIDENT + at + h:CIDENT + at + h + 1].to_broadcast([rows, n])

    def gated(r):
        if r == 0:
            return dict(nt=2, hp=2, dk=64, q=P[:, GQ:GQ + 2, :], k=P[:, GK:GK + 2, :], b=HF[:, 0:2, :], d=HF[:, 2:4, :],
                        z=(HF[:, 4:6, :], HF[:, 6:8, :]), A=34, o=GQ, r=GR, v=lambda v, h: words(GV + 2 * v, h * 128, 128),
                        scale=1.0 / 16, y=0, gain="gla_norm")
        h0 = 4 * (r - 1)
        return dict(nt=4, hp=1, dk=128, q=P[:, HQ + h0:HQ + h0 + 4, :], k=P[:, HK:HK + 4, :] if r == 1 else U[:, 6:10, :], b=P[:, HFG + h0:HFG + h0 + 4, :],
                    d=HF[:, 0:4, :], z=(HF[:, 4:8, :], U[:, 10:14, :]), A=None, o=HQ + h0, r=HG + h0,
                    v=lambda v, h: words(HI + 4 * v, (h0 + h) * 128, 128), scale=1.0, y=h0, gain="hg_norm")

    def blocks(ap, half):
        return ap.rearrange("p a t -> p (a t)").rearrange("p (n w) -> p n w", w=2 * half)

    def a_words(g, h):
        at = score_slot(g, h) * 384
        return gated_a(g)[:, at:at + 384]

    def score_slot(g, h):
        tile, j = divmod(h, g["hp"])
        return j * 2 + tile if g["hp"] == 2 else h

    def gated_a(g):
        return words(g["A"], 0, 1536) if g["A"] is not None else U[:, 0:6, :].rearrange("p a t -> p (a t)")

    def level_mask(n, dt):
        m = C[:, CLEVEL + n * 128:CLEVEL + (n + 1) * 128]
        return (m.bitcast(dt) if dt != F32 else m).unsqueeze(1).unsqueeze(1).to_broadcast([128, 4, 2, 128])

    def gated_pe(pe, r, st):
        g = gated(r)
        if r == 0:
            pe.wait_ge(S("g1_copied"), 1)
            for t in range(2):
                i = pe.matmul(bank(3)[:, t * 256:t * 256 + 256], G2W[:, t * 128:t * 128 + 128], SM[0:16, 0:256], start=True, stop=True)
            i.then_inc(S("logit_ready"), 1)
        for n in range(9):
            if n == 0:
                pe.wait_ge(S("gated_inputs_ready"), r + 1)
            else:
                pe.wait_ge(S("gated_z_ready"), 2 * (8 * r + n))
            if n >= 2 or r:
                pe.wait_ge(S("scores_taken"), 9 * r + n - 1 if n >= 2 else 9 * r)
            if n <= 1 and r:
                pe.wait_ge(S("gated_y_done"), r)
            st.go(1 if n % 2 or r == 0 and n < 6 else 0)
            b0 = 1024 * (n % 2)
            z = g["z"][(n + 1) % 2]
            for h in range(4):
                tile, j = divmod(h, g["hp"])
                rows = slice(j * g["dk"], (j + 1) * g["dk"])
                at_h = b0 + score_slot(g, h) * 256
                if n == 1:
                    i = pe.matmul(pm[:, at_h:at_h + 128], z[rows, tile, 0:128],
                                  z[rows, tile, 128:256], start=True, stop=True)
                    continue
                for u in range(2):
                    at = slice(u * 128, u * 128 + 128)
                    lhs, rhs = (g["k"], g["q"]) if n == 0 else (z, z)
                    i = pe.matmul(pm[:, at_h + u * 128:at_h + u * 128 + 128], lhs[rows, tile, at],
                                  rhs[rows, tile, at], start=True, stop=True)
            i.then_inc(S("scores_ready"), 1)
        pe.wait_ge(S("scores_taken"), 9 * r + 9)
        for h in range(4):
            o = pm[:, h * 256:h * 256 + 256]
            pe.matmul(o, g["v"](0, h), a_words(g, h)[:, 0:256], start=True, stop=False)
            i = pe.matmul(o[:, 128:256], g["v"](1, h), a_words(g, h)[:, 256:384], start=False, stop=True)
        i.then_inc(S("gated_o_ready"), 1)
        st.go(1)
        pe.wait_ge(S("gated_squares"), r + 1)
        for h in range(4):
            i = pe.matmul(bank(2)[0:4, 0:256], head_of(4, h), HF[:, 4 + h, :],
                          start=h == 0, stop=h == 3)
        i.then_inc(S("gated_sums"), 1)
        st.go(1)
        pe.wait_ge(S("gated_rsqrt"), r + 1)
        for h in range(4):
            i = pe.matmul(bank(3 + h // 2)[:, (h % 2) * 256:(h % 2) * 256 + 256], row_sel(4, h), SM[0:4, 256:512], start=True, stop=True)
        i.then_inc(S("gated_norm_spread"), 1)

    def gated_start_act(act, r):
        g = gated(r)
        z = g["z"][0]
        if r == 0:
            act.wait_ge(S("logit_ready"), 1)
            for t in range(2):
                act.activation(HF[:, 2 + t, :], bank(3)[:, t * 256:t * 256 + 256], ACT.Identity, bias=col("gla_b_g", t))\
                   .then_inc(S("gate_logits"), 1)
        else:
            if r == 2:
                act.wait_ge(S("gated_inputs_ready"), 2)
            act.activation(z, g["q"], ACT.Tanh, scale=0.5).then_inc(S("hg_tanh"), 1)
            act.activation(g["k"], g["b"], ACT.Tanh, scale=0.5).then_inc(S("hg_tanh"), 1)
        act.wait_ge(S("gate_abs"), r + 1)
        link(act, act.activation(z, z, ACT.Exp))
        act.activation(z, z, ACT.Ln, bias=one).then_inc(S("gate_log"), 1)

    def gated_act(act, r, st):
        g = gated(r)
        for n in range(8):
            act.wait_ge(S("gated_diff_ready"), 8 * r + n + 1)
            if n >= 2:
                act.wait_ge(S("scores_ready"), 9 * r + n)
            half = LEVELS[n]
            d, z = blocks(g["d"], half), blocks(g["z"][n % 2], half)
            act.activation(z[:, :, half:], d[:, :, half:], ACT.Exp, scale=g["scale"]).then_inc(S("gated_exp"), 1)
            act.activation(z[:, :, :half], d[:, :, :half], ACT.Exp, scale=-g["scale"]).then_inc(S("gated_exp"), 1)
            st.go(1 if n % 2 == 0 or r == 0 and n < 5 else 0)
        act.wait_ge(S("gated_exp"), 2 * (8 * r + 8))
        act.activation(GD(g), P[:, g["r"]:g["r"] + 4, :], ACT.Tanh, scale=0.5).then_inc(S("gated_r_tanh"), 1)
        act.wait_ge(S("gated_o_ready"), r + 1)
        act.activation(P[:, g["o"]:g["o"] + 4, :], pm[:, 0:1024].rearrange("p (a t) -> p a t", a=4), ACT.Copy)\
           .then_inc(S("gated_o_copied"), 1)
        act.activation(HF[:, 4:8, :], pm[:, 0:1024].rearrange("p (a t) -> p a t", a=4), ACT.Square)\
           .then_inc(S("gated_squares"), 1)
        st.go(1)
        load_sqrt(act)
        act.wait_ge(S("gated_sums"), r + 1)
        act.activation(SM[0:4, 0:256], bank(2)[0:4, 0:256], ACT.Sqrt, bias=eps4[0:4], scale=4.0 / 128).then_inc(S("gated_rms"), 1)
        st.go(1)
        act.wait_ge(S("gated_y_ready"), r + 1)
        act.activation(Y[:, g["y"]:g["y"] + 4, :], P[:, g["o"]:g["o"] + 4, :], ACT.Copy).then_inc(S("gated_y_hi"), 1)

    def GD(g):
        return HF[:, 0:4, :]

    def gated_start_dve(dve, r):
        g = gated(r)
        z = g["z"][0]
        logits = HF[:, 2:4, :] if r == 0 else g["b"]
        if r == 0:
            dve.wait_ge(S("gate_logits"), 2)
        else:
            dve.wait_ge(S("hg_tanh"), 2 * r - 1)
            link(dve, dve.scalar_tensor_tensor(g["q"], z, 1.0, g["q"], ALU.add, ALU.mult))
            dve.wait_ge(S("hg_tanh"), 2 * r)
            link(dve, dve.tensor_scalar(g["k"], g["k"], -0.25, 0.25, ALU.mult, ALU.add))
        dve.scalar_tensor_tensor(z, logits, -1.0, logits, ALU.mult, ALU.min).then_inc(S("gate_abs"), 1)
        dve.wait_ge(S("gate_log"), r + 1)
        link(dve, dve.scalar_tensor_tensor(g["d"], logits, 0.0, z, ALU.min, ALU.subtract))
        for t in range(g["nt"]):
            i = dve.tensor_tensor_scan(g["b"][:, t, :], C[:, CONES:CONES + 256], g["d"][:, t, :], 0.0, ALU.mult, ALU.add)
            if t < g["nt"] - 1:
                link(dve, i)
        i.then_inc(S("gated_inputs_ready"), 1)
        dve.wait_ge(S("gated_inputs_ready"), r + 1)

    def gated_dve(dve, r, st):
        g = gated(r)
        A = gated_a(g).rearrange("p (h j t) -> p h j t", h=4, j=3)

        def take(n):
            dve.wait_ge(S("scores_ready"), 9 * r + n + 1)
            ps = pm[:, 1024 * (n % 2):1024 * (n % 2) + 1024].rearrange("p (h u t) -> p h u t", h=4, u=2)
            if n == 0:
                i = dve.tensor_tensor(A[:, :, 0::2, :], ps, level_mask(7, F32), ALU.mult)
            elif n == 1:
                i = dve.tensor_copy(A[:, :, 1, :], ps[:, :, 0, :])
            else:
                i = dve.copy_predicated(A[:, :, 0::2, :], level_mask(n - 2, I32), ps)
            i.then_inc(S("scores_taken"), 1)
            dve.wait_ge(S("scores_taken"), 9 * r + n + 1)

        def differences(n):
            half = LEVELS[n]
            b, d = blocks(g["b"], half), blocks(g["d"], half)
            dve.tensor_tensor(d, b, b[:, :, half - 1:half].to_broadcast(list(b.shape)), ALU.subtract).then_inc(S("gated_diff_ready"), 1)

        if r:
            dve.wait_ge(S("gated_y_done"), r)
        differences(0)
        for n in range(8):
            half = LEVELS[n]
            z, q, k = blocks(g["z"][n % 2], half), blocks(g["q"], half), blocks(g["k"], half)
            dve.wait_ge(S("gated_exp"), 2 * (8 * r + n) + 2)
            dve.tensor_tensor(z[:, :, half:], z[:, :, half:], q[:, :, half:], ALU.mult).then_inc(S("gated_z_ready"), 1)
            dve.tensor_tensor(z[:, :, :half], z[:, :, :half], k[:, :, :half], ALU.mult).then_inc(S("gated_z_ready"), 1)
            if n < 7:
                differences(n + 1)
            take(n)
            st.go(1 if n % 2 == 0 or r == 0 and n < 5 else 0)
        take(8)
        dve.wait_ge(S("gated_r_tanh"), r + 1)
        link(dve, dve.scalar_tensor_tensor(GD(g), GD(g), 1.0, P[:, g["r"]:g["r"] + 4, :], ALU.add, ALU.mult))
        dve.wait_ge(S("gated_o_copied"), r + 1)
        o = P[:, g["o"]:g["o"] + 4, :]
        link(dve, dve.scalar_tensor_tensor(o, o, col(g["gain"]), GD(g), ALU.mult, ALU.mult))
        st.go(1)
        dve.wait_ge(S("gated_rms"), r + 1)
        dve.reciprocal(SM[0:4, 256:512], SM[0:4, 0:256]).then_inc(S("gated_rsqrt"), 1)
        st.go(1)
        dve.wait_ge(S("gated_norm_spread"), r + 1)
        dve.tensor_tensor(o, o, pm[:, 1536:2560].rearrange("p (a t) -> p a t", a=4), ALU.mult).then_inc(S("gated_y_ready"), 1)
        dve.wait_ge(S("gated_y_hi"), r + 1)
        dve.tensor_tensor(Y[:, 8 + g["y"]:12 + g["y"], :], o, Y[:, g["y"]:g["y"] + 4, :].bitcast(F32), ALU.subtract)\
           .then_inc(S("gated_y_done"), 1)

    def head_rows(h):
        return slice(64 * (h % 2), 64 * (h % 2) + 64), h // 2

    def moba_pe(pe, st):
        for h in range(8):
            rows, tile = head_rows(h)
            q, k = P[rows, MQ + tile, :], P[rows, MK + tile, :]
            if h >= 2:
                pe.wait_ge(S("moba_max"), 2 * (h - 1))
            for u in range(2):
                s = bank(h % 2)[:, u * 128:u * 128 + (u + 1) * 128]
                pe.matmul(s, q[:, u * 128:u * 128 + 128], k[:, 0:(u + 1) * 128], start=True, stop=False)
                pe.matmul(s, row_sel(8, h), C[0:8, CALIBI:CALIBI + (u + 1) * 128], start=False, stop=False)
                i = pe.matmul(s[:, u * 128:u * 128 + 128], CR[:, 0:128], CR[:, 256:384], start=False, stop=True)
            i.then_inc(S("moba_scores"), 1)
            st.go(1 if h % 2 else 0)
        pe.wait_ge(S("moba_max"), 16)
        for u in range(2):
            i = pe.matmul(bank(2)[0:8, u * 128:u * 128 + 128], SC[:, 72 + 8 * u:80 + 8 * u], ident, start=True, stop=True)
        i.then_inc(S("moba_max_rows"), 1)
        pe.wait_ge(S("moba_max_copied"), 1)
        for h in range(9):
            if h < 8:
                rows, tile = head_rows(h)
                q, k = P[rows, MQ + tile, :], P[rows, MK + tile, :]
                if h >= 2:
                    pe.wait_ge(S("moba_exp"), 2 * (h - 1))
                for v in range(2):
                    s = bank(h % 2)[:, 0:256] if v == 0 else bank(h % 2)[:, 256:384]
                    pe.matmul(s, k[:, v * 128:v * 128 + 128], q[:, v * 128:256], start=True, stop=False)
                    pe.matmul(s, row_sel(8, h), SM[0:8, v * 128:256], start=False, stop=False)
                    i = pe.matmul(s[:, 0:128], CR[:, 0:128], CR[:, 128:256], start=False, stop=True)
                i.then_inc(S("moba_scores_t"), 1)
                st.go(1)
            if h:
                moba_values(pe, h - 1)
        pe.wait_ge(S("moba_recip"), 1)
        pe.wait_ge(S("moba_o_copied"), 2)
        for h in range(8):
            rows, t = head_rows(h)
            i = pe.matmul(bank(t // 2)[rows, (t % 2) * 256:(t % 2) * 256 + 256], row_sel(8, h, 64), SM[0:8, 512:768],
                          start=True, stop=True)
        i.then_inc(S("moba_spread"), 1)

    def moba_values(pe, h):
        rows, tile = head_rows(h)
        w = words(4, (h % 2) * 384, 384)
        pe.wait_ge(S("moba_exp"), 2 * h + 2)
        pe.matmul(bank(2)[0:8, 0:256], head_of(8, h), w[:, 0:256], start=h == 0, stop=False)
        pe.matmul(bank(2)[0:8, 128:256], head_of(8, h), w[:, 256:384], start=False, stop=h == 7).then_inc(S("moba_den"), 1)
        o = bank(3 + tile // 2)[rows, (tile % 2) * 256:(tile % 2) * 256 + 256]
        pe.matmul(o, words(MV, h * 64, 64), w[:, 0:256], start=True, stop=False)
        pe.matmul(o[:, 128:256], words(MV + 2, h * 64, 64), w[:, 256:384], start=False, stop=True).then_inc(S("moba_o"), 1)

    def moba_act(act, st):
        st.go(2)
        for h in range(4):
            st.go(1 if h % 2 else 0)
        act.wait_ge(S("moba_max_rows"), 1)
        act.activation(SM[0:8, 0:256], bank(2)[0:8, 0:256], ACT.Copy).then_inc(S("moba_max_copied"), 1)
        for h in range(8):
            w = words(4, (h % 2) * 384, 384)
            act.wait_ge(S("moba_scores_t"), h + 1)
            if h >= 2:
                act.wait_ge(S("moba_o"), h - 1)
            for v in range(2):
                s = bank(h % 2)[:, 0:256] if v == 0 else bank(h % 2)[:, 256:384]
                act.activation(w[:, 0:256] if v == 0 else w[:, 256:384], s, ACT.Exp,
                               bias=C[:, CALCOL + v * 8 + h:CALCOL + v * 8 + h + 1]).then_inc(S("moba_exp"), 1)
            st.go(1)
        act.wait_ge(S("moba_o"), 8)
        for b in range(2):
            act.activation(P[:, 8 + 2 * b:10 + 2 * b, :], bank(3 + b).rearrange("p (a t) -> p a t", a=2), ACT.Copy)\
               .then_inc(S("moba_o_copied"), 1)
        act.wait_ge(S("moba_y"), 1)
        act.activation(Y[:, 16:20, :], P[:, 8:12, :], ACT.Copy).then_inc(S("moba_y_hi"), 1)
        act.wait_ge(S("pool_mm"), 1)
        for g in range(4):
            act.activation(P[:, g, :], pm[:, 1536 + g * 256:1792 + g * 256], ACT.Copy, scale=col("pool_scale", g))\
               .then_inc(S("pool_y"), 1)
        act.wait_ge(S("pool_y"), 4)
        act.activation(Y[:, 4:8, :], P[:, 0:4, :], ACT.Copy).then_inc(S("pool_y_hi"), 1)

    def moba_dve(dve, st):
        for h in range(8):
            dve.wait_ge(S("moba_scores"), h + 1)
            for u in range(2):
                dve.tensor_reduce(SC[:, 72 + 8 * u + h:73 + 8 * u + h], bank(h % 2)[:, u * 128:u * 128 + (u + 1) * 128],
                                  AX.X, ALU.max, negate=True).then_inc(S("moba_max"), 1)
            st.go(1 if h % 2 else 0)
        for g in range(4):
            u, a = P[:, PU + g, :], P[:, g, :]
            link(dve, dve.tensor_copy(a, u))
            for n in range(g + 1):
                src, dst = (P[:, g, :], P[:, 7, :]) if n % 2 == 0 else (P[:, 7, :], P[:, g, :])
                lag = 1 << n
                link(dve, dve.tensor_tensor(dst[:, lag:], src[:, lag:], src[:, :T - lag], ALU.add))
                link(dve, dve.tensor_copy(dst[:, :lag], src[:, :lag]))
            s = P[:, 7, :] if g % 2 == 0 else P[:, g, :]
            link(dve, dve.tensor_tensor(s[:, 0:16], s[:, 0:16], C[:, CINV + 16 * g:CINV + 16 * g + 16], ALU.mult))
            link(dve, dve.tensor_scalar(s[:, 16:], s[:, 16:], 1.0 / (2 << g), None, ALU.mult))
            dve.tensor_tensor(u, s, u, ALU.subtract).then_inc(S("pool_p"), 1)
            dve.wait_ge(S("pool_p"), g + 1)
            st.go(2)
        dve.wait_ge(S("moba_den"), 8)
        dve.reciprocal(SM[0:8, 512:768], bank(2)[0:8, 0:256]).then_inc(S("moba_recip"), 1)
        dve.wait_ge(S("moba_spread"), 1)
        o = P[:, 8:12, :]
        dve.tensor_tensor(o, o, pm[:, 0:1024].rearrange("p (a t) -> p a t", a=4), ALU.mult).then_inc(S("moba_y"), 1)
        dve.wait_ge(S("moba_y_hi"), 1)
        dve.tensor_tensor(Y[:, 24:28, :], o, Y[:, 16:20, :].bitcast(F32), ALU.subtract).then_inc(S("y1_ready"), 1)
        dve.wait_ge(S("pool_y_hi"), 1)
        dve.tensor_tensor(Y[:, 12:16, :], P[:, 0:4, :], Y[:, 4:8, :].bitcast(F32), ALU.subtract).then_inc(S("y1_ready"), 1)

    def pool_pe(pe, st):
        pe.wait_ge(S("pool_p"), 4)
        pe.wait_ge(S("moba_o_copied"), 2)
        for g in range(4):
            i = pe.matmul(pm[:, 1536 + g * 256:1792 + g * 256], PLW[:, g * 128:g * 128 + 128], P[:, PU + g, :], start=True, stop=True)
        i.then_inc(S("pool_mm"), 1)

    def rows_pe(pe, st):
        for j in range(2):
            for k in range(KT):
                i = pe.matmul(bank(4)[32:36, j * 256:j * 256 + 256], IFW[:, k * 8 + 4 * j:k * 8 + 4 * j + 4], HF[:, k, :], start=k == 0, stop=k == KT - 1)
        for k in range(KT):
            i = pe.matmul(bank(3)[0:16, 0:256], DTW[:, k * 16:k * 16 + 16], HF[:, k, :], start=k == 0, stop=k == KT - 1)
        i.then_inc(S("rows_projected"), 1)
        st.go(3)
        pe.wait_ge(S("rows_ready"), 1)
        for v in range(2):
            at = slice(v * 128, v * 128 + 128)
            pe.matmul(bank(2)[:, v * 4:v * 4 + 4], LR[:, 2, at], C[32:36, CIDENT + 32:CIDENT + 36], start=True, stop=True)
            pe.matmul(bank(3)[:, v * 16:16 + v * 16], DR[:, 2, at], C[0:16, CIDENT:CIDENT + 16], start=True, stop=True)
            i = pe.matmul(bank(3)[:, 32 + v * 16:48 + v * 16], DR[:, 0, at], C[0:16, CIDENT:CIDENT + 16], start=True, stop=True)
        i.then_inc(S("columns_ready"), 1)

    def rows_act(act, st):
        act.wait_ge(S("rows_projected"), 1)
        act.activation(LR[:, 0, :], bank(4)[32:36, 0:256], ACT.Identity, bias=RW[32:36, 0:1]).then_inc(S("rows_biased"), 1)
        act.activation(LR[:, 1, :], bank(4)[32:36, 256:512], ACT.Identity, bias=RW[32:36, 1:2]).then_inc(S("rows_biased"), 1)
        act.activation(DR[:, 0, :], bank(3)[0:16, 0:256], ACT.Identity, bias=RW[0:16, 2:3]).then_inc(S("rows_biased"), 1)
        act.activation(RW[0:16, 4:5], RW[0:16, 3:4], ACT.Exp).then_inc(S("rows_biased"), 1)
        st.go(1)
        act.wait_ge(S("rows_abs"), 2)
        link(act, act.activation(LR[:, 4, :], LR[:, 4, :], ACT.Exp))
        link(act, act.activation(DR[:, 3, :], DR[:, 3, :], ACT.Exp))
        act.activation(LR[:, 4, :], LR[:, 4, :], ACT.Ln, bias=one[32:36]).then_inc(S("rows_log"), 1)
        act.activation(DR[:, 3, :], DR[:, 3, :], ACT.Ln, bias=one[0:16]).then_inc(S("rows_log"), 1)
        st.go(1)
        act.wait_ge(S("columns_ready"), 1)
        act.activation(SC[:, 0:8], bank(2)[:, 0:8], ACT.Copy).then_inc(S("columns_copied"), 1)
        act.activation(SC[:, 8:72], bank(3)[:, 0:64], ACT.Copy).then_inc(S("columns_copied"), 1)
        act.activation(LR[:, 5, :], LR[:, 5, :], ACT.Exp, scale=-1.0).then_inc(S("exp_minus_m"), 1)

    def rows_dve(dve, st):
        dve.wait_ge(S("rows_biased"), 4)
        dve.scalar_tensor_tensor(LR[:, 4, :], LR[:, 1, :], -1.0, LR[:, 1, :], ALU.mult, ALU.min).then_inc(S("rows_abs"), 1)
        dve.scalar_tensor_tensor(DR[:, 3, :], DR[:, 0, :], -1.0, DR[:, 0, :], ALU.mult, ALU.min).then_inc(S("rows_abs"), 1)
        st.go(1)
        dve.wait_ge(S("rows_log"), 2)
        link(dve, dve.scalar_tensor_tensor(LR[:, 4, :], LR[:, 1, :], 0.0, LR[:, 4, :], ALU.min, ALU.subtract))
        link(dve, dve.tensor_tensor_scan(LR[:, 1, :], C[32:36, CONES:CONES + 256], LR[:, 4, :], 0.0, ALU.mult, ALU.add))
        link(dve, dve.tensor_tensor(LR[:, 2, :], LR[:, 0, :], LR[:, 1, :], ALU.subtract))
        link(dve, dve.memset(LR[:, 0, :], 0.0))
        link(dve, dve.tensor_tensor_scan(LR[:, 3, :], LR[:, 2, :], LR[:, 0, :], 0.0, ALU.max, ALU.add))
        link(dve, dve.tensor_tensor(LR[:, 5, :], LR[:, 1, :], LR[:, 3, :], ALU.add))
        link(dve, dve.tensor_scalar(LR[:, 3, :], LR[:, 3, :], -1.0, None, ALU.mult))
        link(dve, dve.scalar_tensor_tensor(DR[:, 0, :], DR[:, 0, :], 0.0, DR[:, 3, :], ALU.max, ALU.add))
        link(dve, dve.tensor_scalar(DR[:, 3, :], DR[:, 0, :], RW[0:16, 4:5], -1.0, ALU.mult, ALU.mult))
        link(dve, dve.tensor_tensor_scan(DR[:, 1, :], C[0:16, CONES:CONES + 256], DR[:, 3, :], 0.0, ALU.mult, ALU.add))
        dve.tensor_scalar(DR[:, 2, :], DR[:, 1, :], -1.0, None, ALU.mult).then_inc(S("rows_ready"), 1)
        st.go(1)

    def decay_matmuls(pe, dst, rows, h, src, at=0):
        for v in range(2):
            s = dst[:, 0:256] if v == 0 else dst[:, 256:384]
            pe.matmul(s, row_sel(rows, h, at=at), src[:, v * 128:256], start=True, stop=False)
            i = pe.matmul(s[:, 0:128], CR[:, 0:128], CR[:, 128:256], start=False, stop=True)
        return i

    EW = 16

    def mlstm_pe(pe, st):
        for h in range(5):
            if h < 4:
                if h == 0:
                    pe.wait_ge(S("lm_silu"), 2)
                    pe.wait_ge(S("columns_copied"), 2)
                else:
                    pe.wait_ge(S("lm_w"), 2 * h)
                q, k = P[:, LQ + h, :], P[:, LK + h, :]
                pe.matmul(bank(0)[:, 0:256], k[:, 0:128], q, start=True, stop=True)
                pe.matmul(bank(0)[:, 256:384], k[:, 128:256], q[:, 128:256], start=True, stop=True)
                decay_matmuls(pe, bank(1), 4, h, LR[:, 3, :], 32).then_inc(S("lm_scores"), 1)
                st.go(1)
            if h:
                n = h - 1
                w = words(EW, 768 + (n % 2) * 384, 384)
                pe.wait_ge(S("lm_w"), 2 * n + 2)
                if n >= 2:
                    pe.wait_ge(S("lm_h_copied"), 2 * (n - 1))
                pe.matmul(bank(2)[32:36, 0:256], head_of(4, n), w[:, 0:256], start=n == 0, stop=False, skip_group_check=True)
                pe.matmul(bank(2)[32:36, 128:256], head_of(4, n), w[:, 256:384], start=False, stop=n == 3, skip_group_check=True)
                for j in range(2):
                    o = bank(3 + n % 2)[:, j * 256:j * 256 + 256]
                    at = n * 256 + j * 128
                    pe.matmul(o, words(LV, at, 128), w[:, 0:256], start=True, stop=False)
                    i = pe.matmul(o[:, 128:256], words(LV + 4, at, 128), w[:, 256:384], start=False, stop=True)
                i.then_inc(S("lm_h"), 1)
                st.go(1)
                pe.wait_ge(S("lm_h_copied"), 2 * n + 2)
                for j in range(2):
                    i = pe.matmul(bank(2)[32:36, 256:512], head_of(4, n), P[:, EW + 6 + j, :], start=False,
                                  stop=n == 3 and j == 1, skip_group_check=True)
                i.then_inc(S("lm_sums"), 1)
        st.go(1)
        pe.wait_ge(S("lm_comb"), 1)
        for h in range(4):
            i = pe.matmul(pm[:, h * 256:h * 256 + 256], row_sel(4, h, at=32), LR[:, 2, :], start=True, stop=True)
        i.then_inc(S("lm_spread"), 1)

    def mlstm_act(act, st):
        for b in range(2):
            if b == 0:
                act.wait_ge(S("gated_y_done"), 3)
            act.activation(HF[:, 4 * b:4 * b + 4, :], P[:, LQ + 4 * b:LQ + 4 * b + 4, :], ACT.Tanh, scale=0.5).then_inc(S("lm_tanh"), 1)
        for h in range(4):
            st.go(1)
            e = words(EW, (h % 2) * 384, 384)
            act.wait_ge(S("lm_scores"), h + 1)
            if h >= 2:
                act.wait_ge(S("lm_w"), 2 * (h - 1))
            for v in range(2):
                at = slice(0, 256) if v == 0 else slice(256, 384)
                act.activation(e[:, at], bank(1)[:, at], ACT.Exp, bias=SC[:, v * 4 + h:v * 4 + h + 1]).then_inc(S("lm_exp"), 1)
            st.go(1)
            act.wait_ge(S("lm_h"), h + 1)
            if h == 0:
                act.wait_ge(S("lm_silu"), 2)
            else:
                act.wait_ge(S("lm_sums"), h)
            o = bank(3 + h % 2).rearrange("p (a t) -> p a t", a=2)
            act.activation(HF[:, 2 * h:2 * h + 2, :], o, ACT.Copy).then_inc(S("lm_h_copied"), 1)
            act.activation(P[:, EW + 6:EW + 8, :], o, ACT.Square).then_inc(S("lm_h_copied"), 1)
        load_sqrt(act)
        act.wait_ge(S("lm_ms"), 1)
        act.activation(LR[:, 1, :], LR[:, 1, :], ACT.Sqrt, bias=eps4[32:36], scale=4.0 / 256).then_inc(S("lm_rms"), 1)
        st.go(1)
        for b in range(2):
            act.wait_ge(S("lm_y"), b + 1)
            act.activation(Y[:, 16 + 4 * b:20 + 4 * b, :], HF[:, 4 * b:4 * b + 4, :], ACT.Copy).then_inc(S("lm_y_hi"), 1)

    def mlstm_dve(dve, st):
        for b in range(2):
            dve.wait_ge(S("lm_tanh"), b + 1)
            x = P[:, LQ + 4 * b:LQ + 4 * b + 4, :]
            dve.scalar_tensor_tensor(x, HF[:, 4 * b:4 * b + 4, :], 1.0, x, ALU.add, ALU.mult).then_inc(S("lm_silu"), 1)
        for h in range(4):
            st.go(1)
            e, w = words(EW, (h % 2) * 384, 384), words(EW, 768 + (h % 2) * 384, 384)
            if h >= 2:
                dve.wait_ge(S("lm_h"), h - 1)
            for v in range(2):
                at = slice(0, 256) if v == 0 else slice(256, 384)
                dve.wait_ge(S("lm_exp"), 2 * h + v + 1)
                dve.scalar_tensor_tensor(w[:, at], bank(0)[:, at], 0.25 * 128 ** -0.5, e[:, at], ALU.mult, ALU.mult).then_inc(S("lm_w"), 1)
            st.go(1)
        dve.wait_ge(S("lm_sums"), 4)
        dve.wait_ge(S("exp_minus_m"), 1)
        a, b, c = (LR[:, n, :] for n in range(3))
        link(dve, dve.tensor_copy(a, bank(2)[32:36, 0:256]))
        link(dve, dve.scalar_tensor_tensor(a, a, -1.0, a, ALU.mult, ALU.max))
        link(dve, dve.tensor_tensor(a, a, LR[:, 5, :], ALU.max))
        link(dve, dve.reciprocal(a, a))
        link(dve, dve.tensor_tensor(b, bank(2)[32:36, 256:512], a, ALU.mult))
        dve.tensor_tensor(b, b, a, ALU.mult).then_inc(S("lm_ms"), 1)
        dve.wait_ge(S("lm_rms"), 1)
        link(dve, dve.reciprocal(c, b))
        dve.tensor_tensor(c, c, a, ALU.mult).then_inc(S("lm_comb"), 1)
        st.go(1)
        dve.wait_ge(S("lm_spread"), 1)
        for h in range(4):
            for j in range(2):
                t = HF[:, 2 * h + j, :]
                link(dve, dve.scalar_tensor_tensor(t, t, col("ml_norm", j), pm[:, h * 256:h * 256 + 256], ALU.mult, ALU.mult))
            if h % 2:
                b = h // 2
                t = HF[:, 4 * b:4 * b + 4, :]
                dve.scalar_tensor_tensor(t, P[:, LO + 4 * b:LO + 4 * b + 4, :], 1.0, t, ALU.add, ALU.mult).then_inc(S("lm_y"), 1)
        st.go(1)
        for b in range(2):
            dve.wait_ge(S("lm_y_hi"), b + 1)
            dve.tensor_tensor(Y[:, 24 + 4 * b:28 + 4 * b, :], HF[:, 4 * b:4 * b + 4, :], Y[:, 16 + 4 * b:20 + 4 * b, :].bitcast(F32),
                              ALU.subtract).then_inc(S("lm_y_done"), 1)

    TMP, CB, MW = 24, 48, 8

    def cb_words(g):
        return words(CB, g * 384, 384) if g < 3 else words(MW, 1536, 384)

    def ssd_pe(pe, st):
        pe.wait_ge(S("mb_silu"), 4)
        for g in range(4):
            if g >= 2:
                pe.wait_ge(S("mb_cb"), g - 1)
            b = bank(g % 2)
            pe.matmul(b[:, 0:256], P[:, XB + g, 0:128], P[:, XC + g, :], start=True, stop=True)
            pe.matmul(b[:, 256:384], P[:, XB + g, 128:256], P[:, XC + g, 128:256], start=True, stop=True).then_inc(S("mb_bc"), 1)
        for n in range(4):
            v, q = divmod(n, 2)
            if n >= 2:
                pe.wait_ge(S("mb_xt"), n - 1)
            for j in range(4):
                i = pe.matmul(bank(2 + n % 2)[:, j * 128:j * 128 + 128], P[:, XS + 4 * q + j, v * 128:v * 128 + 128], ident, start=True, stop=True)
            i.then_inc(S("mb_xtp"), 1)
        pe.wait_ge(S("mb_xt"), 4)
        pe.wait_ge(S("mb_cb"), 4)
        for h in range(17):
            if h < 16:
                if h >= 2:
                    pe.wait_ge(S("mb_exp"), 2 * (h - 1))
                decay_matmuls(pe, bank(h % 2), 16, h, DR[:, 1, :]).then_inc(S("mb_decay"), 1)
                st.go(1)
            if h:
                n = h - 1
                w = words(MW, 768 + (n % 2) * 384, 384)
                pe.wait_ge(S("mb_w"), 2 * n + 2)
                if n >= 4 and n % 2 == 0:
                    pe.wait_ge(S("mb_y"), n // 2 - 1)
                o = bank(2 + (n // 2) % 2)[64 * (n % 2):64 * (n % 2) + 64, 0:256]
                pe.matmul(o, words(TMP, n * 64, 64), w[:, 0:256], start=True, stop=False)
                pe.matmul(o[:, 128:256], words(TMP + 4, n * 64, 64), w[:, 256:384], start=False, stop=True).then_inc(S("mb_o"), 1)
        for t in range(8):
            if t % 4 == 0:
                pe.wait_ge(S("mb_squares"), t // 4 + 1)
            i = pe.matmul(bank(4)[0:4, 0:256], head_of(4, t // 2), P[:, TMP + t, :], start=t == 0, stop=t == 7)
        i.then_inc(S("mb_sums"), 1)
        st.go(1)
        pe.wait_ge(S("mb_rsqrt"), 1)
        for g in range(4):
            i = pe.matmul(pm[:, g * 256:g * 256 + 256], row_sel(4, g), SM[0:4, 256:512], start=True, stop=True)
        i.then_inc(S("mb_spread"), 1)

    def ssd_act(act, st):
        for n, at in enumerate((XB, XS, XZ)):
            if n == 0:
                act.wait_ge(S("lm_y_done"), 2)
            else:
                act.wait_ge(S("mb_silu"), 2 * n)
            for b in range(2):
                act.activation(P[:, TMP + 4 * b:TMP + 4 * b + 4, :], P[:, at + 4 * b:at + 4 * b + 4, :], ACT.Tanh, scale=0.5).then_inc(S("mb_tanh"), 1)
        for g in range(4):
            act.wait_ge(S("mb_bc"), g + 1)
            act.activation(cb_words(g), bank(g % 2)[:, 0:384], ACT.Copy, scale=0.25).then_inc(S("mb_cb"), 1)
        act.wait_ge(S("mb_silu"), 6)
        for n in range(4):
            v, q = divmod(n, 2)
            act.wait_ge(S("mb_xtp"), n + 1)
            act.activation(words(TMP, v * 1024 + q * 512, 512), bank(2 + n % 2), ACT.Copy).then_inc(S("mb_xt"), 1)
        for h in range(16):
            e = words(MW, (h % 2) * 384, 384)
            act.wait_ge(S("mb_decay"), h + 1)
            if h >= 2:
                act.wait_ge(S("mb_w"), 2 * (h - 1))
            for v in range(2):
                at = slice(0, 256) if v == 0 else slice(256, 384)
                act.activation(e[:, at], bank(h % 2)[:, at], ACT.Exp, bias=SC[:, 8 + v * 16 + h:9 + v * 16 + h]).then_inc(S("mb_exp"), 1)
            st.go(1)
        for b in range(2):
            act.wait_ge(S("mb_u"), b + 1)
            act.activation(P[:, TMP + 4 * b:TMP + 4 * b + 4, :], P[:, XS + 4 * b:XS + 4 * b + 4, :], ACT.Square).then_inc(S("mb_squares"), 1)
        load_sqrt(act)
        act.wait_ge(S("mb_sums"), 1)
        act.activation(SM[0:4, 0:256], bank(4)[0:4, 0:256], ACT.Sqrt, bias=eps16[0:4], scale=1.0 / 256).then_inc(S("mb_rms"), 1)
        st.go(1)
        act.wait_ge(pair_done, Y0_READ)
        for b in range(2):
            act.wait_ge(S("mb_yn"), b + 1)
            act.activation(Y[:, 4 * b:4 * b + 4, :], P[:, XS + 4 * b:XS + 4 * b + 4, :], ACT.Copy).then_inc(S("mb_y_hi"), 1)

    def ssd_dve(dve, st):
        for n, at in enumerate((XB, XS, XZ)):
            for b in range(2):
                dve.wait_ge(S("mb_tanh"), 2 * n + b + 1)
                x = P[:, at + 4 * b:at + 4 * b + 4, :]
                dve.scalar_tensor_tensor(x, P[:, TMP + 4 * b:TMP + 4 * b + 4, :], 1.0, x, ALU.add, ALU.mult).then_inc(S("mb_silu"), 1)
        for h in range(17):
            if h < 16:
                e, w = words(MW, (h % 2) * 384, 384), words(MW, 768 + (h % 2) * 384, 384)
                if h == 0:
                    dve.wait_ge(S("mb_cb"), 4)
                if h >= 2:
                    dve.wait_ge(S("mb_o"), h - 1)
                for v in range(2):
                    at = slice(0, 256) if v == 0 else slice(256, 384)
                    dve.wait_ge(S("mb_exp"), 2 * h + v + 1)
                    dve.scalar_tensor_tensor(w[:, at], e[:, at], SC[:, 40 + v * 16 + h:41 + v * 16 + h],
                                             cb_words(h // 4)[:, at], ALU.mult, ALU.mult).then_inc(S("mb_w"), 1)
                st.go(1)
            if h and h % 2 == 0:
                t = h // 2 - 1
                dve.wait_ge(S("mb_o"), h)
                x = P[:, XS + t, :]
                dve.scalar_tensor_tensor(x, x, col("mb_d", t), bank(2 + t % 2)[:, 0:256], ALU.mult, ALU.add).then_inc(S("mb_y"), 1)
        dve.wait_ge(S("mb_y"), 8)
        for b in range(2):
            x = P[:, XS + 4 * b:XS + 4 * b + 4, :]
            dve.tensor_tensor(x, x, P[:, XZ + 4 * b:XZ + 4 * b + 4, :], ALU.mult).then_inc(S("mb_u"), 1)
        dve.wait_ge(S("mb_rms"), 1)
        dve.reciprocal(SM[0:4, 256:512], SM[0:4, 0:256]).then_inc(S("mb_rsqrt"), 1)
        st.go(1)
        dve.wait_ge(S("mb_spread"), 1)
        for t in range(8):
            x = P[:, XS + t, :]
            i = dve.scalar_tensor_tensor(x, x, col("mb_norm", t), pm[:, (t // 2) * 256:(t // 2) * 256 + 256], ALU.mult, ALU.mult)
            if t % 4 == 3:
                i.then_inc(S("mb_yn"), 1)
            else:
                link(dve, i)
        dve.wait_ge(S("mb_yn"), 2)
        for b in range(2):
            dve.wait_ge(S("mb_y_hi"), b + 1)
            dve.tensor_tensor(Y[:, 8 + 4 * b:12 + 4 * b, :], P[:, XS + 4 * b:XS + 4 * b + 4, :], Y[:, 4 * b:4 * b + 4, :].bitcast(F32),
                              ALU.subtract).then_inc(S("mb_y_done"), 1)

    Y0_READ = BLK2 + 12 + 12 + 16 + 4 + 4
    L.update({k: v for k, v in locals().items() if k != "L"})
    feed_forward(nc, block, S, L)


def feed_forward(nc, block, S, L):
    (X, HF, XH, XL, Y, P, C, PC, SM, SC, pp, pm, bank, col, link, Stream, pair_done, hi_ready, lo_ready, norm_pe,
     norm_act, norm_dve, lo_parts, mix_act, x_ready, mixes, three_passes, whi, wlo, raw, split_hi, split_lo,
     wait_evac, x_tiles_ready) = (
        L[k] for k in ("X HF XH XL Y P C PC SM SC pp pm bank col link Stream pair_done hi_ready lo_ready norm_pe "
                       "norm_act norm_dve lo_parts mix_act x_ready mixes three_passes whi wlo raw split_hi split_lo "
                       "wait_evac x_tiles_ready").split())
    moba_pe, moba_act, moba_dve, pool_pe, gated_pe, gated_act, gated_dve, gated_start_act, gated_start_dve = (
        L[k] for k in "moba_pe moba_act moba_dve pool_pe gated_pe gated_act gated_dve gated_start_act gated_start_dve".split())
    rows_pe, rows_act, rows_dve, mlstm_pe, mlstm_act, mlstm_dve, ssd_pe, ssd_act, ssd_dve = (
        L[k] for k in "rows_pe rows_act rows_dve mlstm_pe mlstm_act mlstm_dve ssd_pe ssd_act ssd_dve".split())
    G1W = L["G1W"]

    F0 = [FFN1, FFN2]

    def up_pe(pe, b, p, slot, g, rewrite=None):
        pe.wait_ge(lo_ready, p + 1)
        if not (isinstance(g, int) and g < 2):
            pe.wait_ge(S("up_taken" if b else "up_product"), g - 1)
        for half in range(2):
            for k in range(KT):
                at = k * 256 + half * 128
                if half == 0:
                    x_tiles_ready(pe, rewrite, k)
                done = three_passes(pe, pp[slot][:, half * 256:half * 256 + 256], [u[:, slot, at:at + 128] for u in (whi, wlo)],
                                    [u[:, k, :] for u in (XH, XL)], k == 0, k == KT - 1)
        done.then_inc(pair_done, 1)

    def down_pe(pe, b, p, slot, j, parity):
        pe.wait_ge(lo_ready, p + 1)
        first = isinstance(j, int) and j == 0
        last = isinstance(j, int) and j == FT // 2 - 1
        for kk in range(2):
            pe.wait_ge(S("hidden_ready"), 2 * j + (FT * b + 1 + kk))
            y = [Y[:, 4 * part + 2 * parity + kk, :] for part in range(2)]
            for m in range(KT):
                at = kk * 1024 + m * 128
                for n, (a, c) in enumerate(((whi, 0), (whi, 1), (wlo, 0))):
                    done = pe.matmul(pm[:, 512 + m * 256:768 + m * 256], a[:, slot, at:at + 128], y[c],
                                     start=first and kk == 0 and n == 0 and m % 2 == 0,
                                     stop=last and kk == 1 and n == 2, skip_group_check=True)
        done.then_inc(pair_done, 1)

    def ffn_pe(pe, b, rewrite):
        f = F0[b]
        for g in range(2):
            up_pe(pe, b, f + g, (f + g) % RING, g, rewrite if g == 0 else None)
        up_pe(pe, b, f + 2, (f + 2) % RING, 2)
        up_pe(pe, b, f + 3, (f + 3) % RING, 3)
        down_pe(pe, b, f + 4, (f + 4) % RING, 0, 0)
        with pe.Fori(0, 4) as i:
            p, s = i * 6 + (f + 5), f + 5
            up_pe(pe, b, p, s % RING, i * 4 + 4)
            up_pe(pe, b, p + 1, (s + 1) % RING, i * 4 + 5)
            down_pe(pe, b, p + 2, (s + 2) % RING, i * 2 + 1, 1)
            up_pe(pe, b, p + 3, (s + 3) % RING, i * 4 + 6)
            up_pe(pe, b, p + 4, (s + 4) % RING, i * 4 + 7)
            down_pe(pe, b, p + 5, (s + 5) % RING, i * 2 + 2, 0)
        up_pe(pe, b, f + 29, (f + 29) % RING, 20)
        up_pe(pe, b, f + 30, (f + 30) % RING, 21)
        down_pe(pe, b, f + 31, (f + 31) % RING, 9, 1)
        down_pe(pe, b, f + 32, (f + 32) % RING, 10, 0)

    def temps(par):
        return [P[:, 16 + 4 * par + n, :] for n in range(4)]

    def fcol(name, k):
        return PC[:, COLS[name] + k:COLS[name] + k + 1] if isinstance(k, int) else PC[:, bass.ds(k + COLS[name], 1)]

    def act_turn(act, b, p, slot, turn, prev, late):
        if prev is not None:
            g, ps_slot, par = prev
            n = g + (FT * b + 1)
            th, pr, cg, cu = temps(par % 2)
            gate, value = pp[ps_slot][:, 0:256], pp[ps_slot][:, 256:512]
            act.wait_ge(pair_done, p)
            if b == 0:
                act.activation(th, gate, ACT.Tanh, scale=0.5).then_inc(S("up_tanh"), 1)
            else:
                act.activation(cg, gate, ACT.Identity, bias=fcol("ffn_conv_b", g), scale=fcol("ffn_conv_w", g + 88)).then_inc(S("up_conv"), 1)
                act.activation(cu, value, ACT.Identity, bias=fcol("ffn_conv_b", g + 22), scale=fcol("ffn_conv_w", g + 110)).then_inc(S("up_conv"), 1)
        if turn is not None:
            split_hi(act, p + 2, slot, turn)
        if prev is not None:
            if b:
                act.wait_ge(S("up_taps"), 3 * g + 3)
                act.activation(th, cg, ACT.Tanh, scale=0.5).then_inc(S("up_tanh"), 1)
            act.wait_ge(S("up_product"), n)
            act.activation(Y[:, par, :], pr, ACT.Copy).then_inc(S("hidden_hi"), 1)

    def dve_turn(dve, b, p, slot, turn, prev, late):
        if prev is not None:
            g, ps_slot, par = prev
            n = g + (FT * b + 1)
            th, pr, cg, cu = temps(par % 2)
            gate, value = pp[ps_slot][:, 0:256], pp[ps_slot][:, 256:512]
            if b:
                dve.wait_ge(S("up_conv"), 2 * g + 2)
                for k in (1, 0):
                    lag = 2 - k
                    for c, src, off in ((cg, gate, 0), (cu, value, 22)):
                        if k == 0:
                            dve.wait_ge(S("up_taps"), 3 * g + (2 if off else 1))
                        i = dve.scalar_tensor_tensor(c[:, lag:], src[:, 0:256 - lag], fcol("ffn_conv_w", g + (44 * k + off)),
                                                     c[:, lag:], ALU.mult, ALU.add)
                        i.then_inc(S("up_taken" if k == 0 and off else "up_taps"), 1)
        if late is not None:
            g2, par2 = late
            dve.wait_ge(S("hidden_hi"), g2 + (FT * b + 1))
            dve.tensor_tensor(Y[:, 4 + par2, :], temps(par2 % 2)[1], Y[:, par2, :].bitcast(F32), ALU.subtract)\
               .then_inc(S("hidden_ready"), 1)
        if turn is not None:
            split_lo(dve, p + 2, slot)
        if prev is not None:
            dve.wait_ge(S("up_tanh"), n)
            if b:
                dve.wait_ge(S("up_taken"), g + 1)
            dve.scalar_tensor_tensor(pr, th, 1.0, cg if b else gate, ALU.add, ALU.mult).then_inc(S("up_gated"), 1)
            dve.wait_ge(S("up_gated"), n)
            dve.scalar_tensor_tensor(pr, pr, 0.5, cu if b else value, ALU.mult, ALU.mult).then_inc(S("up_product"), 1)

    def ffn_side(eng, b, turn_fn):
        f = F0[b]

        def turn(n, g=None, late=None):
            at = f + n + 2
            turn_fn(eng, b, f + n, at % RING, at // RING if at < NPAIRS else None,
                    None if g is None else (g, (f + n - 1) % RING, g % 4), None if late is None else (late, late % 4))

        turn(0)
        turn(1, 0)
        turn(2, 1, 0)
        turn(3, 2, 1)
        turn(4, 3, 2)
        with eng.Fori(0, 4) as i:
            for j, (g, late) in enumerate(((None, 3), (4, None), (5, 4), (None, 5), (6, None), (7, 6))):
                n = 5 + j
                at = f + n + 2
                turn_fn(eng, b, i * 6 + (f + n), at % RING, i * 2 + at // RING,
                        None if g is None else (i * 4 + g, (f + n - 1) % RING, g % 4),
                        None if late is None else (i * 4 + late, late % 4))
        turn(29, None, 19)
        turn(30, 20)
        turn(31, 21, 20)
        turn(32, None, 21)

    def acc(q):
        return pm[:, 512 + q * 512:1024 + q * 512].rearrange("p (a t) -> p a t", a=2)

    @block.tensor
    def _(pe):
        st = Stream(pe, "pe")
        pe.wait_ge(S("consts_loaded"), 16)
        norm_pe(pe, 0)
        st.window(0, 6, 0)
        st.go(1)
        pe.wait_ge(S("tables_loaded"), 16)
        for w in ("G1W", "G2W", "PLW", "IFW", "DTW"):
            pe.wait_ge(S(f"loaded_{w}"), 16)
        for k in range(KT):
            i = pe.matmul(bank(4)[0:16, 0:256], G1W[:, k * 16:k * 16 + 16], HF[:, k, :], start=k == 0, stop=k == KT - 1)
        i.then_inc(S("g1_ready"), 1)
        st.finish()
        st.window(6, 6)
        wait_evac(pe, 5)
        gated_pe(pe, 0, st)
        st.finish()
        st.window(12, 14)
        st.go(1)
        wait_evac(pe, 11)
        pe.wait_ge(S("tables_loaded"), 16)
        pe.wait_ge(S("masks_rounded"), 2)
        moba_pe(pe, st)
        pool_pe(pe, st)
        st.finish()
        st.window(26, 6)
        pe.wait_ge(S("gated_y_done"), 1)
        pe.wait_ge(S("y1_ready"), 2)
        st.finish()
        st.window(32, 4, 1)
        st.finish()
        norm_pe(pe, 1)
        norm_pe(pe, 2)
        ffn_pe(pe, 0, 2)
        norm_pe(pe, 3)
        norm_pe(pe, 4)
        st.p = BLK2
        st.window(BLK2, 12, 3)
        st.go(1)
        rows_pe(pe, st)
        st.finish()
        st.window(BLK2 + 12, 12)
        st.go(1)
        wait_evac(pe, BLK2 + 11)
        gated_pe(pe, 1, st)
        gated_pe(pe, 2, st)
        st.finish()
        st.window(BLK2 + 24, 16)
        st.go(1)
        wait_evac(pe, BLK2 + 23)
        mlstm_pe(pe, st)
        st.finish()
        st.window(BLK2 + 40, 20)
        st.go(1)
        wait_evac(pe, BLK2 + 39)
        pe.wait_ge(S("gated_y_done"), 3)
        pe.wait_ge(S("lm_y_done"), 2)
        ssd_pe(pe, st)
        st.finish()
        st.window(BLK2 + 60, 4)
        pe.wait_ge(S("mb_y_done"), 2)
        st.finish()
        st.window(BLK2 + 64, 4, 4)
        st.finish()
        norm_pe(pe, 5)
        ffn_pe(pe, 1, 5)
        norm_pe(pe, 6)

    @block.scalar
    def _(act):
        st = Stream(act, "act")
        act.wait_ge(S("x_loaded"), 16)
        act.wait_ge(S("cols_loaded"), 16)
        act.wait_ge(S("scalars_set"), 4)
        norm_act(act, 0, X, 0, between=st.start)
        act.wait_ge(S("g1_ready"), 1)
        act.activation(SM[0:16, 0:256], bank(4)[0:16, 0:256], ACT.Copy).then_inc(S("g1_copied"), 1)
        st.window(0, 6)
        st.finish()
        st.window(6, 6)
        wait_evac(act, 5)
        act.wait_ge(S("tables_loaded"), 16)
        act.wait_ge(S("masks_loaded"), 16)
        act.activation(L["CR"][:, 0:128], C[:, CIDENT:CIDENT + 128], ACT.Copy).then_inc(S("masks_rounded"), 1)
        act.activation(L["CR"][:, 128:384], P[:, MASKS, :], ACT.Copy).then_inc(S("masks_rounded"), 1)
        gated_start_act(act, 0)
        gated_act(act, 0, st)
        st.finish()
        st.window(12, 14)
        wait_evac(act, 11)
        moba_act(act, st)
        st.finish()
        st.window(26, 6)
        st.finish()
        mix_act(act, 1)
        st.window(32, 4)
        st.finish()
        wait_evac(act, 35)
        norm_act(act, 1, P[:, OUT:OUT + 8, :], None)
        norm_act(act, 2, X, 1, updated=0)
        ffn_side(act, 0, act_turn)
        act.wait_ge(pair_done, BLK2)
        for q in range(4):
            act.activation(P[:, OUT + 2 * q:OUT + 2 * q + 2, :], acc(q), ACT.Copy).then_inc(S("ffn_out"), 1)
        act.wait_ge(S("ffn_out"), 4)
        norm_act(act, 3, P[:, OUT:OUT + 8, :], None)
        norm_act(act, 4, X, 2, updated=8)
        st.p = BLK2
        st.window(BLK2, 12)
        st.go(1)
        rows_act(act, st)
        st.go(BLK2 + 9 - st.p)
        wait_evac(act, BLK2 + 7)
        gated_start_act(act, 1)
        st.go(1)
        gated_start_act(act, 2)
        st.finish()
        st.window(BLK2 + 12, 12)
        gated_act(act, 1, st)
        gated_act(act, 2, st)
        st.finish()
        st.window(BLK2 + 24, 16)
        wait_evac(act, BLK2 + 23)
        mlstm_act(act, st)
        st.finish()
        st.window(BLK2 + 40, 20)
        wait_evac(act, BLK2 + 39)
        ssd_act(act, st)
        st.finish()
        st.window(BLK2 + 60, 4)
        st.finish()
        mix_act(act, 2)
        st.window(BLK2 + 64, 4)
        st.finish()
        wait_evac(act, BLK2 + 67)
        norm_act(act, 5, X, 3)
        ffn_side(act, 1, act_turn)
        act.wait_ge(S("x_final"), 4)
        norm_act(act, 6, X, None)

    @block.vector
    def _(dve):
        st = Stream(dve, "dve")
        for n, v in ((127, EPS), (126, 4 * EPS), (125, 1.0), (124, 16 * EPS)):
            dve.memset(SC[:, n:n + 1], v).then_inc(S("scalars_set"), 1)
        dve.wait_ge(S("consts_loaded"), 16)
        dve.wait_ge(S("cols_loaded"), 16)
        dve.wait_ge(S("x_loaded"), 16)
        st.start()
        norm_dve(dve, 0, X, "norm_mix_pre", 0)
        st.window(0, 6)
        st.finish()
        st.window(6, 6)
        wait_evac(dve, 5)
        dve.wait_ge(S("tables_loaded"), 16)
        gated_start_dve(dve, 0)
        gated_dve(dve, 0, st)
        st.finish()
        st.window(12, 14)
        wait_evac(dve, 11)
        moba_dve(dve, st)
        st.finish()
        st.window(26, 6)
        wait_evac(dve, 25)
        st.finish()
        lo_parts(dve, 4 * mixes[1], 0.5)
        st.window(32, 4)
        st.finish()
        norm_dve(dve, 1, P[:, OUT:OUT + 8, :], "norm_mix_post", None)
        norm_dve(dve, 2, X, "norm_ffn_pre", 1)
        ffn_side(dve, 0, dve_turn)
        norm_dve(dve, 3, P[:, OUT:OUT + 8, :], "norm_ffn_post", None)
        norm_dve(dve, 4, X, "norm1_g", 2)
        st.p = BLK2
        st.window(BLK2, 12)
        dve.wait_ge(S("loaded_RW"), 16)
        st.go(1)
        rows_dve(dve, st)
        st.go(BLK2 + 9 - st.p)
        wait_evac(dve, BLK2 + 7)
        gated_start_dve(dve, 1)
        st.go(1)
        gated_start_dve(dve, 2)
        st.finish()
        st.window(BLK2 + 12, 12)
        gated_dve(dve, 1, st)
        gated_dve(dve, 2, st)
        st.finish()
        st.window(BLK2 + 24, 16)
        wait_evac(dve, BLK2 + 23)
        mlstm_dve(dve, st)
        st.finish()
        st.window(BLK2 + 40, 20)
        wait_evac(dve, BLK2 + 39)
        ssd_dve(dve, st)
        st.finish()
        st.window(BLK2 + 60, 4)
        st.finish()
        lo_parts(dve, 4 * mixes[2], 0.5)
        st.window(BLK2 + 64, 4)
        st.finish()
        norm_dve(dve, 5, X, "norm2_g", 3)
        ffn_side(dve, 1, dve_turn)
        dve.wait_ge(pair_done, NPAIRS)
        for q in range(4):
            dve.tensor_tensor(X[:, 2 * q:2 * q + 2, :], X[:, 2 * q:2 * q + 2, :], acc(q), ALU.add).then_inc(S("x_final"), 1)
        norm_dve(dve, 6, X, "final_g", None, P[:, 8:16, :], "result_ready")


def pair_columns(w, cols):
    return w[:, cols].reshape(KT, 128, 256).transpose(1, 0, 2).reshape(128, PW)


def weight_stream(i):
    s = np.empty((NPAIRS, 128, PW), np.float32)
    n = 0

    def put(a):
        nonlocal n
        s[n] = a
        n += 1

    def span(w, start, width):
        for c in range(start, start + width, 256):
            put(pair_columns(w, slice(c, c + 256)))

    w = i["w_in"][0]
    q, k, v, g1, r, u, mq, mk, mv, gates = np.cumsum([0, 256, 256, 512, 16, 512, 512, 512, 512, 512]).tolist()
    for start, width in ((q, 256), (k, 256), (r, 512), (v, 512), (mq, 512), (mk, 512), (mv, 512), (u, 512), (gates, 3072)):
        span(w, start, width)
    branches = [i[f"w_branch_{x}"][0] for x in "abc"]
    for j in range(6):
        groups = [divmod(4 * j + g, 3) for g in range(4)]
        put(np.concatenate([branches[br][:, m * 128:m * 128 + 128].reshape(4, 128, 128).transpose(1, 0, 2).reshape(128, 512)
                            for m, br in groups], 1))
    span(i["w_out"][0], 0, 1024)

    def ffn(gate, up, down):
        def one(g):
            put(np.concatenate([gate[:, g * 128:g * 128 + 128].reshape(KT, 128, 128),
                                up[:, g * 128:g * 128 + 128].reshape(KT, 128, 128)], 2).transpose(1, 0, 2).reshape(128, PW))

        def two(j):
            put(down[j * 256:j * 256 + 256].reshape(2, 128, 1024).transpose(1, 0, 2).reshape(128, PW))

        one(0)
        one(1)
        for j in range(1, FT // 2):
            one(2 * j)
            one(2 * j + 1)
            two(j - 1)
        two(FT // 2 - 1)

    ffn(i["ffn_w_gate"][0], i["ffn_w_up"][0], i["ffn_w_down"][0])
    w = i["w_in_2"][0]
    hq, hf, hi, hg, lqk, lv, lif, lo, z, xbc, dt, gates = np.cumsum(
        [0, 1024, 1024, 1024, 1024, 1024, 1024, 8, 1024, 1024, 2048, 16]).tolist()
    for start, width in ((hq, 1024), (hf, 1024), (hi, 1024), (hg, 1024), (lqk, 1024), (lv, 1024), (lo, 1024), (xbc, 2048), (z, 1024)):
        span(w, start, width)
    for b, name in enumerate(("w_br_hg_2", "w_br_ml_2", "w_br_mb_2")):
        span(w, gates + 1024 * b, 1024)
        span(i[name][0], 0, 1024)
    span(i["w_out_2"][0], 0, 1024)
    up = i["w_up_2"][0]
    ffn(up[:, :FF], up[:, FF:], i["w_down_2"][0])
    assert n == NPAIRS, n
    return s


def channel_columns(i):
    def cols(v):
        return np.asarray(v).reshape(-1, 128).T

    parts = [cols(i[k][0]) for k in ("norm_mix_pre", "norm_mix_post", "norm_ffn_pre", "norm_ffn_post", "gla_b_g", "gla_norm",
                                     "pool_scale", "norm1_g_2", "hg_norm_g_2", "ml_norm_g_2")]
    parts += [cols(np.repeat(i["mb_d_2"][0], 64)), cols(i["mb_norm_g_2"][0]), cols(i["norm2_g_2"][0]), cols(i["final_g_2"])]
    parts += [cols(np.concatenate([i["ml_conv_b_2"][0], i["mb_conv_b_2"][0]]))]
    parts += [cols(np.concatenate([i["ml_conv_w_2"][0][k], i["mb_conv_w_2"][0][k]])) for k in range(4)]
    parts += [cols(i["ffn_conv_b_2"][0])] + [cols(i["ffn_conv_w_2"][0][k]) for k in range(3)]
    return np.ascontiguousarray(np.concatenate(parts, 1))


def kernel(**inputs):
    import concourse.bacc as bacc
    from concourse.bass_utils import run_bass_kernel_spmd

    i = {k: np.asarray(v) for k, v in inputs.items()}

    def small(w):
        return np.ascontiguousarray(w.reshape(KT, 128, -1).transpose(1, 0, 2).reshape(128, -1))

    head_rows = np.zeros((36, 8), np.float32)
    head_rows[32:36, 0], head_rows[32:36, 1] = i["ml_gate_b_2"][0][:4], i["ml_gate_b_2"][0][4:]
    head_rows[0:16, 2], head_rows[0:16, 3] = i["mb_dt_bias_2"][0], i["mb_a_log_2"][0]
    w1, w2 = i["w_in"][0], i["w_in_2"][0]
    arrays = {
        "stream": weight_stream(i),
        "xT": small(i["x"][0].T).reshape(128, KT, T),
        "cols": channel_columns(i),
        "consts": constants(),
        "masks": causal_masks(),
        "g1w": small(w1[:, 1024:1040]),
        "g2w": np.ascontiguousarray(i["gla_w_g2"][0]),
        "poolw": np.ascontiguousarray(i["pool_w"][0].transpose(1, 0, 2).reshape(128, 512)),
        "ifw": small(w2[:, 6144:6152]),
        "dtw": small(w2[:, 10248:10264]),
        "rows": head_rows,
    }
    nc = bacc.Bacc("TRN2", target_bir_lowering=False, num_devices=1)
    aps = [nc.dram_tensor(k, a.shape, F32, kind="ExternalInput").ap() for k, a in arrays.items()]
    out = nc.dram_tensor("out", (128, KT, T), F32, kind="ExternalOutput").ap()
    build(nc, *aps, out)
    r = run_bass_kernel_spmd(nc, [arrays], core_ids=[0]).results[0]["out"]
    return np.ascontiguousarray(r.reshape(128, KT, T).transpose(2, 1, 0).reshape(1, T, D))
```

```python
import concourse.bass as bass
from concourse import mybir
from contextlib import ExitStack
import numpy as np

F32 = mybir.dt.float32
F32R = mybir.dt.float32r
I32 = mybir.dt.int32
ACT = mybir.ActivationFunctionType
ALU = mybir.AluOpType
AX = mybir.AxisListType

T = 256
D = 1024
KT = D // 128
FF = 2816
FT = FF // 128
PW = 2048
EPS = 1e-6
NEG = -1e30
RING = 3
LEVELS = [128, 64, 32, 16, 8, 4, 2, 1]

GQ, GK, GR, GV = 0, 2, 4, 8
MQ, MK, MV = 12, 16, 20
PU, GATE1 = 24, 28
HQ, HFG, HI, HG, HK = 0, 8, 16, 24, 48
LQ, LK, LV, LO = 32, 36, 40, 24
XS, XB, XC, XZ = 0, 8, 12, 16
GATE2 = [32, 40, 32]
SQ = 40
RMS_T, RCP_T = 38, 39
MASKS = 52
OUT = 0
POOL_TILES = 53

PAIRS1 = (
    [("B", "copy", GQ, 0.125)] + [("B", "copy", GK, 1.0)]
    + [("B", "copy", GR + 2 * j, 1.0) for j in range(2)]
    + [("A", "copyA", GV + j, 2) for j in range(2)]
    + [("B", "copy", MQ + 2 * j, 0.125) for j in range(2)]
    + [("B", "copy", MK + 2 * j, 1.0) for j in range(2)]
    + [("A", "copyA", MV + j, 2) for j in range(2)]
    + [("B", "copy", PU + 2 * j, 1.0) for j in range(2)]
    + [("B", "tanh", GATE1 + 2 * j, 0.5) for j in range(12)]
    + [("BR1", "mix1", j, 0) for j in range(6)]
    + [("B", "copy", OUT + 2 * j, 1.0) for j in range(4)]
)
_order = "xoxoxoxxoxxx"
SSD_ORDER = [(what, _order[:n].count(what)) for n, what in enumerate(_order)]
LAST_O = _order.rindex("o")
PAIRS2 = (
    [("B", "copy", HQ + 2 * j, 1.0) for j in range(4)]
    + [("B", "copy", HFG + 2 * j, 1.0) for j in range(4)]
    + [("A", "copyA", HI + j, 4) for j in range(4)]
    + [("B", "copy", HG + 2 * j, 1.0) for j in range(4)]
    + [("B", "conv", LQ + 2 * j, 2 * j) for j in range(4)]
    + [("A", "copyA", LV + j, 4) for j in range(4)]
    + [("B", "conv", XS + 2 * j, 8 + 2 * j) if what == "x" else ("B", "tanh", LO + 2 * j, 0.5) for what, j in SSD_ORDER]
    + [("B", "copy", XZ + 2 * j, 1.0) for j in range(4)]
    + [("B", "tanh", GATE2[0] + 2 * j, 0.5) for j in range(4)]
    + [("Y0", "mix2", j, 0) for j in range(4)]
    + [("B", "tanh", GATE2[1] + 2 * j, 0.5) for j in range(4)]
    + [("Y1", "mix2", j, 1) for j in range(4)]
    + [("B", "tanh", GATE2[2] + 2 * j, 0.5) for j in range(4)]
    + [("Y0", "mix2", j, 2) for j in range(4)]
    + [("B", "resid", 2 * j, 0) for j in range(4)]
)
N1, N2, NF = len(PAIRS1), len(PAIRS2), FT + FT // 2
FFN1 = N1
BLK2 = N1 + NF
FFN2 = BLK2 + N2
NPAIRS = FFN2 + NF
PAIR = dict(enumerate(PAIRS1)) | {BLK2 + n: s for n, s in enumerate(PAIRS2)}


W_GLA, W_MOBA, W_BRANCH, W_OUT = (6, 8), (14, 12), (26, 6), (32, 4)
W_START = (0, 6)
W_ROWS, W_HGRN, W_MLSTM, W_SSD, W_BRANCH2, W_OUT2 = (
    (BLK2 + first, n) for first, n in ((0, 12), (12, 12), (24, 16), (40, 20), (60, 4), (64, 4)))
Y0_READ = W_SSD[0] + 8


def taken(p):
    who = "act_taken" if PAIR[p][1] in ("copy", "tanh", "copyA") else "dve_taken"
    act = ("copy", "tanh", "copyA")
    return who, sum((PAIR[x][1] in act) == (who == "act_taken") for x in PAIR if x <= p)


COLS = {}
_n = 0
for _name, _k in (("norm_mix_pre", KT), ("norm_mix_post", KT), ("norm_ffn_pre", KT), ("norm_ffn_post", KT),
                  ("gla_b_g", 2), ("gla_norm", 1), ("pool_scale", 4), ("norm1_g", KT), ("hg_norm", 1),
                  ("ml_norm", 2), ("mb_d", KT), ("mb_norm", KT), ("norm2_g", KT), ("final_g", KT),
                  ("conv_b", 24), ("conv_w", 96), ("ffn_conv_b", 44), ("ffn_conv_w", 132)):
    COLS[_name] = _n
    _n += _k
NCOLS = _n

CIDENT, CONES, CLEVEL = 0, 128, 384
CALIBI = CLEVEL + 8 * 128
CALCOL, CHEAD, CINV = CALIBI + 256, CALIBI + 272, CALIBI + 303
NCONST = CINV + 64


def constants():
    c = np.zeros((128, NCONST), np.float32)
    s, t = np.arange(128)[:, None], np.arange(128)[None, :]
    c[:, CIDENT:CIDENT + 128] = np.eye(128)
    c[:, CONES:CONES + 256] = 1.0
    for n, half in enumerate(LEVELS[1:]):
        same = (s // (2 * half)) == (t // (2 * half))
        c[:, CLEVEL + n * 128:CLEVEL + (n + 1) * 128] = same & (s % (2 * half) < half) & (t % (2 * half) >= half)
    c[:, CLEVEL + 7 * 128:CLEVEL + 8 * 128] = s == t
    slope = 2.0 ** -(np.arange(8) + 1.0)
    c[:8, CALIBI:CALIBI + 256] = slope[:, None] * np.arange(256)[None, :]
    for v in range(2):
        c[:, CALCOL + v * 8:CALCOL + v * 8 + 8] = slope[None, :] * (np.arange(128)[:, None] + 128 * v)
    c[:, CHEAD + 15] = 1.0
    for g, w in enumerate((2, 4, 8, 16)):
        c[:, CINV + 16 * g:CINV + 16 * g + 16] = 1.0 / np.minimum(np.arange(16) + 1, w)
    return c


def causal_masks():
    s, t = np.arange(128)[:, None], np.arange(128)[None, :]
    return np.concatenate([np.where(s <= t, 0.0, NEG), np.where(t <= s, 0.0, NEG)], 1).astype(np.float32)


def build(nc, *arrays):
    with ExitStack() as ctx:
        program(nc, ctx, *arrays)


def program(nc, ctx, stream, xT, cols, consts, masks, g1w, g2w, poolw, ifw, dtw, rows, out):
    def sb(name, shape, dt=F32):
        return ctx.enter_context(nc.sbuf_tensor(name, shape, dt))

    sems = {}

    def S(name):
        if name not in sems:
            sems[name] = ctx.enter_context(nc.semaphore(name))
        return sems[name]

    raw = sb("raw", [128, RING, PW])
    whi = sb("whi", [128, RING, PW], F32R)
    wlo = sb("wlo", [128, RING, PW], F32R)
    X = sb("X", [128, KT, T])
    HF = sb("HF", [128, KT, T])
    XH = sb("XH", [128, KT, T], F32R)
    XL = sb("XL", [128, KT, T], F32R)
    y_at = nc.sbuf_base
    Y = sb("Y", [128, 32, T], F32R)
    U = nc.alloc_sbuf_tensor_at("U", [128, 16, T], F32, offset=y_at + 16 * T * 4)
    P = sb("P", [128, POOL_TILES, T])
    C = sb("C", [128, NCONST])
    CR = sb("CR", [128, 384], F32R)
    PC = sb("PC", [128, NCOLS])
    G1W = sb("G1W", [128, KT * 16])
    IFW = sb("IFW", [128, KT * 8])
    DTW = sb("DTW", [128, KT * 16])
    RW = sb("RW", [36, 8])
    SC = sb("SC", [128, 128])
    R = sb("R", [36, 7 * T])
    SM = R[0:16, 0:3 * T]
    LR = R[32:36, 0:6 * T].rearrange("p (a t) -> p a t", a=6)
    DR = R[0:16, 3 * T:7 * T].rearrange("p (a t) -> p a t", a=4)
    RMS, RCP = P[:, RMS_T, :], P[:, RCP_T, :]
    G2W, PLW = U[0:16, 4:5, :].rearrange("p a t -> p (a t)"), U[:, 6:8, :].rearrange("p a t -> p (a t)")
    pp = [ctx.enter_context(nc.psum_tensor(f"pp{i}", [128, 512], F32)) for i in range(RING)]
    pm = ctx.enter_context(nc.psum_tensor("pm", [128, 5 * 512], F32))

    arrived = [S(f"weights_arrived{i}") for i in range(RING)]
    hi_ready, lo_ready, pair_done = (S(n) for n in ("hi_ready", "lo_ready", "pair_done"))
    conv_started = S("conv_started")
    ident = C[:, CIDENT:CIDENT + 128]
    ones = C[:, CONES:CONES + 128]

    def col(name, i=0):
        return PC[:, COLS[name] + i:COLS[name] + i + 1]

    block = ctx.enter_context(nc.Block())

    @block.sync
    def _(sp):
        def load(p, slot):
            src = stream[p] if isinstance(p, int) else stream[bass.ds(p, 1), :, :].rearrange("a p n -> p (a n)")
            sp.dma_start(raw[:, slot, :], src).then_inc(arrived[slot], 16)

        sp.dma_start(X[:, :, :], xT).then_inc(S("x_loaded"), 16)
        sp.dma_start(C[:, 0:CLEVEL], consts[:, 0:CLEVEL]).then_inc(S("consts_loaded"), 16)
        sp.dma_start(PC[:, :], cols).then_inc(S("cols_loaded"), 16)
        for p in range(RING):
            load(p, p)
        sp.dma_start(C[:, CLEVEL:], consts[:, CLEVEL:]).then_inc(S("tables_loaded"), 16)
        sp.dma_start(P[:, MASKS, :], masks).then_inc(S("masks_loaded"), 16)
        for name, dst, src in (("G1W", G1W, g1w), ("G2W", G2W, g2w), ("PLW", PLW, poolw), ("IFW", IFW, ifw),
                               ("DTW", DTW, dtw), ("RW", RW, rows)):
            sp.dma_start(dst[:, :], src).then_inc(S(f"loaded_{name}"), 16)
        whole = (NPAIRS - RING) // RING
        with sp.Fori(1, 1 + whole) as i:
            for slot in range(RING):
                sp.wait_ge(lo_ready, i * RING + (slot + 1 - RING))
                load(i * RING + slot, slot)
        for p in range(RING * (1 + whole), NPAIRS):
            sp.wait_ge(lo_ready, p - RING + 1)
            load(p, p % RING)
        for k in range(0, KT, 2):
            sp.wait_ge(S("result_ready"), k + 2)
            sp.dma_start(out[:, k:k + 2, :], P[:, 8 + k:10 + k, :]).then_inc(S("result_stored"), 16)
        sp.wait_ge(S("result_stored"), 16 * KT // 2)

    def bank(n):
        return pm[:, n * 512:(n + 1) * 512]

    def split_hi(act, p, slot, turn):
        act.wait_ge(arrived[slot], turn * 16 + 16)
        if not isinstance(p, int) or p >= RING:
            act.wait_ge(pair_done, p - (RING - 1))
        act.activation(whi[:, slot, :], raw[:, slot, :], ACT.Copy).then_inc(hi_ready, 1)

    def split_lo(dve, p, slot):
        dve.wait_ge(hi_ready, p + 1)
        if not isinstance(p, int) or p >= RING:
            dve.wait_ge(pair_done, p - (RING - 1))
        dve.tensor_tensor(wlo[:, slot, :], raw[:, slot, :], whi[:, slot, :].bitcast(F32), ALU.subtract).then_inc(lo_ready, 1)

    def three_passes(pe, dst, lhs, rhs, first, last, **kw):
        for n, (a, b) in enumerate(((lhs[0], rhs[0]), (lhs[0], rhs[1]), (lhs[1], rhs[0]))):
            done = pe.matmul(dst, a, b, start=first and n == 0, stop=last and n == 2, **kw)
        return done

    def first_pair(pe, slot, rewrite):
        for need, passes in (("x_hi", ((whi, XH), (wlo, XH))), ("x_lo", ((whi, XL),))):
            for k in range(KT):
                if k % 2 == 0:
                    pe.wait_ge(S(need), 4 * rewrite + k // 2 + 1)
                for half in range(2):
                    at = k * 256 + half * 128
                    for w, x in passes:
                        done = pe.matmul(pp[slot][:, half * 256:half * 256 + 256], w[:, slot, at:at + 128], x[:, k, :],
                                         start=need == "x_hi" and k == 0 and half == 0 and w is whi,
                                         stop=need == "x_lo" and k == KT - 1, skip_group_check=True)
        done.then_inc(pair_done, 1)

    def pair_matmuls(pe, p, slot, form, rewrite=None):
        pe.wait_ge(lo_ready, p + 1)
        if rewrite is not None:
            first_pair(pe, slot, rewrite)
            return
        w = [t[:, slot, :] for t in (whi, wlo)]
        if form == "BR1":
            q = p - (FFN1 - 10)
            for g in range(4):
                br = (4 * q + g) % 3
                dst = (pp[slot][:, g * 256:g * 256 + 256] if g < 2
                       else bank(slot)[:, (g - 2) * 256:(g - 2) * 256 + 256])
                for k in range(4):
                    y = [Y[:, 8 * part + br * 4 + k if br < 2 else 16 + 8 * part + k, :] for part in range(2)]
                    at = (g * 4 + k) * 128
                    done = three_passes(pe, dst, [u[:, at:at + 128] for u in w], y, k == 0, k == 3)
            done.then_inc(pair_done, 1)
            return
        x = [XH, XL]
        base = 0
        if form in ("Y0", "Y1"):
            x, base = None, 16 * (form == "Y1")
        for half in range(2):
            for k in range(KT):
                dst = pp[slot][:, half * 256:half * 256 + 256]
                if form == "A":
                    lhs = [u[:, k, half * 128:half * 128 + 128] for u in x]
                    rhs = [u[:, k * 256:k * 256 + 256] for u in w]
                else:
                    at = k * 256 + half * 128
                    lhs = [u[:, at:at + 128] for u in w]
                    rhs = ([u[:, k, :] for u in x] if x else [Y[:, base + 8 * part + k, :] for part in range(2)])
                done = three_passes(pe, dst, lhs, rhs, k == 0, k == KT - 1)
        done.then_inc(pair_done, 1)

    def evac_act(act, p, spec):
        form, kind, at, arg = spec
        ps = pp[p % RING]
        if kind in ("copy", "tanh", "copyA", "conv"):
            act.wait_ge(pair_done, p + 1)
        if kind == "copy":
            act.activation(P[:, at:at + 2, :], ps[:, :].rearrange("p (a t) -> p a t", a=2), ACT.Copy,
                           scale=arg).then_inc(S("act_taken"), 1)
        elif kind == "tanh":
            act.activation(P[:, at:at + 2, :], ps[:, :].rearrange("p (a t) -> p a t", a=2), ACT.Tanh,
                           scale=arg).then_inc(S("act_taken"), 1)
        elif kind == "copyA":
            act.activation(P[:, at:at + arg + 1:arg, :], ps[:, :].rearrange("p (a t) -> p a t", a=2),
                           ACT.Copy).then_inc(S("act_taken"), 1)
        elif kind == "conv":
            for h in range(2):
                act.activation(P[:, at + h, :], ps[:, h * 256:h * 256 + 256], ACT.Identity,
                               bias=col("conv_b", arg + h), scale=col("conv_w", 72 + arg + h)).then_inc(conv_started, 1)

    dve_count = {"conv": 0}

    def evac_dve(dve, p, spec):
        form, kind, at, arg = spec
        ps = pp[p % RING]
        own = (S("dve_taken"), taken(p)[1])
        if kind == "conv":
            dve_count["conv"] += 2
            dve.wait_ge(conv_started, dve_count["conv"])
            before = [None, None]
            for k in (2, 1, 0):
                lag = 3 - k
                for h in range(2):
                    if before[h]:
                        settled(dve, before[h])
                    i = dve.scalar_tensor_tensor(P[:, at + h, lag:], ps[:, h * 256:h * 256 + 256 - lag],
                                                 col("conv_w", 24 * k + arg + h), P[:, at + h, lag:],
                                                 ALU.mult, ALU.add)
                    if (k, h) == (0, 1):
                        i.then_inc(S("dve_taken"), 1)
                    else:
                        before[h] = mark(dve, i)
            settled(dve, before[0])
            dve.wait_ge(*own)
        elif kind == "mix2":
            dve.wait_ge(pair_done, p + 1)
            g = GATE2[arg] + 2 * at
            flat = ps[:, :].rearrange("p (a t) -> p a t", a=2)
            dst = HF[:, 2 * at:2 * at + 2, :] if arg == 0 else P[:, g:g + 2, :]
            dve.scalar_tensor_tensor(dst, P[:, g:g + 2, :], 1.0, flat, ALU.add, ALU.mult).then_inc(S("dve_taken"), 1)
            if arg:
                dve.wait_ge(*own)
                i = dve.tensor_tensor(HF[:, 2 * at:2 * at + 2, :], HF[:, 2 * at:2 * at + 2, :], P[:, g:g + 2, :], ALU.add)
                if arg == 2:
                    i.then_inc(S("mixed_ready2"), 1)
                else:
                    link(dve, i)
        elif kind == "mix1":
            dve.wait_ge(pair_done, p + 1)
            groups = [divmod(4 * at + g, 3) for g in range(4)]
            for g, (m, br) in enumerate(groups):
                src = (ps[:, g * 256:g * 256 + 256] if g < 2
                       else bank(p % RING)[:, (g - 2) * 256:(g - 2) * 256 + 256])
                gt = GATE1 + 8 * br + m
                i = dve.scalar_tensor_tensor(P[:, gt, :] if br else HF[:, m, :], P[:, gt, :], 1.0, src, ALU.add, ALU.mult)
                if g == 3:
                    i.then_inc(S("dve_taken"), 1)
                else:
                    last = mark(dve, i)
            settled(dve, last)
            for g, (m, br) in enumerate(groups):
                if g == 3:
                    dve.wait_ge(*own)
                if br:
                    i = dve.tensor_tensor(HF[:, m, :], HF[:, m, :], P[:, GATE1 + 8 * br + m, :], ALU.add)
                    if br == 2:
                        i.then_inc(S("mixed_ready1"), 1)
                    else:
                        link(dve, i)
        elif kind == "resid":
            dve.wait_ge(pair_done, p + 1)
            dve.tensor_tensor(X[:, at:at + 2, :], X[:, at:at + 2, :],
                              ps[:, :].rearrange("p (a t) -> p a t", a=2), ALU.add).then_inc(S("dve_taken"), 1)

    def wait_evac(eng, p, of=("act_taken", "dve_taken")):
        found = {}
        for x in PAIR:
            if x <= p:
                who, n = taken(x)
                found[who] = n
        for who, n in found.items():
            if who in of:
                eng.wait_ge(S(who), n)

    chains = {}

    def mark(eng, ins):
        name = "chain_" + chains["names"][id(eng)]
        chains[name] = chains.get(name, 0) + 1
        ins.then_inc(S(name), 1)
        return chains[name]

    def settled(eng, n):
        eng.wait_ge(S("chain_" + chains["names"][id(eng)]), n)

    def link(eng, ins):
        settled(eng, mark(eng, ins))

    class Stream:

        def __init__(self, eng, who):
            self.eng, self.who, self.p = eng, who, 0
            chains.setdefault("names", {})[id(eng)] = who

        def start(self):
            for p in range(2):
                if self.who == "act":
                    split_hi(self.eng, p, p, 0)
                elif self.who == "dve":
                    split_lo(self.eng, p, p)

        def ahead(self, p):
            if p + 2 < NPAIRS:
                if self.who == "act":
                    split_hi(self.eng, p + 2, (p + 2) % RING, (p + 2) // RING)
                elif self.who == "dve":
                    split_lo(self.eng, p + 2, (p + 2) % RING)

        def evac(self, p):
            if p in PAIR:
                if self.who == "act":
                    evac_act(self.eng, p, PAIR[p])
                elif self.who == "dve":
                    evac_dve(self.eng, p, PAIR[p])

        def go(self, n=1):
            for _ in range(n):
                p = self.p
                if p >= self.stop:
                    return
                if self.who == "pe":
                    if p - RING in PAIR:
                        who, n = taken(p - RING)
                        self.eng.wait_ge(S(who), n)
                    pair_matmuls(self.eng, p, p % RING, PAIR[p][0], self.rewrite)
                    self.rewrite = None
                else:
                    self.ahead(p)
                    if p > self.first:
                        self.evac(p - 1)
                self.p += 1

        def window(self, first, n, rewrite=None):
            assert self.p == first, (self.p, first)
            self.first, self.stop, self.rewrite = first, first + n, rewrite

        def finish(self):
            self.go(self.stop - self.p)
            if self.who != "pe":
                self.evac(self.stop - 1)

    def norm_pe(pe, n):
        for k in range(KT):
            if k % 2 == 0:
                pe.wait_ge(S("norm_squares"), 4 * n + k // 2 + 1)
            i = pe.matmul(bank(0)[:, 0:256], ones, P[:, SQ + k, :], start=k == 0, stop=k == KT - 1)
        i.then_inc(S("norm_sums"), 1)

    def wait_acc(eng, b, q):
        if q < 3:
            eng.wait_ge(S("acc_done"), 3 * b + q + 1)
        else:
            eng.wait_ge(pair_done, BLK2 if b == 0 else NPAIRS)

    def acc(q):
        return pm[:, 512 + q * 512:1024 + q * 512].rearrange("p (a t) -> p a t", a=2)

    def load_sqrt(act):
        link(act, act.activation(SC[:, 123:124], SC[:, 125:126], ACT.Sqrt))

    def norm_act(act, n, src, split, updated=None, between=None, first=False, counter="x_updated"):
        for k in range(0, KT, 2):
            if updated is not None:
                act.wait_ge(S(counter), updated + (k + 2 if counter == "x_updated" else k // 2 + 1))
            if first:
                wait_acc(act, 0, k // 2)
                act.activation(P[:, SQ + k:SQ + k + 2, :], acc(k // 2), ACT.Square).then_inc(S("norm_squares"), 1)
                act.activation(P[:, OUT + k:OUT + k + 2, :], acc(k // 2), ACT.Copy).then_inc(S("ffn_out"), 1)
                continue
            act.activation(P[:, SQ + k:SQ + k + 2, :], src[:, k:k + 2, :], ACT.Square).then_inc(S("norm_squares"), 1)
        if between:
            between()
        load_sqrt(act)
        act.wait_ge(S("norm_sums"), n + 1)
        act.activation(RMS[:, :], bank(0)[:, 0:256], ACT.Sqrt, bias=SC[:, 127:128], scale=1.0 / D).then_inc(S("norm_rms"), 1)
        if split is not None:
            for k in range(0, KT, 2):
                act.wait_ge(S("norm_tiles"), 8 * split + k + 2)
                act.activation(XH[:, k:k + 2, :], HF[:, k:k + 2, :], ACT.Copy).then_inc(S("x_hi"), 1)

    def norm_dve(dve, n, src, gain, split, dst=None, done=None):
        dve.wait_ge(S("norm_rms"), n + 1)
        link(dve, dve.reciprocal(RCP[:, :], RMS[:, :]))
        if split is not None:
            for k in range(KT):
                dve.scalar_tensor_tensor(HF[:, k, :], src[:, k, :], col(gain, k), RCP[:, :], ALU.mult, ALU.mult)\
                   .then_inc(S("norm_tiles"), 1)
            lo_parts(dve, 4 * splits[split])
        elif done:
            for k in range(KT):
                dve.scalar_tensor_tensor(dst[:, k, :], src[:, k, :], col(gain, k), RCP[:, :], ALU.mult, ALU.mult)\
                   .then_inc(S(done), 1)
        else:
            before = 8 * (n == 3)
            for k in range(KT + 1):
                if k < KT:
                    dve.scalar_tensor_tensor(src[:, k, :], src[:, k, :], col(gain, k), RCP[:, :], ALU.mult, ALU.mult)\
                       .then_inc(S("post_scaled"), 1)
                if k:
                    dve.wait_ge(S("post_scaled"), before + k)
                    dve.tensor_tensor(X[:, k - 1, :], X[:, k - 1, :], src[:, k - 1, :], ALU.add).then_inc(S("x_updated"), 1)

    splits = {0: 0, 1: 2, 2: 3, 3: 5}
    mixes = {1: 1, 2: 4}

    def lo_part(dve, base, k, scale=1.0):
        dve.wait_ge(S("x_hi"), base + k // 2 + 1)
        dve.scalar_tensor_tensor(XL[:, k:k + 2, :], HF[:, k:k + 2, :], scale, XH[:, k:k + 2, :].bitcast(F32),
                                 ALU.mult, ALU.subtract).then_inc(S("x_lo"), 1)

    def lo_parts(dve, base, scale=1.0):
        for k in range(0, KT, 2):
            lo_part(dve, base, k, scale)

    def mix_act(act, b):
        for k in range(0, KT, 2):
            act.wait_ge(S(f"mixed_ready{b}"), k + 2 if b == 1 else k // 2 + 1)
            act.activation(XH[:, k:k + 2, :], HF[:, k:k + 2, :], ACT.Copy, scale=0.5).then_inc(S("x_hi"), 1)

    eps1, eps4, one, eps16 = (SC[:, 127:128], SC[:, 126:127], SC[:, 125:126], SC[:, 124:125])

    def words(tile, start, n):
        return P[:, :, :].rearrange("p a t -> p (a t)")[:, tile * T + start:tile * T + start + n]

    def head_of(m, h):
        return C[:, CHEAD + 15 - h:CHEAD + 15 - h + m]

    def row_sel(rows, h, n=128, at=0):
        return C[at:at + rows, CIDENT + at + h:CIDENT + at + h + 1].to_broadcast([rows, n])

    def gated(r):
        if r == 0:
            return dict(nt=2, hp=2, dk=64, q=P[:, GQ:GQ + 2, :], k=P[:, GK:GK + 2, :], b=HF[:, 0:2, :], d=HF[:, 2:4, :],
                        z=(HF[:, 4:6, :], HF[:, 6:8, :]), A=34, o=GQ, r=GR, v=lambda v, h: words(GV + 2 * v, h * 128, 128),
                        scale=1.0 / 16, y=0, gain="gla_norm")
        h0 = 4 * (r - 1)
        return dict(nt=4, hp=1, dk=128, q=P[:, HQ + h0:HQ + h0 + 4, :], k=P[:, HK:HK + 4, :] if r == 1 else U[:, 6:10, :], b=P[:, HFG + h0:HFG + h0 + 4, :],
                    d=HF[:, 0:4, :], z=(HF[:, 4:8, :], U[:, 10:14, :]), A=None, o=HQ + h0, r=HG + h0,
                    v=lambda v, h: words(HI + 4 * v, (h0 + h) * 128, 128), scale=1.0, y=h0, gain="hg_norm")

    def blocks(ap, half):
        return ap.rearrange("p a t -> p (a t)").rearrange("p (n w) -> p n w", w=2 * half)

    def a_words(g, h):
        at = score_slot(g, h) * 384
        return gated_a(g)[:, at:at + 384]

    def score_slot(g, h):
        tile, j = divmod(h, g["hp"])
        return j * 2 + tile if g["hp"] == 2 else h

    def gated_a(g):
        return words(g["A"], 0, 1536) if g["A"] is not None else U[:, 0:6, :].rearrange("p a t -> p (a t)")

    def level_mask(n, dt):
        m = C[:, CLEVEL + n * 128:CLEVEL + (n + 1) * 128]
        return (m.bitcast(dt) if dt != F32 else m).unsqueeze(1).unsqueeze(1).to_broadcast([128, 4, 2, 128])

    def gated_pe(pe, r, st):
        g = gated(r)
        if r == 0:
            pe.wait_ge(S("g1_copied"), 1)
            for t in range(2):
                i = pe.matmul(bank(3)[:, t * 256:t * 256 + 256], G2W[:, t * 128:t * 128 + 128], SM[0:16, 0:256], start=True, stop=True)
            i.then_inc(S("logit_ready"), 1)
        for n in range(9):
            if n == 0:
                st.go(1 if r == 0 else 0)
                pe.wait_ge(S("gated_inputs_ready"), r + 1)
            else:
                pe.wait_ge(S("gated_z_ready"), 2 * (8 * r + n))
            if n >= 2 or r:
                pe.wait_ge(S("scores_taken"), 9 * r + n - 1 if n >= 2 else 9 * r)
            if n == 1 and r:
                pe.wait_ge(S("gated_y_ready"), r)
            st.go(1 if n % 2 or r == 0 and 0 < n < 6 else 0)
            b0 = 1024 * (n % 2)
            z = g["z"][(n + 1) % 2]
            for h in range(4):
                tile, j = divmod(h, g["hp"])
                rows = slice(j * g["dk"], (j + 1) * g["dk"])
                at_h = b0 + score_slot(g, h) * 256
                if n == 1:
                    i = pe.matmul(pm[:, at_h:at_h + 128], z[rows, tile, 0:128],
                                  z[rows, tile, 128:256], start=True, stop=True)
                    continue
                for u in range(2):
                    at = slice(u * 128, u * 128 + 128)
                    lhs, rhs = (g["k"], g["q"]) if n == 0 else (z, z)
                    i = pe.matmul(pm[:, at_h + u * 128:at_h + u * 128 + 128], lhs[rows, tile, at],
                                  rhs[rows, tile, at], start=True, stop=True)
            i.then_inc(S("scores_ready"), 1)
        pe.wait_ge(S("scores_taken"), 9 * r + 9)
        for h in range(4):
            o = pm[:, h * 256:h * 256 + 256]
            pe.matmul(o, g["v"](0, h), a_words(g, h)[:, 0:256], start=True, stop=False)
            i = pe.matmul(o[:, 128:256], g["v"](1, h), a_words(g, h)[:, 256:384], start=False, stop=True)
        i.then_inc(S("gated_o_ready"), 1)
        st.go(1)
        pe.wait_ge(S("gated_squares"), r + 1)
        for h in range(4):
            i = pe.matmul(bank(2)[0:4, 0:256], head_of(4, h), HF[:, 4 + h, :],
                          start=h == 0, stop=h == 3)
        i.then_inc(S("gated_sums"), 1)
        st.go(1)
        pe.wait_ge(S("gated_rsqrt"), r + 1)
        for h in range(4):
            i = pe.matmul(bank(3 + h // 2)[:, (h % 2) * 256:(h % 2) * 256 + 256], row_sel(4, h), SM[0:4, 256:512], start=True, stop=True)
        i.then_inc(S("gated_norm_spread"), 1)

    def gated_start_act(act, r, st):
        g = gated(r)
        z = g["z"][0]
        if r == 0:
            act.wait_ge(S("logit_ready"), 1)
            for t in range(2):
                act.activation(HF[:, 2 + t, :], bank(3)[:, t * 256:t * 256 + 256], ACT.Identity, bias=col("gla_b_g", t))\
                   .then_inc(S("gate_logits"), 1)
        else:
            if r == 2:
                act.wait_ge(S("gated_inputs_ready"), 2)
            act.activation(z, g["q"], ACT.Tanh, scale=0.5).then_inc(S("hg_tanh"), 1)
            act.activation(g["k"], g["b"], ACT.Tanh, scale=0.5).then_inc(S("hg_tanh"), 1)
            st.go(1)
        act.wait_ge(S("gate_abs"), r + 1)
        link(act, act.activation(z, z, ACT.Exp))
        act.activation(z, z, ACT.Ln, bias=one).then_inc(S("gate_log"), 1)

    def gated_act(act, r, st):
        def exponentials(n, r=r):
            g = gated(r)
            act.wait_ge(S("gated_diff_ready"), 8 * r + n + 1)
            if n >= 2:
                act.wait_ge(S("scores_ready"), 9 * r + n)
            half = LEVELS[n]
            d, z = blocks(g["d"], half), blocks(g["z"][n % 2], half)
            act.activation(z[:, :, half:], d[:, :, half:], ACT.Exp, scale=g["scale"]).then_inc(S("gated_exp"), 1)
            act.activation(z[:, :, :half], d[:, :, :half], ACT.Exp, scale=-g["scale"]).then_inc(S("gated_exp"), 1)

        g = gated(r)
        for n in range(8):
            if n or r < 2:
                exponentials(n)
            st.go(1 if n % 2 == 0 or r == 0 and n < 5 else 0)
        act.wait_ge(S("gated_exp"), 2 * (8 * r + 8))
        act.activation(GD(g), P[:, g["r"]:g["r"] + 4, :], ACT.Tanh, scale=0.5).then_inc(S("gated_r_tanh"), 1)
        act.wait_ge(S("gated_o_ready"), r + 1)
        act.activation(P[:, g["o"]:g["o"] + 4, :], pm[:, 0:1024].rearrange("p (a t) -> p a t", a=4), ACT.Copy)\
           .then_inc(S("gated_o_copied"), 1)
        act.activation(HF[:, 4:8, :], pm[:, 0:1024].rearrange("p (a t) -> p a t", a=4), ACT.Square)\
           .then_inc(S("gated_squares"), 1)
        st.go(1)
        load_sqrt(act)
        act.wait_ge(S("gated_sums"), r + 1)
        act.activation(SM[0:4, 0:256], bank(2)[0:4, 0:256], ACT.Sqrt, bias=eps4[0:4], scale=4.0 / 128).then_inc(S("gated_rms"), 1)
        st.go(1)
        if r == 1:
            exponentials(0, 2)
        act.wait_ge(S("gated_y_ready"), r + 1)
        act.activation(Y[:, g["y"]:g["y"] + 4, :], P[:, g["o"]:g["o"] + 4, :], ACT.Copy).then_inc(S("gated_y_hi"), 1)

    def GD(g):
        return HF[:, 0:4, :]

    def gated_start_dve(dve, r, st):
        g = gated(r)
        z = g["z"][0]
        logits = HF[:, 2:4, :] if r == 0 else g["b"]
        if r == 0:
            dve.wait_ge(S("gate_logits"), 2)
        else:
            dve.wait_ge(S("hg_tanh"), 2 * r - 1)
            link(dve, dve.scalar_tensor_tensor(g["q"], z, 1.0, g["q"], ALU.add, ALU.mult))
            dve.wait_ge(S("hg_tanh"), 2 * r)
            link(dve, dve.tensor_scalar(g["k"], g["k"], -0.25, 0.25, ALU.mult, ALU.add))
        dve.scalar_tensor_tensor(z, logits, -1.0, logits, ALU.mult, ALU.min).then_inc(S("gate_abs"), 1)
        if r:
            st.go(1)
        dve.wait_ge(S("gate_log"), r + 1)
        link(dve, dve.scalar_tensor_tensor(g["d"], logits, 0.0, z, ALU.min, ALU.subtract))
        for t in range(g["nt"]):
            i = dve.tensor_tensor_scan(g["b"][:, t, :], C[:, CONES:CONES + 256], g["d"][:, t, :], 0.0, ALU.mult, ALU.add)
            if t < g["nt"] - 1:
                link(dve, i)
        i.then_inc(S("gated_inputs_ready"), 1)
        dve.wait_ge(S("gated_inputs_ready"), r + 1)

    def gated_dve(dve, r, st):
        g = gated(r)
        A = gated_a(g).rearrange("p (h j t) -> p h j t", h=4, j=3)

        def take(n):
            dve.wait_ge(S("scores_ready"), 9 * r + n + 1)
            ps = pm[:, 1024 * (n % 2):1024 * (n % 2) + 1024].rearrange("p (h u t) -> p h u t", h=4, u=2)
            if n == 0:
                i = dve.tensor_tensor(A[:, :, 0::2, :], ps, level_mask(7, F32), ALU.mult)
            elif n == 1:
                i = dve.tensor_copy(A[:, :, 1, :], ps[:, :, 0, :])
            else:
                i = dve.copy_predicated(A[:, :, 0::2, :], level_mask(n - 2, I32), ps)
            i.then_inc(S("scores_taken"), 1)
            dve.wait_ge(S("scores_taken"), 9 * r + n + 1)

        def y_low(r):
            g = gated(r)
            o = P[:, g["o"]:g["o"] + 4, :]
            dve.wait_ge(S("gated_y_hi"), r + 1)
            dve.tensor_tensor(Y[:, 8 + g["y"]:12 + g["y"], :], o, Y[:, g["y"]:g["y"] + 4, :].bitcast(F32), ALU.subtract)\
               .then_inc(S("gated_y_done"), 1)

        def differences(n, g=g):
            half = LEVELS[n]
            b, d = blocks(g["b"], half), blocks(g["d"], half)
            dve.tensor_tensor(d, b, b[:, :, half - 1:half].to_broadcast(list(b.shape)), ALU.subtract).then_inc(S("gated_diff_ready"), 1)

        if r < 2:
            differences(0)
        for n in range(8):
            half = LEVELS[n]
            z, q, k = blocks(g["z"][n % 2], half), blocks(g["q"], half), blocks(g["k"], half)
            dve.wait_ge(S("gated_exp"), 2 * (8 * r + n) + 2)
            dve.tensor_tensor(z[:, :, half:], z[:, :, half:], q[:, :, half:], ALU.mult).then_inc(S("gated_z_ready"), 1)
            dve.tensor_tensor(z[:, :, :half], z[:, :, :half], k[:, :, :half], ALU.mult).then_inc(S("gated_z_ready"), 1)
            if n < 7:
                differences(n + 1)
            if r == 2 and n == 0:
                y_low(1)
            take(n)
            st.go(1 if n % 2 == 0 or r == 0 and n < 5 else 0)
        take(8)
        dve.wait_ge(S("gated_r_tanh"), r + 1)
        link(dve, dve.scalar_tensor_tensor(GD(g), GD(g), 1.0, P[:, g["r"]:g["r"] + 4, :], ALU.add, ALU.mult))
        dve.wait_ge(S("gated_o_copied"), r + 1)
        o = P[:, g["o"]:g["o"] + 4, :]
        link(dve, dve.scalar_tensor_tensor(o, o, col(g["gain"]), GD(g), ALU.mult, ALU.mult))
        if r == 1:
            differences(0, gated(2))
        st.go(1)
        dve.wait_ge(S("gated_rms"), r + 1)
        dve.reciprocal(SM[0:4, 256:512], SM[0:4, 0:256]).then_inc(S("gated_rsqrt"), 1)
        st.go(1)
        dve.wait_ge(S("gated_norm_spread"), r + 1)
        dve.tensor_tensor(o, o, pm[:, 1536:2560].rearrange("p (a t) -> p a t", a=4), ALU.mult).then_inc(S("gated_y_ready"), 1)
        if r != 1:
            y_low(r)

    def head_rows(h):
        return slice(64 * (h % 2), 64 * (h % 2) + 64), h // 2

    def moba_pe(pe, st):
        for h in range(8):
            rows, tile = head_rows(h)
            q, k = P[rows, MQ + tile, :], P[rows, MK + tile, :]
            if h >= 2:
                pe.wait_ge(S("moba_max"), 2 * (h - 1))
            for u in range(2):
                s = bank(h % 2)[:, u * 128:u * 128 + (u + 1) * 128]
                pe.matmul(s, q[:, u * 128:u * 128 + 128], k[:, 0:(u + 1) * 128], start=True, stop=False)
                pe.matmul(s, row_sel(8, h), C[0:8, CALIBI:CALIBI + (u + 1) * 128], start=False, stop=False)
                i = pe.matmul(s[:, u * 128:u * 128 + 128], CR[:, 0:128], CR[:, 256:384], start=False, stop=True)
            i.then_inc(S("moba_scores"), 1)
            st.go(1 if h in (3, 5, 7) else 0)
        pe.wait_ge(S("moba_max"), 16)
        for u in range(2):
            i = pe.matmul(bank(2)[0:8, u * 128:u * 128 + 128], SC[:, 72 + 8 * u:80 + 8 * u], ident, start=True, stop=True)
        i.then_inc(S("moba_max_rows"), 1)
        pe.wait_ge(S("moba_max_copied"), 1)
        for h in range(9):
            if h < 8:
                rows, tile = head_rows(h)
                q, k = P[rows, MQ + tile, :], P[rows, MK + tile, :]
                if h >= 2:
                    pe.wait_ge(S("moba_exp"), 2 * (h - 1))
                for v in range(2):
                    s = bank(h % 2)[:, 0:256] if v == 0 else bank(h % 2)[:, 256:384]
                    pe.matmul(s, k[:, v * 128:v * 128 + 128], q[:, v * 128:256], start=True, stop=False)
                    pe.matmul(s, row_sel(8, h), SM[0:8, v * 128:256], start=False, stop=False)
                    i = pe.matmul(s[:, 0:128], CR[:, 0:128], CR[:, 128:256], start=False, stop=True)
                i.then_inc(S("moba_scores_t"), 1)
                st.go(1 if h < 6 else 0)
            if h:
                moba_values(pe, h - 1)
        st.go(1)
        pe.wait_ge(S("moba_recip"), 1)
        pe.wait_ge(S("moba_o_copied"), 2)
        for h in range(8):
            rows, t = head_rows(h)
            i = pe.matmul(bank(t // 2)[rows, (t % 2) * 256:(t % 2) * 256 + 256], row_sel(8, h, 64), SM[0:8, 512:768],
                          start=True, stop=True)
        i.then_inc(S("moba_spread"), 1)

    def moba_values(pe, h):
        rows, tile = head_rows(h)
        w = words(4, (h % 2) * 384, 384)
        pe.wait_ge(S("moba_exp"), 2 * h + 2)
        pe.matmul(bank(2)[0:8, 0:256], head_of(8, h), w[:, 0:256], start=h == 0, stop=False)
        pe.matmul(bank(2)[0:8, 128:256], head_of(8, h), w[:, 256:384], start=False, stop=h == 7).then_inc(S("moba_den"), 1)
        o = bank(3 + tile // 2)[rows, (tile % 2) * 256:(tile % 2) * 256 + 256]
        pe.matmul(o, words(MV, h * 64, 64), w[:, 0:256], start=True, stop=False)
        pe.matmul(o[:, 128:256], words(MV + 2, h * 64, 64), w[:, 256:384], start=False, stop=True).then_inc(S("moba_o"), 1)

    def moba_act(act, st):
        st.go(2)
        for h in range(4):
            st.go(1 if h % 2 else 0)
        act.wait_ge(S("moba_max_rows"), 1)
        act.activation(SM[0:8, 0:256], bank(2)[0:8, 0:256], ACT.Copy).then_inc(S("moba_max_copied"), 1)
        for h in range(8):
            w = words(4, (h % 2) * 384, 384)
            act.wait_ge(S("moba_scores_t"), h + 1)
            if h >= 2:
                act.wait_ge(S("moba_o"), h - 1)
            for v in range(2):
                s = bank(h % 2)[:, 0:256] if v == 0 else bank(h % 2)[:, 256:384]
                act.activation(w[:, 0:256] if v == 0 else w[:, 256:384], s, ACT.Exp,
                               bias=C[:, CALCOL + v * 8 + h:CALCOL + v * 8 + h + 1]).then_inc(S("moba_exp"), 1)
            st.go(1 if h < 6 else 0)
        act.wait_ge(S("moba_o"), 8)
        for b in range(2):
            act.activation(P[:, 8 + 2 * b:10 + 2 * b, :], bank(3 + b).rearrange("p (a t) -> p a t", a=2), ACT.Copy)\
               .then_inc(S("moba_o_copied"), 1)
        st.go(1)
        act.wait_ge(S("moba_y"), 1)
        act.activation(Y[:, 16:20, :], P[:, 8:12, :], ACT.Copy).then_inc(S("moba_y_hi"), 1)
        act.wait_ge(S("pool_mm"), 1)
        for g in range(4):
            act.activation(P[:, g, :], pm[:, 1536 + g * 256:1792 + g * 256], ACT.Copy, scale=col("pool_scale", g))\
               .then_inc(S("pool_y"), 1)
        act.wait_ge(S("pool_y"), 4)
        act.activation(Y[:, 4:8, :], P[:, 0:4, :], ACT.Copy).then_inc(S("pool_y_hi"), 1)

    def moba_dve(dve, st):
        for h in range(8):
            dve.wait_ge(S("moba_scores"), h + 1)
            for u in range(2):
                dve.tensor_reduce(SC[:, 72 + 8 * u + h:73 + 8 * u + h], bank(h % 2)[:, u * 128:u * 128 + (u + 1) * 128],
                                  AX.X, ALU.max, negate=True).then_inc(S("moba_max"), 1)
            st.go(1 if h % 2 else 0)
        for g in range(4):
            u, a = P[:, PU + g, :], P[:, g, :]
            link(dve, dve.tensor_copy(a, u))
            for n in range(g + 1):
                src, dst = (P[:, g, :], P[:, 7, :]) if n % 2 == 0 else (P[:, 7, :], P[:, g, :])
                lag = 1 << n
                link(dve, dve.tensor_tensor(dst[:, lag:], src[:, lag:], src[:, :T - lag], ALU.add))
                link(dve, dve.tensor_copy(dst[:, :lag], src[:, :lag]))
            s = P[:, 7, :] if g % 2 == 0 else P[:, g, :]
            link(dve, dve.tensor_tensor(s[:, 0:16], s[:, 0:16], C[:, CINV + 16 * g:CINV + 16 * g + 16], ALU.mult))
            link(dve, dve.tensor_scalar(s[:, 16:], s[:, 16:], 1.0 / (2 << g), None, ALU.mult))
            dve.tensor_tensor(u, s, u, ALU.subtract).then_inc(S("pool_p"), 1)
            dve.wait_ge(S("pool_p"), g + 1)
            st.go(2 if g < 3 else 0)
        dve.wait_ge(S("moba_den"), 8)
        dve.reciprocal(SM[0:8, 512:768], bank(2)[0:8, 0:256]).then_inc(S("moba_recip"), 1)
        st.go(1)
        dve.wait_ge(S("moba_spread"), 1)
        o = P[:, 8:12, :]
        dve.tensor_tensor(o, o, pm[:, 0:1024].rearrange("p (a t) -> p a t", a=4), ALU.mult).then_inc(S("moba_y"), 1)
        dve.wait_ge(S("moba_y_hi"), 1)
        dve.tensor_tensor(Y[:, 24:28, :], o, Y[:, 16:20, :].bitcast(F32), ALU.subtract).then_inc(S("y1_ready"), 1)
        dve.wait_ge(S("pool_y_hi"), 1)
        dve.tensor_tensor(Y[:, 12:16, :], P[:, 0:4, :], Y[:, 4:8, :].bitcast(F32), ALU.subtract).then_inc(S("y1_ready"), 1)

    def pool_pe(pe, st):
        pe.wait_ge(S("pool_p"), 4)
        pe.wait_ge(S("moba_o_copied"), 2)
        for g in range(4):
            i = pe.matmul(pm[:, 1536 + g * 256:1792 + g * 256], PLW[:, g * 128:g * 128 + 128], P[:, PU + g, :], start=True, stop=True)
        i.then_inc(S("pool_mm"), 1)

    def rows_pe(pe, st):
        for j in range(2):
            for k in range(KT):
                i = pe.matmul(bank(4)[32:36, j * 256:j * 256 + 256], IFW[:, k * 8 + 4 * j:k * 8 + 4 * j + 4], HF[:, k, :], start=k == 0, stop=k == KT - 1)
        for k in range(KT):
            i = pe.matmul(bank(3)[0:16, 0:256], DTW[:, k * 16:k * 16 + 16], HF[:, k, :], start=k == 0, stop=k == KT - 1)
        i.then_inc(S("rows_projected"), 1)
        st.go(3)
        pe.wait_ge(S("rows_ready"), 1)
        for v in range(2):
            at = slice(v * 128, v * 128 + 128)
            pe.matmul(bank(2)[:, v * 4:v * 4 + 4], LR[:, 2, at], C[32:36, CIDENT + 32:CIDENT + 36], start=True, stop=True)
            pe.matmul(bank(3)[:, v * 16:16 + v * 16], DR[:, 2, at], C[0:16, CIDENT:CIDENT + 16], start=True, stop=True)
            i = pe.matmul(bank(3)[:, 32 + v * 16:48 + v * 16], DR[:, 0, at], C[0:16, CIDENT:CIDENT + 16], start=True, stop=True)
        i.then_inc(S("columns_ready"), 1)

    def rows_act(act, st):
        act.wait_ge(S("rows_projected"), 1)
        act.activation(LR[:, 0, :], bank(4)[32:36, 0:256], ACT.Identity, bias=RW[32:36, 0:1]).then_inc(S("rows_biased"), 1)
        act.activation(LR[:, 1, :], bank(4)[32:36, 256:512], ACT.Identity, bias=RW[32:36, 1:2]).then_inc(S("rows_biased"), 1)
        act.activation(DR[:, 0, :], bank(3)[0:16, 0:256], ACT.Identity, bias=RW[0:16, 2:3]).then_inc(S("rows_biased"), 1)
        act.activation(RW[0:16, 4:5], RW[0:16, 3:4], ACT.Exp).then_inc(S("rows_biased"), 1)
        st.go(1)
        act.wait_ge(S("rows_abs"), 2)
        link(act, act.activation(LR[:, 4, :], LR[:, 4, :], ACT.Exp))
        link(act, act.activation(DR[:, 3, :], DR[:, 3, :], ACT.Exp))
        act.activation(LR[:, 4, :], LR[:, 4, :], ACT.Ln, bias=one[32:36]).then_inc(S("rows_log"), 1)
        act.activation(DR[:, 3, :], DR[:, 3, :], ACT.Ln, bias=one[0:16]).then_inc(S("rows_log"), 1)
        st.go(1)
        act.wait_ge(S("columns_ready"), 1)
        act.activation(SC[:, 0:8], bank(2)[:, 0:8], ACT.Copy).then_inc(S("columns_copied"), 1)
        act.activation(SC[:, 8:72], bank(3)[:, 0:64], ACT.Copy).then_inc(S("columns_copied"), 1)
        act.activation(LR[:, 5, :], LR[:, 5, :], ACT.Exp, scale=-1.0).then_inc(S("exp_minus_m"), 1)

    def rows_dve(dve, st):
        dve.wait_ge(S("rows_biased"), 4)
        dve.scalar_tensor_tensor(LR[:, 4, :], LR[:, 1, :], -1.0, LR[:, 1, :], ALU.mult, ALU.min).then_inc(S("rows_abs"), 1)
        dve.scalar_tensor_tensor(DR[:, 3, :], DR[:, 0, :], -1.0, DR[:, 0, :], ALU.mult, ALU.min).then_inc(S("rows_abs"), 1)
        st.go(1)
        dve.wait_ge(S("rows_log"), 2)
        link(dve, dve.scalar_tensor_tensor(LR[:, 4, :], LR[:, 1, :], 0.0, LR[:, 4, :], ALU.min, ALU.subtract))
        link(dve, dve.tensor_tensor_scan(LR[:, 1, :], C[32:36, CONES:CONES + 256], LR[:, 4, :], 0.0, ALU.mult, ALU.add))
        link(dve, dve.tensor_tensor(LR[:, 2, :], LR[:, 0, :], LR[:, 1, :], ALU.subtract))
        link(dve, dve.memset(LR[:, 0, :], 0.0))
        link(dve, dve.tensor_tensor_scan(LR[:, 3, :], LR[:, 2, :], LR[:, 0, :], 0.0, ALU.max, ALU.add))
        link(dve, dve.tensor_tensor(LR[:, 5, :], LR[:, 1, :], LR[:, 3, :], ALU.add))
        link(dve, dve.tensor_scalar(LR[:, 3, :], LR[:, 3, :], -1.0, None, ALU.mult))
        link(dve, dve.scalar_tensor_tensor(DR[:, 0, :], DR[:, 0, :], 0.0, DR[:, 3, :], ALU.max, ALU.add))
        link(dve, dve.tensor_scalar(DR[:, 3, :], DR[:, 0, :], RW[0:16, 4:5], -1.0, ALU.mult, ALU.mult))
        link(dve, dve.tensor_tensor_scan(DR[:, 1, :], C[0:16, CONES:CONES + 256], DR[:, 3, :], 0.0, ALU.mult, ALU.add))
        dve.tensor_scalar(DR[:, 2, :], DR[:, 1, :], -1.0, None, ALU.mult).then_inc(S("rows_ready"), 1)
        st.go(1)

    def decay_matmuls(pe, dst, rows, h, src, at=0):
        for v in range(2):
            s = dst[:, 0:256] if v == 0 else dst[:, 256:384]
            pe.matmul(s, row_sel(rows, h, at=at), src[:, v * 128:256], start=True, stop=False)
            i = pe.matmul(s[:, 0:128], CR[:, 0:128], CR[:, 128:256], start=False, stop=True)
        return i

    EW = 16

    def mlstm_pe(pe, st):
        for h in range(5):
            if h < 4:
                if h == 0:
                    pe.wait_ge(S("lm_silu"), 2)
                    pe.wait_ge(S("columns_copied"), 2)
                else:
                    pe.wait_ge(S("lm_w"), 2 * h)
                q, k = P[:, LQ + h, :], P[:, LK + h, :]
                pe.matmul(bank(0)[:, 0:256], k[:, 0:128], q, start=True, stop=True)
                pe.matmul(bank(0)[:, 256:384], k[:, 128:256], q[:, 128:256], start=True, stop=True)
                decay_matmuls(pe, bank(1), 4, h, LR[:, 3, :], 32).then_inc(S("lm_scores"), 1)
                st.go(1)
            if h:
                n = h - 1
                w = words(EW, 768 + (n % 2) * 384, 384)
                pe.wait_ge(S("lm_w"), 2 * n + 2)
                if n >= 2:
                    pe.wait_ge(S("lm_h_copied"), 2 * (n - 1))
                pe.matmul(bank(2)[32:36, 0:256], head_of(4, n), w[:, 0:256], start=n == 0, stop=False, skip_group_check=True)
                pe.matmul(bank(2)[32:36, 128:256], head_of(4, n), w[:, 256:384], start=False, stop=n == 3, skip_group_check=True)
                for j in range(2):
                    o = bank(3 + n % 2)[:, j * 256:j * 256 + 256]
                    at = n * 256 + j * 128
                    pe.matmul(o, words(LV, at, 128), w[:, 0:256], start=True, stop=False)
                    i = pe.matmul(o[:, 128:256], words(LV + 4, at, 128), w[:, 256:384], start=False, stop=True)
                i.then_inc(S("lm_h"), 1)
                st.go(1)
                pe.wait_ge(S("lm_h_copied"), 2 * n + 2)
                for j in range(2):
                    i = pe.matmul(bank(2)[32:36, 256:512], head_of(4, n), P[:, EW + 6 + j, :], start=False,
                                  stop=n == 3 and j == 1, skip_group_check=True)
                i.then_inc(S("lm_sums"), 1)
        st.go(1)
        pe.wait_ge(S("lm_comb"), 1)
        for h in range(4):
            i = pe.matmul(pm[:, h * 256:h * 256 + 256], row_sel(4, h, at=32), LR[:, 2, :], start=True, stop=True)
        i.then_inc(S("lm_spread"), 1)

    def mlstm_act(act, st):
        for b in range(2):
            if b == 0:
                act.wait_ge(S("gated_y_done"), 3)
            act.activation(HF[:, 4 * b:4 * b + 4, :], P[:, LQ + 4 * b:LQ + 4 * b + 4, :], ACT.Tanh, scale=0.5).then_inc(S("lm_tanh"), 1)
        for h in range(4):
            st.go(1)
            e = words(EW, (h % 2) * 384, 384)
            act.wait_ge(S("lm_scores"), h + 1)
            if h >= 2:
                act.wait_ge(S("lm_w"), 2 * (h - 1))
            for v in range(2):
                at = slice(0, 256) if v == 0 else slice(256, 384)
                act.activation(e[:, at], bank(1)[:, at], ACT.Exp, bias=SC[:, v * 4 + h:v * 4 + h + 1]).then_inc(S("lm_exp"), 1)
            st.go(1)
            act.wait_ge(S("lm_h"), h + 1)
            if h == 0:
                act.wait_ge(S("lm_silu"), 2)
            else:
                act.wait_ge(S("lm_sums"), h)
            o = bank(3 + h % 2).rearrange("p (a t) -> p a t", a=2)
            act.activation(HF[:, 2 * h:2 * h + 2, :], o, ACT.Copy).then_inc(S("lm_h_copied"), 1)
            act.activation(P[:, EW + 6:EW + 8, :], o, ACT.Square).then_inc(S("lm_h_copied"), 1)
        load_sqrt(act)
        act.wait_ge(S("lm_ms"), 1)
        act.activation(LR[:, 1, :], LR[:, 1, :], ACT.Sqrt, bias=eps4[32:36], scale=4.0 / 256).then_inc(S("lm_rms"), 1)
        st.go(W_MLSTM[0] + LAST_O + 2 - st.p)
        for b in range(2):
            act.wait_ge(S("lm_y"), b + 1)
            act.activation(Y[:, 16 + 4 * b:20 + 4 * b, :], HF[:, 4 * b:4 * b + 4, :], ACT.Copy).then_inc(S("lm_y_hi"), 1)
            st.go(1)

    def mlstm_dve(dve, st):
        for b in range(2):
            dve.wait_ge(S("lm_tanh"), b + 1)
            x = P[:, LQ + 4 * b:LQ + 4 * b + 4, :]
            dve.scalar_tensor_tensor(x, HF[:, 4 * b:4 * b + 4, :], 1.0, x, ALU.add, ALU.mult).then_inc(S("lm_silu"), 1)
        for h in range(4):
            st.go(1)
            e, w = words(EW, (h % 2) * 384, 384), words(EW, 768 + (h % 2) * 384, 384)
            if h >= 2:
                dve.wait_ge(S("lm_h"), h - 1)
            for v in range(2):
                at = slice(0, 256) if v == 0 else slice(256, 384)
                dve.wait_ge(S("lm_exp"), 2 * h + v + 1)
                dve.scalar_tensor_tensor(w[:, at], bank(0)[:, at], 0.25 * 128 ** -0.5, e[:, at], ALU.mult, ALU.mult).then_inc(S("lm_w"), 1)
            st.go(1)
        dve.wait_ge(S("lm_sums"), 4)
        dve.wait_ge(S("exp_minus_m"), 1)
        a, b, c = (LR[:, n, :] for n in range(3))
        link(dve, dve.tensor_copy(a, bank(2)[32:36, 0:256]))
        link(dve, dve.scalar_tensor_tensor(a, a, -1.0, a, ALU.mult, ALU.max))
        link(dve, dve.tensor_tensor(a, a, LR[:, 5, :], ALU.max))
        link(dve, dve.reciprocal(a, a))
        link(dve, dve.tensor_tensor(b, bank(2)[32:36, 256:512], a, ALU.mult))
        dve.tensor_tensor(b, b, a, ALU.mult).then_inc(S("lm_ms"), 1)
        dve.wait_ge(S("lm_rms"), 1)
        link(dve, dve.reciprocal(c, b))
        dve.tensor_tensor(c, c, a, ALU.mult).then_inc(S("lm_comb"), 1)
        st.go(1)
        dve.wait_ge(S("lm_spread"), 1)
        wait_evac(dve, W_MLSTM[0] + LAST_O, ("act_taken",))
        for h in range(4):
            for j in range(2):
                t = HF[:, 2 * h + j, :]
                link(dve, dve.scalar_tensor_tensor(t, t, col("ml_norm", j), pm[:, h * 256:h * 256 + 256], ALU.mult, ALU.mult))
            if h % 2:
                b = h // 2
                t = HF[:, 4 * b:4 * b + 4, :]
                dve.scalar_tensor_tensor(t, P[:, LO + 4 * b:LO + 4 * b + 4, :], 1.0, t, ALU.add, ALU.mult).then_inc(S("lm_y"), 1)
                if b == 0:
                    st.go(1)
        st.go(1)
        for b in range(2):
            dve.wait_ge(S("lm_y_hi"), b + 1)
            dve.tensor_tensor(Y[:, 24 + 4 * b:28 + 4 * b, :], HF[:, 4 * b:4 * b + 4, :], Y[:, 16 + 4 * b:20 + 4 * b, :].bitcast(F32),
                              ALU.subtract).then_inc(S("lm_y_done"), 1)

    TMP, CB, MW = 24, 48, 8

    def cb_words(g):
        return words(CB, g * 384, 384) if g < 3 else words(MW, 1536, 384)

    def ssd_pe(pe, st):
        pe.wait_ge(S("mb_silu"), 4)
        for g in range(4):
            if g >= 2:
                pe.wait_ge(S("mb_cb"), g - 1)
            b = bank(g % 2)
            pe.matmul(b[:, 0:256], P[:, XB + g, 0:128], P[:, XC + g, :], start=True, stop=True)
            pe.matmul(b[:, 256:384], P[:, XB + g, 128:256], P[:, XC + g, 128:256], start=True, stop=True).then_inc(S("mb_bc"), 1)
        for n in range(4):
            v, q = divmod(n, 2)
            if n >= 2:
                pe.wait_ge(S("mb_xt"), n - 1)
            for j in range(4):
                i = pe.matmul(bank(2 + n % 2)[:, j * 128:j * 128 + 128], P[:, XS + 4 * q + j, v * 128:v * 128 + 128], ident, start=True, stop=True)
            i.then_inc(S("mb_xtp"), 1)
        pe.wait_ge(S("mb_xt"), 4)
        pe.wait_ge(S("mb_cb"), 4)
        for h in range(17):
            if h < 16:
                if h >= 2:
                    pe.wait_ge(S("mb_exp"), 2 * (h - 1))
                decay_matmuls(pe, bank(h % 2), 16, h, DR[:, 1, :]).then_inc(S("mb_decay"), 1)
                st.go(1)
            if h:
                n = h - 1
                w = words(MW, 768 + (n % 2) * 384, 384)
                pe.wait_ge(S("mb_w"), 2 * n + 2)
                if n >= 4 and n % 2 == 0:
                    pe.wait_ge(S("mb_y"), n // 2 - 1)
                o = bank(2 + (n // 2) % 2)[64 * (n % 2):64 * (n % 2) + 64, 0:256]
                pe.matmul(o, words(TMP, n * 64, 64), w[:, 0:256], start=True, stop=False)
                pe.matmul(o[:, 128:256], words(TMP + 4, n * 64, 64), w[:, 256:384], start=False, stop=True).then_inc(S("mb_o"), 1)
        for t in range(8):
            if t % 4 == 0:
                pe.wait_ge(S("mb_squares"), t // 4 + 1)
            i = pe.matmul(bank(4)[0:4, 0:256], head_of(4, t // 2), P[:, TMP + t, :], start=t == 0, stop=t == 7)
        i.then_inc(S("mb_sums"), 1)
        st.go(1)
        pe.wait_ge(S("mb_rsqrt"), 1)
        for g in range(4):
            i = pe.matmul(pm[:, g * 256:g * 256 + 256], row_sel(4, g), SM[0:4, 256:512], start=True, stop=True)
        i.then_inc(S("mb_spread"), 1)

    def ssd_act(act, st):
        for n, at in enumerate((XB, XS, XZ)):
            if n == 0:
                act.wait_ge(S("lm_y_done"), 2)
            else:
                act.wait_ge(S("mb_silu"), 2 * n)
            for b in range(2):
                act.activation(P[:, TMP + 4 * b:TMP + 4 * b + 4, :], P[:, at + 4 * b:at + 4 * b + 4, :], ACT.Tanh, scale=0.5).then_inc(S("mb_tanh"), 1)
        for g in range(4):
            act.wait_ge(S("mb_bc"), g + 1)
            act.activation(cb_words(g), bank(g % 2)[:, 0:384], ACT.Copy, scale=0.25).then_inc(S("mb_cb"), 1)
        act.wait_ge(S("mb_silu"), 6)
        for n in range(4):
            v, q = divmod(n, 2)
            act.wait_ge(S("mb_xtp"), n + 1)
            act.activation(words(TMP, v * 1024 + q * 512, 512), bank(2 + n % 2), ACT.Copy).then_inc(S("mb_xt"), 1)
        for h in range(16):
            e = words(MW, (h % 2) * 384, 384)
            act.wait_ge(S("mb_decay"), h + 1)
            if h >= 2:
                act.wait_ge(S("mb_w"), 2 * (h - 1))
            for v in range(2):
                at = slice(0, 256) if v == 0 else slice(256, 384)
                act.activation(e[:, at], bank(h % 2)[:, at], ACT.Exp, bias=SC[:, 8 + v * 16 + h:9 + v * 16 + h]).then_inc(S("mb_exp"), 1)
            st.go(1)
        for b in range(2):
            act.wait_ge(S("mb_u"), b + 1)
            act.activation(P[:, TMP + 4 * b:TMP + 4 * b + 4, :], P[:, XS + 4 * b:XS + 4 * b + 4, :], ACT.Square).then_inc(S("mb_squares"), 1)
        load_sqrt(act)
        act.wait_ge(S("mb_sums"), 1)
        act.activation(SM[0:4, 0:256], bank(4)[0:4, 0:256], ACT.Sqrt, bias=eps16[0:4], scale=1.0 / 256).then_inc(S("mb_rms"), 1)
        st.go(1)
        act.wait_ge(pair_done, Y0_READ)
        for b in range(2):
            act.wait_ge(S("mb_yn"), b + 1)
            act.activation(Y[:, 4 * b:4 * b + 4, :], P[:, XS + 4 * b:XS + 4 * b + 4, :], ACT.Copy).then_inc(S("mb_y_hi"), 1)
            st.go(1)

    def ssd_dve(dve, st):
        for n, at in enumerate((XB, XS, XZ)):
            for b in range(2):
                dve.wait_ge(S("mb_tanh"), 2 * n + b + 1)
                x = P[:, at + 4 * b:at + 4 * b + 4, :]
                dve.scalar_tensor_tensor(x, P[:, TMP + 4 * b:TMP + 4 * b + 4, :], 1.0, x, ALU.add, ALU.mult).then_inc(S("mb_silu"), 1)
        for h in range(17):
            if h < 16:
                e, w = words(MW, (h % 2) * 384, 384), words(MW, 768 + (h % 2) * 384, 384)
                if h == 0:
                    dve.wait_ge(S("mb_cb"), 4)
                if h >= 2:
                    dve.wait_ge(S("mb_o"), h - 1)
                for v in range(2):
                    at = slice(0, 256) if v == 0 else slice(256, 384)
                    dve.wait_ge(S("mb_exp"), 2 * h + v + 1)
                    dve.scalar_tensor_tensor(w[:, at], e[:, at], SC[:, 40 + v * 16 + h:41 + v * 16 + h],
                                             cb_words(h // 4)[:, at], ALU.mult, ALU.mult).then_inc(S("mb_w"), 1)
                st.go(1)
            if h and h % 2 == 0:
                t = h // 2 - 1
                dve.wait_ge(S("mb_o"), h)
                x = P[:, XS + t, :]
                dve.scalar_tensor_tensor(x, x, col("mb_d", t), bank(2 + t % 2)[:, 0:256], ALU.mult, ALU.add).then_inc(S("mb_y"), 1)
        dve.wait_ge(S("mb_y"), 8)
        for b in range(2):
            x = P[:, XS + 4 * b:XS + 4 * b + 4, :]
            dve.tensor_tensor(x, x, P[:, XZ + 4 * b:XZ + 4 * b + 4, :], ALU.mult).then_inc(S("mb_u"), 1)
        dve.wait_ge(S("mb_rms"), 1)
        dve.reciprocal(SM[0:4, 256:512], SM[0:4, 0:256]).then_inc(S("mb_rsqrt"), 1)
        st.go(1)
        dve.wait_ge(S("mb_spread"), 1)
        for t in range(8):
            x = P[:, XS + t, :]
            i = dve.scalar_tensor_tensor(x, x, col("mb_norm", t), pm[:, (t // 2) * 256:(t // 2) * 256 + 256], ALU.mult, ALU.mult)
            if t % 4 == 3:
                i.then_inc(S("mb_yn"), 1)
            else:
                link(dve, i)
        st.go(1)
        dve.wait_ge(S("mb_yn"), 2)
        for b in range(2):
            dve.wait_ge(S("mb_y_hi"), b + 1)
            dve.tensor_tensor(Y[:, 8 + 4 * b:12 + 4 * b, :], P[:, XS + 4 * b:XS + 4 * b + 4, :], Y[:, 4 * b:4 * b + 4, :].bitcast(F32),
                              ALU.subtract).then_inc(S("mb_y_done"), 1)

    F0 = [FFN1, FFN2]

    def up_pe(pe, b, p, slot, g, rewrite=None):
        pe.wait_ge(lo_ready, p + 1)
        if not (isinstance(g, int) and g < 2):
            pe.wait_ge(S("up_taken" if b else "up_product"), g - 1)
        if rewrite is not None:
            first_pair(pe, slot, rewrite)
            return
        for half in range(2):
            for k in range(KT):
                at = k * 256 + half * 128
                done = three_passes(pe, pp[slot][:, half * 256:half * 256 + 256], [u[:, slot, at:at + 128] for u in (whi, wlo)],
                                    [u[:, k, :] for u in (XH, XL)], k == 0, k == KT - 1)
        done.then_inc(pair_done, 1)

    def down_pe(pe, b, p, slot, j, parity):
        pe.wait_ge(lo_ready, p + 1)
        first = isinstance(j, int) and j == 0
        last = isinstance(j, int) and j == FT // 2 - 1
        if last:
            for kk in range(2):
                pe.wait_ge(S("hidden_ready"), FT * b + FT - 1 + kk)
                for m in range(KT):
                    at = kk * 1024 + m * 128
                    for n, (a, part) in enumerate(((whi, 0), (whi, 1), (wlo, 0))):
                        done = pe.matmul(pm[:, 512 + m * 256:768 + m * 256], a[:, slot, at:at + 128],
                                         Y[:, 4 * part + 2 * parity + kk, :], start=False, stop=kk == 1 and n == 2,
                                         skip_group_check=True)
                    if kk == 1 and m in (1, 3, 5):
                        done.then_inc(S("acc_done"), 1)
            done.then_inc(pair_done, 1)
            return
        for kk in range(2):
            pe.wait_ge(S("hidden_ready"), 2 * j + (FT * b + 1 + kk))
            y = [Y[:, 4 * part + 2 * parity + kk, :] for part in range(2)]
            for m in range(KT):
                at = kk * 1024 + m * 128
                for n, (a, c) in enumerate(((whi, 0), (whi, 1), (wlo, 0))):
                    done = pe.matmul(pm[:, 512 + m * 256:768 + m * 256], a[:, slot, at:at + 128], y[c],
                                     start=first and kk == 0 and n == 0 and m % 2 == 0, stop=False, skip_group_check=True)
        done.then_inc(pair_done, 1)

    def ffn_pe(pe, b, rewrite):
        f = F0[b]
        for g in range(2):
            up_pe(pe, b, f + g, (f + g) % RING, g, rewrite if g == 0 else None)
        up_pe(pe, b, f + 2, (f + 2) % RING, 2)
        up_pe(pe, b, f + 3, (f + 3) % RING, 3)
        down_pe(pe, b, f + 4, (f + 4) % RING, 0, 0)
        with pe.Fori(0, 4) as i:
            p, s = i * 6 + (f + 5), f + 5
            up_pe(pe, b, p, s % RING, i * 4 + 4)
            up_pe(pe, b, p + 1, (s + 1) % RING, i * 4 + 5)
            down_pe(pe, b, p + 2, (s + 2) % RING, i * 2 + 1, 1)
            up_pe(pe, b, p + 3, (s + 3) % RING, i * 4 + 6)
            up_pe(pe, b, p + 4, (s + 4) % RING, i * 4 + 7)
            down_pe(pe, b, p + 5, (s + 5) % RING, i * 2 + 2, 0)
        up_pe(pe, b, f + 29, (f + 29) % RING, 20)
        up_pe(pe, b, f + 30, (f + 30) % RING, 21)
        down_pe(pe, b, f + 31, (f + 31) % RING, 9, 1)
        down_pe(pe, b, f + 32, (f + 32) % RING, 10, 0)

    def temps(par):
        return [P[:, 16 + 4 * par + n, :] for n in range(4)]

    def fcol(name, k):
        return PC[:, COLS[name] + k:COLS[name] + k + 1] if isinstance(k, int) else PC[:, bass.ds(k + COLS[name], 1)]

    def act_turn(act, b, p, slot, turn, prev, late):
        if prev is not None:
            g, ps_slot, par = prev
            n = g + (FT * b + 1)
            th, pr, cg, cu = temps(par % 2)
            gate, value = pp[ps_slot][:, 0:256], pp[ps_slot][:, 256:512]
            act.wait_ge(pair_done, p)
            if b == 0:
                act.activation(th, gate, ACT.Tanh, scale=0.5).then_inc(S("up_tanh"), 1)
            else:
                act.activation(cg, gate, ACT.Identity, bias=fcol("ffn_conv_b", g), scale=fcol("ffn_conv_w", g + 88)).then_inc(S("up_conv"), 1)
                act.activation(cu, value, ACT.Identity, bias=fcol("ffn_conv_b", g + 22), scale=fcol("ffn_conv_w", g + 110)).then_inc(S("up_conv"), 1)
        if turn is not None:
            split_hi(act, p + 2, slot, turn)
        if prev is not None:
            if b:
                act.wait_ge(S("up_taps"), 3 * g + 3)
                act.activation(th, cg, ACT.Tanh, scale=0.5).then_inc(S("up_tanh"), 1)
            act.wait_ge(S("up_product"), n)
            act.activation(Y[:, par, :], pr, ACT.Copy).then_inc(S("hidden_hi"), 1)

    def dve_turn(dve, b, p, slot, turn, prev, late):
        if prev is not None:
            g, ps_slot, par = prev
            n = g + (FT * b + 1)
            th, pr, cg, cu = temps(par % 2)
            gate, value = pp[ps_slot][:, 0:256], pp[ps_slot][:, 256:512]
            if b:
                dve.wait_ge(S("up_conv"), 2 * g + 2)
                for k in (1, 0):
                    lag = 2 - k
                    for c, src, off in ((cg, gate, 0), (cu, value, 22)):
                        if k == 0:
                            dve.wait_ge(S("up_taps"), 3 * g + (2 if off else 1))
                        i = dve.scalar_tensor_tensor(c[:, lag:], src[:, 0:256 - lag], fcol("ffn_conv_w", g + (44 * k + off)),
                                                     c[:, lag:], ALU.mult, ALU.add)
                        i.then_inc(S("up_taken" if k == 0 and off else "up_taps"), 1)
        if late is not None:
            g2, par2 = late
            dve.wait_ge(S("hidden_hi"), g2 + (FT * b + 1))
            dve.tensor_tensor(Y[:, 4 + par2, :], temps(par2 % 2)[1], Y[:, par2, :].bitcast(F32), ALU.subtract)\
               .then_inc(S("hidden_ready"), 1)
        if turn is not None:
            split_lo(dve, p + 2, slot)
        if prev is not None:
            dve.wait_ge(S("up_tanh"), n)
            if b:
                dve.wait_ge(S("up_taken"), g + 1)
            dve.scalar_tensor_tensor(pr, th, 1.0, cg if b else gate, ALU.add, ALU.mult).then_inc(S("up_gated"), 1)
            dve.wait_ge(S("up_gated"), n)
            dve.scalar_tensor_tensor(pr, pr, 0.5, cu if b else value, ALU.mult, ALU.mult).then_inc(S("up_product"), 1)

    def ffn_side(eng, b, turn_fn):
        f = F0[b]

        def turn(n, g=None, late=None):
            at = f + n + 2
            turn_fn(eng, b, f + n, at % RING, at // RING if at < NPAIRS else None,
                    None if g is None else (g, (f + n - 1) % RING, g % 4), None if late is None else (late, late % 4))

        turn(0)
        turn(1, 0)
        turn(2, 1, 0)
        turn(3, 2, 1)
        turn(4, 3, 2)
        with eng.Fori(0, 4) as i:
            for j, (g, late) in enumerate(((None, 3), (4, None), (5, 4), (None, 5), (6, None), (7, 6))):
                n = 5 + j
                at = f + n + 2
                turn_fn(eng, b, i * 6 + (f + n), at % RING, i * 2 + at // RING,
                        None if g is None else (i * 4 + g, (f + n - 1) % RING, g % 4),
                        None if late is None else (i * 4 + late, late % 4))
        turn(29, None, 19)
        turn(30, 20)
        turn(31, 21, 20)
        turn(32, None, 21)

    @block.tensor
    def _(pe):
        st = Stream(pe, "pe")
        pe.wait_ge(S("consts_loaded"), 16)
        norm_pe(pe, 0)
        st.window(*W_START, 0)
        st.go(1)
        pe.wait_ge(S("tables_loaded"), 16)
        for w in ("G1W", "G2W", "PLW", "IFW", "DTW"):
            pe.wait_ge(S(f"loaded_{w}"), 16)
        for k in range(KT):
            i = pe.matmul(bank(4)[0:16, 0:256], G1W[:, k * 16:k * 16 + 16], HF[:, k, :], start=k == 0, stop=k == KT - 1)
        i.then_inc(S("g1_ready"), 1)
        st.finish()
        st.window(*W_GLA)
        wait_evac(pe, W_GLA[0] - 1)
        gated_pe(pe, 0, st)
        st.finish()
        st.window(*W_MOBA)
        st.go(1)
        wait_evac(pe, W_MOBA[0] - 1)
        pe.wait_ge(S("tables_loaded"), 16)
        pe.wait_ge(S("masks_rounded"), 2)
        moba_pe(pe, st)
        pool_pe(pe, st)
        st.finish()
        st.window(*W_BRANCH)
        pe.wait_ge(S("gated_y_done"), 1)
        pe.wait_ge(S("y1_ready"), 2)
        st.finish()
        st.window(*W_OUT, 1)
        st.finish()
        norm_pe(pe, 1)
        norm_pe(pe, 2)
        ffn_pe(pe, 0, 2)
        norm_pe(pe, 3)
        norm_pe(pe, 4)
        st.p = BLK2
        st.window(*W_ROWS, 3)
        st.go(1)
        rows_pe(pe, st)
        st.finish()
        st.window(*W_HGRN)
        st.go(1)
        wait_evac(pe, W_HGRN[0] - 1)
        gated_pe(pe, 1, st)
        gated_pe(pe, 2, st)
        st.finish()
        st.window(*W_MLSTM)
        st.go(1)
        wait_evac(pe, W_MLSTM[0] - 1)
        mlstm_pe(pe, st)
        st.finish()
        st.window(*W_SSD)
        st.go(1)
        wait_evac(pe, W_SSD[0] - 1)
        pe.wait_ge(S("gated_y_done"), 3)
        pe.wait_ge(S("lm_y_done"), 2)
        ssd_pe(pe, st)
        st.finish()
        st.window(*W_BRANCH2)
        pe.wait_ge(S("mb_y_done"), 2)
        st.finish()
        st.window(*W_OUT2, 4)
        st.finish()
        norm_pe(pe, 5)
        ffn_pe(pe, 1, 5)
        norm_pe(pe, 6)

    @block.scalar
    def _(act):
        st = Stream(act, "act")
        act.wait_ge(S("x_loaded"), 16)
        act.wait_ge(S("cols_loaded"), 16)
        act.wait_ge(S("scalars_set"), 4)
        norm_act(act, 0, X, 0, between=st.start)
        act.wait_ge(S("g1_ready"), 1)
        act.activation(SM[0:16, 0:256], bank(4)[0:16, 0:256], ACT.Copy).then_inc(S("g1_copied"), 1)
        st.window(*W_START)
        st.finish()
        st.window(*W_GLA)
        wait_evac(act, W_GLA[0] - 1)
        act.wait_ge(S("tables_loaded"), 16)
        act.wait_ge(S("masks_loaded"), 16)
        act.activation(CR[:, 0:128], C[:, CIDENT:CIDENT + 128], ACT.Copy).then_inc(S("masks_rounded"), 1)
        act.activation(CR[:, 128:384], P[:, MASKS, :], ACT.Copy).then_inc(S("masks_rounded"), 1)
        gated_start_act(act, 0, st)
        gated_act(act, 0, st)
        st.finish()
        st.window(*W_MOBA)
        wait_evac(act, W_MOBA[0] - 1)
        moba_act(act, st)
        st.finish()
        st.window(*W_BRANCH)
        st.finish()
        mix_act(act, 1)
        st.window(*W_OUT)
        st.finish()
        wait_evac(act, FFN1 - 1)
        norm_act(act, 1, P[:, OUT:OUT + 8, :], None)
        norm_act(act, 2, X, 1, updated=0)
        ffn_side(act, 0, act_turn)
        norm_act(act, 3, None, None, first=True)
        norm_act(act, 4, X, 2, updated=8)
        st.p = BLK2
        st.window(*W_ROWS)
        st.go(1)
        rows_act(act, st)
        st.go(BLK2 + 9 - st.p)
        wait_evac(act, BLK2 + 7)
        gated_start_act(act, 1, st)
        gated_start_act(act, 2, st)
        st.finish()
        st.window(*W_HGRN)
        gated_act(act, 1, st)
        gated_act(act, 2, st)
        st.finish()
        st.window(*W_MLSTM)
        wait_evac(act, W_MLSTM[0] - 1)
        mlstm_act(act, st)
        st.finish()
        st.window(*W_SSD)
        wait_evac(act, W_SSD[0] - 1)
        ssd_act(act, st)
        st.finish()
        st.window(*W_BRANCH2)
        st.finish()
        mix_act(act, 2)
        st.window(*W_OUT2)
        st.finish()
        wait_evac(act, FFN2 - 1)
        norm_act(act, 5, X, 3)
        ffn_side(act, 1, act_turn)
        norm_act(act, 6, X, None, updated=0, counter="x_final")

    @block.vector
    def _(dve):
        st = Stream(dve, "dve")
        for n, v in ((127, EPS), (126, 4 * EPS), (125, 1.0), (124, 16 * EPS)):
            dve.memset(SC[:, n:n + 1], v).then_inc(S("scalars_set"), 1)
        dve.wait_ge(S("consts_loaded"), 16)
        dve.wait_ge(S("cols_loaded"), 16)
        dve.wait_ge(S("x_loaded"), 16)
        st.start()
        norm_dve(dve, 0, X, "norm_mix_pre", 0)
        st.window(*W_START)
        st.finish()
        st.window(*W_GLA)
        wait_evac(dve, W_GLA[0] - 1)
        dve.wait_ge(S("tables_loaded"), 16)
        gated_start_dve(dve, 0, st)
        gated_dve(dve, 0, st)
        st.finish()
        st.window(*W_MOBA)
        wait_evac(dve, W_MOBA[0] - 1)
        moba_dve(dve, st)
        st.finish()
        st.window(*W_BRANCH)
        wait_evac(dve, W_BRANCH[0] - 1)
        st.finish()
        lo_parts(dve, 4 * mixes[1], 0.5)
        st.window(*W_OUT)
        st.finish()
        norm_dve(dve, 1, P[:, OUT:OUT + 8, :], "norm_mix_post", None)
        norm_dve(dve, 2, X, "norm_ffn_pre", 1)
        ffn_side(dve, 0, dve_turn)
        dve.wait_ge(S("ffn_out"), 4)
        norm_dve(dve, 3, P[:, OUT:OUT + 8, :], "norm_ffn_post", None)
        norm_dve(dve, 4, X, "norm1_g", 2)
        st.p = BLK2
        st.window(*W_ROWS)
        dve.wait_ge(S("loaded_RW"), 16)
        st.go(1)
        rows_dve(dve, st)
        st.go(BLK2 + 9 - st.p)
        wait_evac(dve, BLK2 + 7)
        gated_start_dve(dve, 1, st)
        gated_start_dve(dve, 2, st)
        st.finish()
        st.window(*W_HGRN)
        gated_dve(dve, 1, st)
        gated_dve(dve, 2, st)
        st.finish()
        st.window(*W_MLSTM)
        wait_evac(dve, W_MLSTM[0] - 1)
        mlstm_dve(dve, st)
        st.finish()
        st.window(*W_SSD)
        wait_evac(dve, W_SSD[0] - 1)
        ssd_dve(dve, st)
        st.finish()
        st.window(*W_BRANCH2)
        st.finish()
        lo_parts(dve, 4 * mixes[2], 0.5)
        st.window(*W_OUT2)
        st.finish()
        norm_dve(dve, 5, X, "norm2_g", 3)
        ffn_side(dve, 1, dve_turn)
        for q in range(4):
            wait_acc(dve, 1, q)
            dve.tensor_tensor(X[:, 2 * q:2 * q + 2, :], X[:, 2 * q:2 * q + 2, :], acc(q), ALU.add).then_inc(S("x_final"), 1)
        norm_dve(dve, 6, X, "final_g", None, P[:, 8:16, :], "result_ready")


def pair_columns(w, cols):
    return w[:, cols].reshape(KT, 128, 256).transpose(1, 0, 2).reshape(128, PW)


def weight_stream(i):
    s = np.empty((NPAIRS, 128, PW), np.float32)
    n = 0

    def put(a):
        nonlocal n
        s[n] = a
        n += 1

    def span(w, start, width):
        for c in range(start, start + width, 256):
            put(pair_columns(w, slice(c, c + 256)))

    w = i["w_in"][0]
    q, k, v, g1, r, u, mq, mk, mv, gates = np.cumsum([0, 256, 256, 512, 16, 512, 512, 512, 512, 512]).tolist()
    for start, width in ((q, 256), (k, 256), (r, 512), (v, 512), (mq, 512), (mk, 512), (mv, 512), (u, 512), (gates, 3072)):
        span(w, start, width)
    branches = [i[f"w_branch_{x}"][0] for x in "abc"]
    for j in range(6):
        groups = [divmod(4 * j + g, 3) for g in range(4)]
        put(np.concatenate([branches[br][:, m * 128:m * 128 + 128].reshape(4, 128, 128).transpose(1, 0, 2).reshape(128, 512)
                            for m, br in groups], 1))
    span(i["w_out"][0], 0, 1024)

    def ffn(gate, up, down):
        def one(g):
            put(np.concatenate([gate[:, g * 128:g * 128 + 128].reshape(KT, 128, 128),
                                up[:, g * 128:g * 128 + 128].reshape(KT, 128, 128)], 2).transpose(1, 0, 2).reshape(128, PW))

        def two(j):
            put(down[j * 256:j * 256 + 256].reshape(2, 128, 1024).transpose(1, 0, 2).reshape(128, PW))

        one(0)
        one(1)
        for j in range(1, FT // 2):
            one(2 * j)
            one(2 * j + 1)
            two(j - 1)
        two(FT // 2 - 1)

    ffn(i["ffn_w_gate"][0], i["ffn_w_up"][0], i["ffn_w_down"][0])
    w = i["w_in_2"][0]
    hq, hf, hi, hg, lqk, lv, lif, lo, z, xbc, dt, gates = np.cumsum(
        [0, 1024, 1024, 1024, 1024, 1024, 1024, 8, 1024, 1024, 2048, 16]).tolist()
    for start, width in ((hq, 1024), (hf, 1024), (hi, 1024), (hg, 1024), (lqk, 1024), (lv, 1024),
                         *(((xbc if what == "x" else lo) + 256 * j, 256) for what, j in SSD_ORDER), (z, 1024)):
        span(w, start, width)
    for b, name in enumerate(("w_br_hg_2", "w_br_ml_2", "w_br_mb_2")):
        span(w, gates + 1024 * b, 1024)
        span(i[name][0], 0, 1024)
    span(i["w_out_2"][0], 0, 1024)
    up = i["w_up_2"][0]
    ffn(up[:, :FF], up[:, FF:], i["w_down_2"][0])
    assert n == NPAIRS, n
    return s


def channel_columns(i):
    def cols(v):
        return np.asarray(v).reshape(-1, 128).T

    parts = [cols(i[k][0]) for k in ("norm_mix_pre", "norm_mix_post", "norm_ffn_pre", "norm_ffn_post", "gla_b_g", "gla_norm",
                                     "pool_scale", "norm1_g_2", "hg_norm_g_2", "ml_norm_g_2")]
    parts += [cols(np.repeat(i["mb_d_2"][0], 64)), cols(i["mb_norm_g_2"][0]), cols(i["norm2_g_2"][0]), cols(i["final_g_2"])]
    parts += [cols(np.concatenate([i["ml_conv_b_2"][0], i["mb_conv_b_2"][0]]))]
    parts += [cols(np.concatenate([i["ml_conv_w_2"][0][k], i["mb_conv_w_2"][0][k]])) for k in range(4)]
    parts += [cols(i["ffn_conv_b_2"][0])] + [cols(i["ffn_conv_w_2"][0][k]) for k in range(3)]
    return np.ascontiguousarray(np.concatenate(parts, 1))


def kernel(**inputs):
    import concourse.bacc as bacc
    from concourse.bass_utils import run_bass_kernel_spmd

    i = {k: np.asarray(v) for k, v in inputs.items()}

    def small(w):
        return np.ascontiguousarray(w.reshape(KT, 128, -1).transpose(1, 0, 2).reshape(128, -1))

    head_rows = np.zeros((36, 8), np.float32)
    head_rows[32:36, 0], head_rows[32:36, 1] = i["ml_gate_b_2"][0][:4], i["ml_gate_b_2"][0][4:]
    head_rows[0:16, 2], head_rows[0:16, 3] = i["mb_dt_bias_2"][0], i["mb_a_log_2"][0]
    w1, w2 = i["w_in"][0], i["w_in_2"][0]
    arrays = {
        "stream": weight_stream(i),
        "xT": small(i["x"][0].T).reshape(128, KT, T),
        "cols": channel_columns(i),
        "consts": constants(),
        "masks": causal_masks(),
        "g1w": small(w1[:, 1024:1040]),
        "g2w": np.ascontiguousarray(i["gla_w_g2"][0]),
        "poolw": np.ascontiguousarray(i["pool_w"][0].transpose(1, 0, 2).reshape(128, 512)),
        "ifw": small(w2[:, 6144:6152]),
        "dtw": small(w2[:, 10248:10264]),
        "rows": head_rows,
    }
    nc = bacc.Bacc("TRN2", target_bir_lowering=False, num_devices=1)
    aps = [nc.dram_tensor(k, a.shape, F32, kind="ExternalInput").ap() for k, a in arrays.items()]
    out = nc.dram_tensor("out", (128, KT, T), F32, kind="ExternalOutput").ap()
    build(nc, *aps, out)
    r = run_bass_kernel_spmd(nc, [arrays], core_ids=[0]).results[0]["out"]
    return np.ascontiguousarray(r.reshape(128, KT, T).transpose(2, 1, 0).reshape(1, T, D))
```
